# Optimizing a Trainium2 kernel written in Bass

```python
import jax, jax.numpy as jnp
from jax import lax
import numpy as np
import math

D_MODEL = 1024
BATCH = 1
SEQ = 256
DEPTH = 1

D_MIX = D_MODEL
POOL_WIDTH = D_MIX // 4
POOL_WINDOWS = (2, 4, 8, 16)
N_POOL_GROUPS = len(POOL_WINDOWS)
POOL_GROUP_DIM = POOL_WIDTH // N_POOL_GROUPS
SSD_WIDTH = D_MIX - POOL_WIDTH
SSD_HEAD_DIM = 64
SSD_HEADS = SSD_WIDTH // SSD_HEAD_DIM
SSD_GROUPS = 4
SSD_HEADS_PER_GROUP = SSD_HEADS // SSD_GROUPS
SSD_STATE = 128
SSD_CONV = 4
SSD_CHUNK = 128
SSD_CONV_DIM = SSD_WIDTH + 2 * SSD_GROUPS * SSD_STATE
IN_PROJ_DIM = POOL_WIDTH + SSD_WIDTH + SSD_CONV_DIM + SSD_HEADS
N_EXPERT_GROUPS = 4
EXPERTS_PER_GROUP = 8
N_EXPERTS = N_EXPERT_GROUPS * EXPERTS_PER_GROUP
TOP_K = 2
EXPERT_FF = 512
MOE_BLOCK = 128
NORM_EPS = 1e-6


def rms_norm(x, eps=NORM_EPS):
    xf = x.astype(jnp.float32)
    y = xf * lax.rsqrt(jnp.mean(xf * xf, axis=-1, keepdims=True) + eps)
    return y.astype(x.dtype)

def modulate(x, shift, scale):
    return rms_norm(x) * (1 + scale[:, None, :]) + shift[:, None, :]

def pool_mixer(u, w_pool, pool_scale):
    b, s, _ = u.shape
    ug = u.reshape(b, s, N_POOL_GROUPS, POOL_GROUP_DIM)
    cs = jnp.cumsum(ug.astype(jnp.float32), axis=1)
    pos = jnp.arange(1, s + 1, dtype=jnp.float32)
    means = []
    for g, w in enumerate(POOL_WINDOWS):
        csg = cs[:, :, g]
        lagged = jnp.pad(csg, ((0, 0), (w, 0), (0, 0)))[:, :s]
        cnt = jnp.minimum(pos, float(w))
        means.append((csg - lagged) / cnt[None, :, None])
    mean = jnp.stack(means, axis=2).astype(u.dtype)
    y = jnp.einsum('bsgc,gcd->bsgd', mean - ug, w_pool)
    return y.reshape(b, s, POOL_WIDTH) * pool_scale

def causal_depthwise_conv(x, w, bias):
    ch = x.shape[-1]
    y = lax.conv_general_dilated(
        x, w[:, None, :].astype(x.dtype), window_strides=(1,),
        padding=((SSD_CONV - 1, 0),), dimension_numbers=('NWC', 'WIO', 'NWC'),
        feature_group_count=ch)
    return y + bias

def ssd_scan(xh, dt, a, bmat, cmat):
    b, s = xh.shape[:2]
    L = SSD_CHUNK
    nc = s // L
    G, R, P, N = SSD_GROUPS, SSD_HEADS_PER_GROUP, SSD_HEAD_DIM, SSD_STATE
    xc = (xh.astype(jnp.float32) * dt[..., None]).reshape(b, nc, L, G, R, P)
    bc = bmat.astype(jnp.float32).reshape(b, nc, L, G, N)
    cc = cmat.astype(jnp.float32).reshape(b, nc, L, G, N)
    a_cs = jnp.cumsum((dt * a).reshape(b, nc, L, G, R), axis=2)
    causal = jnp.tril(jnp.ones((L, L), dtype=bool))
    seg = a_cs[:, :, :, None] - a_cs[:, :, None, :]
    decay = jnp.exp(jnp.where(causal[None, None, :, :, None, None], seg, -jnp.inf))
    cb = jnp.einsum('bclgn,bcsgn->bclsg', cc, bc)
    y_diag = jnp.einsum('bclsgr,bcsgrp->bclgrp', cb[..., None] * decay, xc)
    decay_to_end = jnp.exp(a_cs[:, :, -1:] - a_cs)
    chunk_states = jnp.einsum('bclgn,bclgrp->bcgrpn', bc, xc * decay_to_end[..., None])
    chunk_decay = jnp.exp(a_cs[:, :, -1])

    def step(state, inp):
        st, dec = inp
        return state * dec[..., None, None] + st, state

    init = jnp.zeros((b, G, R, P, N), jnp.float32)
    _, prev = lax.scan(step, init, (jnp.moveaxis(chunk_states, 1, 0),
                                    jnp.moveaxis(chunk_decay, 1, 0)))
    prev = jnp.moveaxis(prev, 0, 1)
    y_off = jnp.einsum('bclgn,bcgrpn->bclgrp', cc, prev) * jnp.exp(a_cs)[..., None]
    return (y_diag + y_off).reshape(b, s, G, R, P)

def ssd_mixer(z, xbc, dt_raw, conv_w, conv_b, dt_bias, a_log, d_skip, norm_w):
    b, s, _ = z.shape
    G, R, P, N = SSD_GROUPS, SSD_HEADS_PER_GROUP, SSD_HEAD_DIM, SSD_STATE
    xbc = jax.nn.silu(causal_depthwise_conv(xbc, conv_w, conv_b))
    xs, bm, cm = jnp.split(xbc, [SSD_WIDTH, SSD_WIDTH + G * N], axis=-1)
    xh = xs.reshape(b, s, G, R, P)
    bm = bm.reshape(b, s, G, N)
    cm = cm.reshape(b, s, G, N)
    dt = jax.nn.softplus(dt_raw.astype(jnp.float32) + dt_bias.astype(jnp.float32)).reshape(b, s, G, R)
    a = -jnp.exp(a_log.astype(jnp.float32)).reshape(G, R)
    y = ssd_scan(xh, dt, a, bm, cm) + xh.astype(jnp.float32) * d_skip.astype(jnp.float32).reshape(G, R)[..., None]
    y = y.reshape(b, s, SSD_WIDTH).astype(z.dtype) * jax.nn.silu(z)
    y = rms_norm(y.reshape(b, s, G, SSD_WIDTH // G)).reshape(b, s, SSD_WIDTH)
    return y * norm_w

def hier_moe(h, w_group, b_group, w_router, b_router, w13, w2):
    b, s, d = h.shape
    T = b * s
    hf = h.reshape(T, d)
    g_logits = (hf @ w_group + b_group).astype(jnp.float32)
    g_prob = jax.nn.softmax(g_logits, axis=-1)
    p_g, g_idx = lax.top_k(g_prob, 1)
    e_logits = (hf @ w_router + b_router).astype(jnp.float32).reshape(T, N_EXPERT_GROUPS, EXPERTS_PER_GROUP)
    within = jnp.take_along_axis(e_logits, g_idx[:, :, None], axis=1)[:, 0]
    top_v, top_i = lax.top_k(within, TOP_K)
    gate = p_g * jax.nn.softmax(top_v, axis=-1)
    expert_id = (g_idx * EXPERTS_PER_GROUP + top_i).astype(jnp.int32)
    A = T * TOP_K
    flat_e = expert_id.reshape(A)
    flat_tok = jnp.repeat(jnp.arange(T, dtype=jnp.int32), TOP_K)
    flat_w = gate.reshape(A)
    order = jnp.argsort(flat_e)
    se, stok, sw = flat_e[order], flat_tok[order], flat_w[order]
    counts = jnp.bincount(flat_e, length=N_EXPERTS)
    starts = jnp.cumsum(counts) - counts
    padded = ((counts + MOE_BLOCK - 1) // MOE_BLOCK) * MOE_BLOCK
    pends = jnp.cumsum(padded)
    pstarts = pends - padded
    dest = pstarts[se] + (jnp.arange(A, dtype=jnp.int32) - starts[se])
    R = A + N_EXPERTS * MOE_BLOCK
    n_blk = R // MOE_BLOCK
    row_tok = jnp.zeros((R,), jnp.int32).at[dest].set(stok)
    row_w = jnp.zeros((R,), h.dtype).at[dest].set(sw.astype(h.dtype))
    blk_start = jnp.arange(n_blk, dtype=jnp.int32) * MOE_BLOCK
    blk_e = jnp.clip(jnp.searchsorted(pends, blk_start, side='right'), 0, N_EXPERTS - 1)
    xs = hf[row_tok].reshape(n_blk, MOE_BLOCK, d)

    def expert_block(args):
        xb, e = args
        hu = xb @ w13[e]
        a_, b_ = jnp.split(hu, 2, axis=-1)
        return (jax.nn.silu(a_) * b_) @ w2[e]

    ys = lax.map(expert_block, (xs, blk_e)).reshape(R, d)
    out = jax.ops.segment_sum(ys * row_w[:, None], row_tok, num_segments=T)
    return out.reshape(b, s, d)

def first_inputs(seed: int = 0) -> dict:
    key = jax.random.key(seed)
    ks = jax.random.split(key, 24)
    f32 = jnp.float32
    nrm = lambda k, shape, scale: jax.random.normal(k, shape, f32) * scale
    x = jax.random.normal(ks[0], (BATCH, SEQ, D_MODEL), f32)
    c = jax.random.normal(ks[1], (BATCH, D_MODEL), f32)
    w_ada = nrm(ks[2], (DEPTH, D_MODEL, 6 * D_MODEL), D_MODEL ** -0.5)
    b_ada = nrm(ks[3], (DEPTH, 6 * D_MODEL), 0.02)
    w_in = nrm(ks[4], (DEPTH, D_MODEL, IN_PROJ_DIM), D_MODEL ** -0.5)
    w_pool = nrm(ks[5], (DEPTH, N_POOL_GROUPS, POOL_GROUP_DIM, POOL_GROUP_DIM), POOL_GROUP_DIM ** -0.5)
    pool_scale = 1.0 + nrm(ks[6], (DEPTH, POOL_WIDTH), 0.1)
    conv_w = nrm(ks[7], (DEPTH, SSD_CONV, SSD_CONV_DIM), SSD_CONV ** -0.5)
    conv_b = nrm(ks[8], (DEPTH, SSD_CONV_DIM), 0.02)
    dt0 = jnp.exp(jax.random.uniform(ks[9], (DEPTH, SSD_HEADS), f32, np.log(1e-3), np.log(1e-1)))
    dt_bias = dt0 + jnp.log(-jnp.expm1(-dt0))
    a_log = jnp.log(jax.random.uniform(ks[10], (DEPTH, SSD_HEADS), f32, 1.0, 16.0))
    d_skip = 1.0 + nrm(ks[11], (DEPTH, SSD_HEADS), 0.1)
    ssd_norm_w = 1.0 + nrm(ks[12], (DEPTH, SSD_WIDTH), 0.1)
    w_out = nrm(ks[13], (DEPTH, D_MIX, D_MODEL), D_MIX ** -0.5)
    w_group = nrm(ks[14], (DEPTH, D_MODEL, N_EXPERT_GROUPS), D_MODEL ** -0.5)
    b_group = nrm(ks[15], (DEPTH, N_EXPERT_GROUPS), 0.01)
    w_router = nrm(ks[16], (DEPTH, D_MODEL, N_EXPERTS), D_MODEL ** -0.5)
    b_router = nrm(ks[17], (DEPTH, N_EXPERTS), 0.01)
    w13 = nrm(ks[18], (DEPTH, N_EXPERTS, D_MODEL, 2 * EXPERT_FF), D_MODEL ** -0.5)
    w2 = nrm(ks[19], (DEPTH, N_EXPERTS, EXPERT_FF, D_MODEL), EXPERT_FF ** -0.5)
    final_norm_w = 1.0 + nrm(ks[20], (D_MODEL,), 0.1)
    return {"x": x, "c": c, "w_ada": w_ada, "b_ada": b_ada, "w_in": w_in,
            "w_pool": w_pool, "pool_scale": pool_scale, "conv_w": conv_w, "conv_b": conv_b,
            "dt_bias": dt_bias, "a_log": a_log, "d_skip": d_skip, "ssd_norm_w": ssd_norm_w,
            "w_out": w_out, "w_group": w_group, "b_group": b_group, "w_router": w_router,
            "b_router": b_router, "w13": w13, "w2": w2, "final_norm_w": final_norm_w}

def first_block(x, c, w_ada, b_ada, w_in, w_pool, pool_scale, conv_w, conv_b, dt_bias, a_log,
              d_skip, ssd_norm_w, w_out, w_group, b_group, w_router, b_router, w13, w2,
              final_norm_w):
    split_at = [POOL_WIDTH, POOL_WIDTH + SSD_WIDTH, POOL_WIDTH + SSD_WIDTH + SSD_CONV_DIM]
    for layer in range(DEPTH):
        mod = jax.nn.silu(c) @ w_ada[layer] + b_ada[layer]
        sh1, sc1, g1, sh2, sc2, g2 = jnp.split(mod, 6, axis=-1)
        h = modulate(x, sh1, sc1)
        proj = h @ w_in[layer]
        u, z, xbc, dt_raw = jnp.split(proj, split_at, axis=-1)
        y_pool = pool_mixer(u, w_pool[layer], pool_scale[layer])
        y_ssd = ssd_mixer(z, xbc, dt_raw, conv_w[layer], conv_b[layer], dt_bias[layer],
                          a_log[layer], d_skip[layer], ssd_norm_w[layer])
        mix = jnp.concatenate([y_pool, y_ssd], axis=-1) @ w_out[layer]
        x = x + g1[:, None, :] * mix
        h = modulate(x, sh2, sc2)
        x = x + g2[:, None, :] * hier_moe(h, w_group[layer], b_group[layer], w_router[layer],
                                           b_router[layer], w13[layer], w2[layer])
    return rms_norm(x) * final_norm_w


MEM_LEN = 256
MLA_NOPE = 128
MLA_ROPE = 64
MLA_V = 128
MLA_HEADS = D_MODEL // MLA_V
MLA_KV_RANK = 256
GLA_HEADS = 4
GLA_DK = D_MODEL // 2 // GLA_HEADS
GLA_DV = D_MODEL // GLA_HEADS
GLA_GATE_RANK = 16
GLA_GATE_NORMALIZER = 16.0
GLA_CHUNK = 64
MEM_HEADS = 4
MEM_DQK = 64
MEM_DV = D_MODEL // MEM_HEADS
N_BRANCHES = 3
D_FF = 4 * D_MODEL
ATTN_BLOCK = 128
ROPE_THETA = 10000.0
EPS = 1e-6

IN_SPLITS = (
    MLA_HEADS * (MLA_NOPE + MLA_ROPE),
    MLA_KV_RANK,
    MLA_ROPE,
    GLA_HEADS * GLA_DK,
    GLA_HEADS * GLA_DK,
    GLA_HEADS * GLA_DV,
    GLA_GATE_RANK,
    GLA_HEADS * GLA_DV,
    MEM_HEADS * MEM_DQK,
    N_BRANCHES * D_MODEL,
)
D_IN = sum(IN_SPLITS)


def rms_norm_2(t, g):
    tf = t.astype(jnp.float32)
    y = tf * lax.rsqrt(jnp.mean(tf * tf, axis=-1, keepdims=True) + EPS)
    return (y * g.astype(jnp.float32)).astype(t.dtype)

def rope_tables(positions):
    inv = 1.0 / (ROPE_THETA ** (jnp.arange(0, MLA_ROPE, 2, dtype=jnp.float32) / MLA_ROPE))
    ang = positions.astype(jnp.float32)[..., None] * inv
    return jnp.cos(ang), jnp.sin(ang)

def apply_rope(t, cos, sin):
    tf = t.astype(jnp.float32)
    t1, t2 = jnp.split(tf, 2, axis=-1)
    c = cos[:, :, None, :]
    s = sin[:, :, None, :]
    return jnp.concatenate([t1 * c - t2 * s, t1 * s + t2 * c], axis=-1).astype(t.dtype)

def causal_block_attention(q, k, v, scale):
    B, S, H, D = q.shape
    Dv = v.shape[-1]
    nb = S // ATTN_BLOCK
    qb = q.reshape(B, nb, ATTN_BLOCK, H, D).transpose(1, 0, 3, 2, 4)
    kh = k.transpose(0, 2, 1, 3)
    vh = v.transpose(0, 2, 1, 3)
    kpos = jnp.arange(S)

    def one_block(args):
        qi, i = args
        s = jnp.einsum('bhqd,bhkd->bhqk', qi, kh).astype(jnp.float32) * scale
        qpos = i * ATTN_BLOCK + jnp.arange(ATTN_BLOCK)
        s = jnp.where(kpos[None, :] <= qpos[:, None], s, -1e30)
        p = jax.nn.softmax(s, axis=-1).astype(vh.dtype)
        return jnp.einsum('bhqk,bhkd->bhqd', p, vh)

    o = lax.map(one_block, (qb, jnp.arange(nb)))
    return o.transpose(1, 0, 3, 2, 4).reshape(B, S, H, Dv)

def gla_chunked(q, k, v, log_a):
    B, S, H, DK = q.shape
    DV = v.shape[-1]
    C = GLA_CHUNK
    nc = S // C

    def to_chunks(t):
        return t.astype(jnp.float32).reshape(B, nc, C, H, t.shape[-1]).transpose(1, 0, 3, 2, 4)

    qc, kc, vc = to_chunks(q), to_chunks(k), to_chunks(v)
    bc = jnp.cumsum(to_chunks(log_a), axis=3)
    mask = jnp.tril(jnp.ones((C, C), dtype=bool))[None, None, :, :, None]

    def step(state, inp):
        qi, ki, vi, bi = inp
        diff = bi[:, :, :, None, :] - bi[:, :, None, :, :]
        decay = jnp.where(mask, jnp.exp(jnp.where(mask, diff, 0.0)), 0.0)
        a = jnp.einsum('bhid,bhjd,bhijd->bhij', qi, ki, decay)
        o_intra = jnp.einsum('bhij,bhje->bhie', a, vi)
        o_inter = jnp.einsum('bhid,bhde->bhie', qi * jnp.exp(bi), state)
        b_last = bi[:, :, -1, :]
        k_dec = ki * jnp.exp(b_last[:, :, None, :] - bi)
        new_state = jnp.exp(b_last)[..., None] * state + jnp.einsum('bhjd,bhje->bhde', k_dec, vi)
        return new_state, o_intra + o_inter

    state0 = jnp.zeros((B, H, DK, DV), jnp.float32)
    _, o = lax.scan(step, state0, (qc, kc, vc, bc))
    return o.transpose(1, 0, 3, 2, 4).reshape(B, S, H, DV).astype(q.dtype)

def hybrid_layer(x, mem, cos, sin, g_mix, w_in, b_gate, g_ckv, w_ukv, g_q_nope, g_k_nope,
                 g_q_rope, g_k_rope, w_gla_gate, b_gla_gate, g_gla_out, g_mem, w_mem_kv,
                 g_q_mem, g_k_mem, w_o, g_ffn, w_up, w_down):
    B, S, _ = x.shape
    M = mem.shape[1]
    h = rms_norm_2(x, g_mix)
    proj = h @ w_in
    offsets = []
    acc = 0
    for n in IN_SPLITS[:-1]:
        acc += n
        offsets.append(acc)
    (q_mla, c_kv, k_rope, q_gla, k_gla, v_gla, a_gla, r_gla, q_mem,
     gate_logits) = jnp.split(proj, offsets, axis=-1)

    q_mla = q_mla.reshape(B, S, MLA_HEADS, MLA_NOPE + MLA_ROPE)
    q_nope = rms_norm_2(q_mla[..., :MLA_NOPE], g_q_nope)
    q_pe = apply_rope(rms_norm_2(q_mla[..., MLA_NOPE:], g_q_rope), cos, sin)
    kv = (rms_norm_2(c_kv, g_ckv) @ w_ukv).reshape(B, S, MLA_HEADS, MLA_NOPE + MLA_V)
    k_nope = rms_norm_2(kv[..., :MLA_NOPE], g_k_nope)
    v_mla = kv[..., MLA_NOPE:]
    k_pe = apply_rope(rms_norm_2(k_rope, g_k_rope)[:, :, None, :], cos, sin)
    q_full = jnp.concatenate([q_nope, q_pe], axis=-1)
    k_full = jnp.concatenate([k_nope, jnp.broadcast_to(k_pe, (B, S, MLA_HEADS, MLA_ROPE))], axis=-1)
    o_mla = causal_block_attention(q_full, k_full, v_mla,
                                   (MLA_NOPE + MLA_ROPE) ** -0.5).reshape(B, S, MLA_HEADS * MLA_V)

    qg = q_gla.reshape(B, S, GLA_HEADS, GLA_DK) * (GLA_DK ** -0.5)
    kg = k_gla.reshape(B, S, GLA_HEADS, GLA_DK)
    vg = v_gla.reshape(B, S, GLA_HEADS, GLA_DV)
    log_a = jax.nn.log_sigmoid((a_gla @ w_gla_gate + b_gla_gate).astype(jnp.float32)) / GLA_GATE_NORMALIZER
    log_a = log_a.reshape(B, S, GLA_HEADS, GLA_DK)
    og = gla_chunked(qg, kg, vg, log_a)
    o_gla = rms_norm_2(og, g_gla_out).reshape(B, S, GLA_HEADS * GLA_DV) * jax.nn.silu(r_gla)

    kv_m = rms_norm_2(mem, g_mem) @ w_mem_kv
    k_m = rms_norm_2(kv_m[..., :MEM_HEADS * MEM_DQK].reshape(B, M, MEM_HEADS, MEM_DQK), g_k_mem)
    v_m = kv_m[..., MEM_HEADS * MEM_DQK:].reshape(B, M, MEM_HEADS, MEM_DV)
    q_m = rms_norm_2(q_mem.reshape(B, S, MEM_HEADS, MEM_DQK), g_q_mem)
    s_m = jnp.einsum('bshd,bmhd->bhsm', q_m, k_m).astype(jnp.float32) * (MEM_DQK ** -0.5)
    p_m = jax.nn.softmax(s_m, axis=-1).astype(v_m.dtype)
    o_mem = jnp.einsum('bhsm,bmhd->bshd', p_m, v_m).reshape(B, S, MEM_HEADS * MEM_DV)

    gates = jax.nn.sigmoid(gate_logits + b_gate).reshape(B, S, N_BRANCHES, D_MODEL)
    y = gates[..., 0, :] * o_mla + gates[..., 1, :] * o_gla + gates[..., 2, :] * o_mem
    x = x + y @ w_o

    h2 = rms_norm_2(x, g_ffn)
    return x + jnp.square(jax.nn.relu(h2 @ w_up)) @ w_down

def second_inputs(seed: int = 0) -> dict:
    key = jax.random.key(seed)
    ks = jax.random.split(key, 24)
    L = DEPTH

    def w(k, shape, fan_in):
        return jax.random.normal(k, (L,) + shape, jnp.float32) * (fan_in ** -0.5)

    def gain(k, n):
        return 1.0 + 0.02 * jax.random.normal(k, (L, n), jnp.float32)

    def bias(k, n):
        return 0.01 * jax.random.normal(k, (L, n), jnp.float32)

    x = jax.random.normal(ks[0], (BATCH, SEQ, D_MODEL), jnp.float32)
    mem = jax.random.normal(ks[1], (BATCH, MEM_LEN, D_MODEL), jnp.float32)
    positions = (jax.random.randint(ks[2], (BATCH, 1), 0, 4096, dtype=jnp.int32)
                 + jnp.arange(SEQ, dtype=jnp.int32)[None, :])
    return {
        'x': x,
        'mem': mem,
        'positions': positions,
        'g_mix': gain(ks[3], D_MODEL),
        'w_in': w(ks[4], (D_MODEL, D_IN), D_MODEL),
        'b_gate': bias(ks[5], N_BRANCHES * D_MODEL),
        'g_ckv': gain(ks[6], MLA_KV_RANK),
        'w_ukv': w(ks[7], (MLA_KV_RANK, MLA_HEADS * (MLA_NOPE + MLA_V)), MLA_KV_RANK),
        'g_q_nope': gain(ks[8], MLA_NOPE),
        'g_k_nope': gain(ks[9], MLA_NOPE),
        'g_q_rope': gain(ks[10], MLA_ROPE),
        'g_k_rope': gain(ks[11], MLA_ROPE),
        'w_gla_gate': w(ks[12], (GLA_GATE_RANK, GLA_HEADS * GLA_DK), GLA_GATE_RANK),
        'b_gla_gate': bias(ks[13], GLA_HEADS * GLA_DK),
        'g_gla_out': gain(ks[14], GLA_DV),
        'g_mem': gain(ks[15], D_MODEL),
        'w_mem_kv': w(ks[16], (D_MODEL, MEM_HEADS * (MEM_DQK + MEM_DV)), D_MODEL),
        'g_q_mem': gain(ks[17], MEM_DQK),
        'g_k_mem': gain(ks[18], MEM_DQK),
        'w_o': w(ks[19], (D_MODEL, D_MODEL), D_MODEL),
        'g_ffn': gain(ks[20], D_MODEL),
        'w_up': w(ks[21], (D_MODEL, D_FF), D_MODEL),
        'w_down': w(ks[22], (D_FF, D_MODEL), D_FF),
    }

def second_block(x, mem, positions, g_mix, w_in, b_gate, g_ckv, w_ukv, g_q_nope, g_k_nope,
              g_q_rope, g_k_rope, w_gla_gate, b_gla_gate, g_gla_out, g_mem, w_mem_kv,
              g_q_mem, g_k_mem, w_o, g_ffn, w_up, w_down):
    cos, sin = rope_tables(positions)
    for l in range(DEPTH):
        x = hybrid_layer(x, mem, cos, sin, g_mix[l], w_in[l], b_gate[l], g_ckv[l], w_ukv[l],
                         g_q_nope[l], g_k_nope[l], g_q_rope[l], g_k_rope[l], w_gla_gate[l],
                         b_gla_gate[l], g_gla_out[l], g_mem[l], w_mem_kv[l], g_q_mem[l],
                         g_k_mem[l], w_o[l], g_ffn[l], w_up[l], w_down[l])
    return x


def setup_inputs(seed=0):
    out = dict(first_inputs(seed))
    for name, value in second_inputs(seed + 1).items():
        if name != "x":
            out[name + "_2"] = value
    return out


def reference(
    x, c, w_ada, b_ada, w_in, w_pool, pool_scale, conv_w, conv_b, dt_bias, a_log, d_skip,
    ssd_norm_w, w_out, w_group, b_group, w_router, b_router, w13, w2, final_norm_w, mem_2,
    positions_2, g_mix_2, w_in_2, b_gate_2, g_ckv_2, w_ukv_2, g_q_nope_2, g_k_nope_2,
    g_q_rope_2, g_k_rope_2, w_gla_gate_2, b_gla_gate_2, g_gla_out_2, g_mem_2, w_mem_kv_2,
    g_q_mem_2, g_k_mem_2, w_o_2, g_ffn_2, w_up_2, w_down_2,
):
    x = first_block(
        x, c, w_ada, b_ada, w_in, w_pool, pool_scale, conv_w, conv_b, dt_bias, a_log, d_skip,
        ssd_norm_w, w_out, w_group, b_group, w_router, b_router, w13, w2, final_norm_w,
    )
    return second_block(
        x, mem_2, positions_2, g_mix_2, w_in_2, b_gate_2, g_ckv_2, w_ukv_2, g_q_nope_2,
        g_k_nope_2, g_q_rope_2, g_k_rope_2, w_gla_gate_2, b_gla_gate_2, g_gla_out_2, g_mem_2,
        w_mem_kv_2, g_q_mem_2, g_k_mem_2, w_o_2, g_ffn_2, w_up_2, w_down_2,
    )


_drawn_inputs = setup_inputs


def setup_inputs(seed=0):
    import zlib

    import numpy as np

    out = dict(_drawn_inputs(seed))
    spreads = {}
    factors = {'conv_b': 2.973,
     'b_group': 8.0,
     'b_router': 3.723,
     'g_mix_2': 3.92,
     'b_gate_2': 27.073,
     'g_ckv_2': 32.594,
     'g_q_nope_2': 35.291,
     'g_k_nope_2': 38.649,
     'g_q_rope_2': 53.38,
     'g_k_rope_2': 47.509,
     'b_gla_gate_2': 25.459,
     'g_gla_out_2': 72.471,
     'g_mem_2': 28.91,
     'g_q_mem_2': 28.091,
     'g_k_mem_2': 22.442,
     'g_ffn_2': 12.485}
    for name, (base, spread) in spreads.items():
        noise = np.random.default_rng([zlib.crc32(name.encode()), seed]).standard_normal(out[name].shape)
        drawn = base * np.exp(spread * noise) if base else spread * noise
        out[name] = __import__('jax').numpy.asarray(drawn.astype(out[name].dtype))
    for name, factor in factors.items():
        out[name] = (out[name] * factor).astype(out[name].dtype)
    return out
```

```python
from contextlib import ExitStack

import numpy as np

import concourse.bass as bass
from concourse import mybir

ALU = mybir.AluOpType
ACT = mybir.ActivationFunctionType
AX = mybir.AxisListType
F32 = mybir.dt.float32
I32 = mybir.dt.int32
U32 = mybir.dt.uint32

P = 128
D = 1024
T = 256
TT = T // P
KD = D // P
EPS = 1e-6

POOL_W, SSD_W, HEADS, HD, GROUPS, STATE, CONV = 256, 768, 12, 64, 4, 128, 4
RPG = HEADS // GROUPS
XBC = SSD_W + 2 * GROUPS * STATE
NXB = XBC // P
IN1 = POOL_W + SSD_W + XBC + HEADS
EG, EPG, FF = 4, 8, 512
NE = EG * EPG
SLOTS = 64
MAXB = NE + 2 * T // SLOTS
MH, NOPE, ROPE, VD, KVR = 8, 128, 64, 128, 256
GH, DK, DV, GRANK = 4, 128, 256, 16
EH, EQ, EV = 4, 64, 256
DFF = 4 * D
O_Q, O_CKV, O_KR = 0, 1536, 1792
O_GQ, O_GK, O_GV, O_GA, O_GR = 1856, 2368, 2880, 3904, 3920
O_MQ, O_GATE = 4944, 5200
LEVELS = 7
BIG = -1e30

ROWS = {}
_r = 0
for _n, _c in (("c", 8), ("conv_w", CONV * NXB), ("conv_b", NXB), ("ssd_norm_w", 6), ("pool_scale", 2),
               ("g_mix", 8), ("g_mem", 8), ("g_ffn", 8), ("g_ckv", 2)):
    ROWS[_n] = _r
    _r += _c
NROWS = _r
BADA = NROWS
assert NROWS <= P

CONST_COLS = {}
_r = 0
for _n, _c in (("ident", P), ("tri", P), ("strict", P), ("ones", P), ("seg_mask", P), ("causal", P),
               ("fold", P), ("iota", P), ("level", LEVELS * P), ("inv", ROPE // 2), ("row_id", 1),
               ("rev4", EG), ("rev8", EPG)):
    CONST_COLS[_n] = (_r, _c)
    _r += _c
NCONST = _r


def constants():
    c = np.zeros((P, NCONST), np.float32)
    p, f = np.arange(P)[:, None], np.arange(P)[None, :]

    def put(name, value):
        a, n = CONST_COLS[name]
        c[:, a:a + n] = value
    put("ident", p == f)
    put("tri", p <= f)
    put("strict", p < f)
    put("ones", 1.0)
    put("seg_mask", np.where(p <= f, 0.0, BIG))
    put("causal", np.where(f <= p, 0.0, BIG))
    put("fold", (f < SLOTS) & (p % SLOTS == f))
    put("iota", np.broadcast_to(f, (P, P)))
    x = p ^ f
    put("level", np.concatenate([(x >= 2 ** l) & (x < 2 ** (l + 1)) & (p < f) for l in range(LEVELS)], 1))
    put("inv", (1.0 / (np.float32(10000.0) ** (np.arange(0, ROPE, 2, dtype=np.float32) / np.float32(ROPE))))[None, :])
    put("row_id", p)
    put("rev4", np.arange(EG, 0, -1)[None, :])
    put("rev8", np.arange(EPG, 0, -1)[None, :])
    pool = np.zeros((P, 2, T), np.float32)
    for g, w in enumerate((2, 4, 8, 16)):
        cnt = np.minimum(np.arange(1, T + 1, dtype=np.float32), np.float32(w))
        pool[64 * (g % 2):64 * (g % 2) + 64, g // 2] = np.float32(1.0) / cnt
    return c, pool.reshape(P, 2 * T)


class Signal:

    def __init__(self, sem):
        self.sem, self.n = sem, 0


class Chained:

    def __init__(self, eng, sem):
        self.eng, self.done = eng, Signal(sem)

    def __call__(self, ins, signal=None):
        s = signal or self.done
        s.n += 1
        ins.then_inc(s.sem, 1)
        self.eng.wait_ge(s.sem, s.n)


class LoopChained:

    def __init__(self, eng, sem, i, per):
        self.eng, self.sem, self.i, self.per, self.n = eng, sem, i, per, 0

    def __call__(self, ins):
        self.n += 1
        ins.then_inc(self.sem, 1)
        self.eng.wait_ge(self.sem, self.i * self.per + (self.n - self.per))

    def end(self):
        assert self.n == self.per, (self.n, self.per)


class PsumBanks:

    def __init__(self, banks, filled, drained):
        self.banks, self.filled, self.drained = banks, filled, drained
        self.order, self.by = [], {}
        self.count = {"dve": 0, "act": 0}
        self.seen = {"dve": 0, "act": 0}

    def fill(self, pe, name, reader):
        n = len(self.order)
        if n >= 8:
            r, k = self.order[n - 8]
            pe.wait_ge(self.drained[r], k + 1)
        assert name not in self.by, name
        self.by[name] = (n % 8, reader, self.count[reader])
        self.order.append((reader, self.count[reader]))
        self.count[reader] += 1
        return self.banks[n % 8]

    def full(self, name, ins):
        ins.then_inc(self.filled[self.by[name][1]], 1)

    def wait_drained(self, pe, name):
        _, r, k = self.by[name]
        pe.wait_ge(self.drained[r], k + 1)

    def wait_filled(self, eng, name):
        _, r, k = self.by[name]
        eng.wait_ge(self.filled[r], k + 1)

    def read(self, eng, name, reader):
        b, r, k = self.by[name]
        assert r == reader and k == self.seen[reader], (name, r, k, self.seen[reader])
        eng.wait_ge(self.filled[r], k + 1)
        return self.banks[b]

    def release(self, name, ins, eng):
        _, r, k = self.by[name]
        self.seen[r] += 1
        ins.then_inc(self.drained[r], 1)
        eng.wait_ge(self.drained[r], k + 1)


class WeightRing:

    def __init__(self, ps, slots, landed):
        self.ps, self.slots, self.landed = ps, slots, landed
        self.n, self.loads, self.taken, self.free_at = len(slots), 0, 0, []

    def take(self, pe):
        k = self.taken
        self.taken += 1
        pe.wait_ge(self.landed[k % self.n], 16 * (k // self.n + 1))
        return self.slots[k % self.n]

    def last_use(self, bank_name):
        self.free_at.append(bank_name)

    def load(self, sp, view, src, need=None):
        k = self.loads
        self.loads += 1
        if k >= self.n:
            at = self.free_at[k - self.n]
            if isinstance(at, tuple):
                sp.wait_ge(*at)
            else:
                self.ps.wait_filled(sp, at)
        if need:
            sp.wait_ge(*need)
        s = k % self.n
        sp.dma_start(view(self.slots[s]), src).then_inc(self.landed[s], 16)


def build(nc, a, out):
    ctx = ExitStack()
    with ctx:
        def sb(name, cols, dt=F32, parts=P):
            return ctx.enter_context(nc.sbuf_tensor(name, [parts, cols], dt))

        def sem(name):
            return ctx.enter_context(nc.semaphore(name))

        def v3(ap, n):
            return ap.rearrange("p (a b) -> p a b", a=n)

        def over(ap, n, axis):
            x = ap.unsqueeze(axis)
            shape = list(x.shape)
            shape[axis] = n
            return x.to_broadcast(shape)

        ring_mem = sb("weight_ring", 6 * 4096)
        cst = sb("constants", NCONST)
        C = {n: cst[:, x:x + w] for n, (x, w) in CONST_COLS.items()}
        ident, ones = C["ident"], C["ones"]
        prm = sb("param_cols", NROWS + 48)
        x = v3(sb("x_tokens", TT * D)[:, :], TT)
        hT_sb = sb("hT", KD * T)
        hT = v3(hT_sb[:, :], KD)
        g1b = sb("gate1_rows", D)
        g2b = sb("gate2_rows", D)
        fnw = sb("final_norm_rows", D)
        rows2 = sb("norm_gain_rows", 512)
        kmT = v3(sb("mem_keysT", 2 * T)[:, :], 2)
        vm_sb = sb("mem_values", TT * D)
        vm = v3(vm_sb[:, :], TT)
        small = sb("small", 1100)
        small_at = [0]

        def tiny(n, dt=F32):
            v = small[:, small_at[0]:small_at[0] + n]
            small_at[0] += n
            assert small_at[0] <= 1100, small_at
            return v if dt == F32 else v.bitcast(dt)

        work = sb("work", 14900)
        extra = ring_mem[:, 4 * 4096:6 * 4096]

        def area(*bases):
            left = [[b, 0] for b in bases]

            def alloc(n):
                for e in left:
                    if e[1] + n <= e[0].shape[1]:
                        e[1] += n
                        return e[0][:, e[1] - n:e[1]]
                raise AssertionError((n, [(b.shape, u) for b, u in left]))
            return alloc

        banks = [ctx.enter_context(nc.psum_tensor(f"bank{i}", [P, 512], F32)) for i in range(8)]

        def flat(v):
            return v.rearrange("p a b -> p (a b)")

        m1 = area(work[:, :])
        xn_f = m1(TT * D)
        xn = v3(xn_f, TT)
        mixT = v3(xn_f, KD)
        raw_f = m1(NXB * (T + 3))
        raw = v3(raw_f, NXB)
        xb_f = m1(NXB * T)
        xb = v3(xb_f, NXB)
        cv_f, ce_f = m1(4 * T), m1(4 * T)
        cv, ce = v3(cv_f, 4), v3(ce_f, 4)
        z = v3(m1(TT * SSD_W), TT)
        wpool = v3(m1(2 * P), 2)
        y_f = m1(TT * SSD_W)
        yv = v3(y_f, TT)
        prc = v3(y_f[:, 0:2 * T], 2)
        prm_rows = cv_f[:, 0:2 * P]
        u_mem = area(vm_sb[:, :])
        PAD = 16
        uT, sA, sB = (v3(u_mem(2 * (T + PAD)), 2) for _ in range(3))
        diff = kmT
        r_mem = area(raw_f)
        xtok = v3(r_mem(TT * 1280), TT)
        prevT = v3(r_mem(GROUPS * RPG * HD), GROUPS)
        xdt = v3(hT_sb[:, 0:TT * SSD_W], TT)
        seg, seg2 = v3(cv_f[:, 0:RPG * P], RPG), v3(cv_f[:, RPG * P:2 * RPG * P], RPG)
        xcd = ce_f[:, 0:SSD_W]
        ybuf = ce_f[:, SSD_W:SSD_W + RPG * HD]
        mem_x = v3(raw_f[:, 0:TT * D], TT)
        m_mem = area(xb_f)
        memT = v3(m_mem(KD * T), KD)
        mk = v3(m_mem(TT * EH * EQ), TT)
        msq = v3(m_mem(TT * EH * EQ), TT)
        m3 = area(work[:, TT * D:])
        xeT = v3(m3(KD * P), KD)
        hs = m3(D)
        ge = v3(m3(4 * SLOTS), 4)
        gt = v3(m3(4 * SLOTS), 4)
        sT = [v3(m3(4 * SLOTS), 4) for _ in range(2)]
        osb = m3(D)
        pick = v3(m3(TT * P), TT)
        wr = v3(m3(KD * (EG + NE)), KD)
        acc_f = m3(TT * D)
        acc = v3(acc_f, TT)
        diag = v3(acc_f[:, D:2 * D], 8)
        slot_rows, gate_rows = m3(2 * T), m3(2 * T)
        share_f = m3(2 * T)
        slot_id = m3(P)
        def m2_area():
            return area(work[:, :], extra)
        m2 = m2_area()
        ysum, obr = v3(m2(TT * D), TT), v3(m2(TT * D), TT)
        m2_used = 2 * TT * D
        sbuf2 = area(work[:, m2_used:], extra)
        pr = [v3(sbuf2(TT * T), TT) for _ in range(2)]
        pT = [v3(sbuf2(TT * T), 4) for _ in range(2)]
        gtmp = sbuf2(512)
        used2 = m2_used + 4 * TT * T + 512

        def branch_area():
            return area(work[:, used2:], extra)
        b0 = branch_area()
        qm = v3(b0(TT * EH * EQ), TT)
        qmT = v3(b0(2 * T), 2)
        qsq = v3(b0(TT * EH * EQ), TT)
        b1 = branch_area()
        gv, gr = v3(b1(TT * D), TT), v3(b1(TT * D), TT)
        gqT, gkT = v3(b1(GH * T), GH), v3(b1(GH * T), GH)
        gbT = v3(b1(GH * T), GH)
        lev, qk = v3(b1(GH * T), GH), v3(b1(GH * T), GH)
        att = [v3(b1(GH * P), GH) for _ in range(3)]
        la, lt = v3(b1(TT * GH * DK), TT), v3(b1(TT * GH * DK), TT)
        ga = b1(TT * GRANK)
        gaT = b1(T)
        wgate = b1(GH * DK)
        bgla = b1(GH * DK)
        ggla = b1(DV)
        b2 = branch_area()
        q = v3(b2(TT * MH * (NOPE + ROPE)), TT)
        ckv = v3(b2(TT * (KVR + ROPE)), TT)
        kv = v3(b2(TT * MH * (NOPE + VD)), TT)
        qnT, qrT = v3(b2(MH * T), MH), v3(b2(4 * T), 4)
        knT, krT = v3(b2(MH * T), MH), b2(T)
        ckT = v3(b2(2 * T), 2)
        ropeb = v3(b2(TT * MH * ROPE), TT)
        kr2 = v3(b2(TT * 2 * ROPE), TT)
        nsq = b2(MH * NOPE)
        aT = v3(area(work[:, :])(4 * D * 2), 4 * D // P)

        S = {}

        def ev(name):
            if name not in S:
                S[name] = sem(name)
            return S[name]
        ps = PsumBanks(banks, {r: ev(f"bank_filled_for_{r}") for r in ("dve", "act")},
                       {r: ev(f"bank_drained_by_{r}") for r in ("dve", "act")})
        ps2 = PsumBanks(banks, {r: ev(f"late_bank_filled_for_{r}") for r in ("dve", "act")},
                        {r: ev(f"late_bank_drained_by_{r}") for r in ("dve", "act")})
        slots = [ring_mem[:, i * 4096:(i + 1) * 4096] for i in range(6)]
        ring = WeightRing(ps, slots, [ev(f"weights_landed_{i}") for i in range(6)])
        ring2 = WeightRing(ps2, slots[:4], [ev(f"late_weights_landed_{i}") for i in range(4)])
        xw_landed = [ev(f"expert_weights_landed_{i}") for i in range(6)]

        cs = tiny(KD)
        ctmp = tiny(KD)
        modc = tiny(48)
        mrow = [y_f[0:1, 512:1024], y_f[0:1, 1024:1536]]
        ss = tiny(2)
        rs = tiny(40)
        rt = [tiny(40) for _ in range(2)]
        dt_b, alog_b, dskip_b = tiny(HEADS), tiny(HEADS), tiny(HEADS)
        dtr, dta, dtv, dte_ = (v3(tiny(TT * HEADS), TT) for _ in range(4))
        nega = tiny(HEADS)
        acs = v3(tiny(3 * HEADS), 3)
        eacs, dte = tiny(HEADS), tiny(HEADS)
        gss = tiny(TT * GROUPS)
        rb = tiny(EG + NE)
        lg = v3(tiny(TT * (EG + NE)), TT)
        gm, pg, gsm = tiny(TT), tiny(TT), tiny(TT)
        ohg = v3(tiny(TT * EG), TT)
        gtm = v3(tiny(TT * EG), TT)
        w8, oh1, oh2, t8 = (v3(tiny(TT * EPG), TT) for _ in range(4))
        v1, v2, e2, gate1, gate2 = (tiny(TT) for _ in range(5))
        route_area = area(acc_f[:, 0:D])
        wide = route_area(TT * NE)
        sel1, sel2, sel = (v3(route_area(TT * NE), TT) for _ in range(3))
        cnt, nblk = route_area(NE), route_area(NE)
        cumA, cumB = route_area(2 * NE), route_area(2 * NE)
        slot_of = v3(route_area(TT * NE), TT)
        dest = [tiny(TT) for _ in range(2)]
        be, slot_col = tiny(1), tiny(1)
        meta = tiny(P + 2, I32)
        npf = tiny(1)
        pos_i, pos_f = tiny(TT, I32), tiny(TT)
        NI = ROPE // 2
        ang, rn, cosv, sinv = (v3(tiny(TT * NI), TT) for _ in range(4))
        mxs, sums = [tiny(TT) for _ in range(2)], [tiny(TT) for _ in range(2)]
        hss = tiny(TT * (2 * MH + 2))

        def k_rows(w, cols):
            return w.rearrange("(k p) n -> p k n", p=P)[:, :, cols]

        w_ada, w_in, w_out = a["w_ada"][0], a["w_in"][0], a["w_out"][0]
        w13, w2 = a["w13"][0], a["w2"][0]
        w_in2, w_ukv, w_mkv = a["w_in_2"][0], a["w_ukv_2"][0], a["w_mem_kv_2"][0]
        w_o2, w_up, w_down = a["w_o_2"][0], a["w_up_2"][0], a["w_down_2"][0]

        def cols_of(n, k=KD):
            return lambda s: s[:, 0:k * n].rearrange("p (k n) -> p k n", k=k)

        block = ctx.enter_context(nc.Block())
        ADA1, ADA2 = range(0, 4), range(4, 12)
        IN_SLOTS = [(i * 512, min(512, IN1 - i * 512)) for i in range(6)]
        MEM_SLOTS = [(0, 512), (512, 512), (1024, 256)]
        LATE_A = ([("mq", O_MQ, 256), ("gate2_0", O_GATE + 2048, 512), ("gate2_1", O_GATE + 2560, 512),
                   ("gq", O_GQ, 512), ("gk", O_GK, 512), ("ga", O_GA, 16), ("gv0", O_GV, 512), ("gv1", O_GV + 512, 512),
                   ("gr0", O_GR, 512), ("gr1", O_GR + 512, 512), ("gate1_0", O_GATE + 1024, 512),
                   ("gate1_1", O_GATE + 1536, 512), ("ckv", O_CKV, 320), ("q0", O_Q, 512), ("q1", 512, 512),
                   ("q2", 1024, 512)])
        LATE_B = [("gate0_0", O_GATE, 512), ("gate0_1", O_GATE + 512, 512)]

        @block.tensor
        def _(pe):
            mm = nc.tensor.matmul

            def transposes(ps, name, reader, pieces):
                bank = ps.fill(pe, name, reader)
                for src, col in pieces:
                    n, w = src.shape[0], src.shape[1]
                    last = nc.tensor.transpose(bank[0:w, col:col + n], src, ident[0:n, 0:n])
                ps.full(name, last)

            def all_channels(ps, name, src):
                for j in range(4):
                    transposes(ps, f"{name}{j}", ("dve", "act")[j % 2],
                               [(src[:, t, (2 * j + b) * P:(2 * j + b + 1) * P], b * T + t * P)
                                for b in range(2) for t in range(TT)])

            def tokens_out(ps, name, reader, lhs, w, width, col=0, k=KD):
                for t in range(TT):
                    bank = ps.fill(pe, f"{name}t{t}", reader)
                    for j in range(k):
                        last = mm(bank[:, 0:width], lhs[:, j, t * P:t * P + P], w[:, j, col:col + width],
                                  start=(j == 0), stop=(j == k - 1))
                    ps.full(f"{name}t{t}", last)

            def channels_out(ps, name, reader, lhs, w, col):
                bank = ps.fill(pe, name, reader)
                for b in range(2):
                    for j in range(KD):
                        last = mm(bank[:, b * T:b * T + T], w[:, j, col + b * P:col + b * P + P], lhs[:, j, :],
                                  start=(j == 0), stop=(j == KD - 1))
                ps.full(name, last)

            pe.wait_ge(ev("constants_loaded"), 16)
            pe.wait_ge(ev("param_rows_loaded"), 160)
            transposes(ps, "params", "dve", [(prm_rows[0:NROWS, 0:P], 0), (prm_rows[0:48, P:2 * P], NROWS)])

            def ada(n):
                w = cols_of(512)(ring.take(pe))
                if n == 0:
                    pe.wait_ge(ev("c_gated"), 1)
                bank = ps.fill(pe, f"ada{n}", "dve")
                for k in range(KD):
                    last = mm(bank[0:1, :], cs[:, k:k + 1], w[:, k, :], start=(k == 0), stop=(k == KD - 1))
                ps.full(f"ada{n}", last)
                ring.last_use(f"ada{n}")

            def ada_spread(n):
                ps.wait_drained(pe, f"ada{n}")
                bank = ps.fill(pe, f"adaT{n}", "dve")
                if n // 2 in (2, 5):
                    last = mm(bank[:, :], ones[0:1, :], mrow[n % 2], start=True, stop=True)
                else:
                    for j in range(4):
                        last = mm(bank[:, j:j + 1], mrow[n % 2][:, j * P:j * P + P], ones[0:1, 0:1],
                                  start=True, stop=True)
                ps.full(f"adaT{n}", last)

            for n in ADA1:
                ada(n)
                if n:
                    ada_spread(n - 1)
            ada_spread(ADA1[-1])

            pe.wait_ge(ev("x_normed"), 1)
            all_channels(ps, "h1", xn)
            for j in range(4):
                ps.wait_drained(pe, f"h1{j}")
            w = cols_of(512)(ring.take(pe))
            channels_out(ps, "u", "act", hT, w, 0)
            bank = ps.fill(pe, "z0", "act")
            for t in range(TT):
                for j in range(KD):
                    last = mm(bank[:, t * 256:t * 256 + 256], hT[:, j, t * P:t * P + P], w[:, j, 256:512],
                              start=(j == 0), stop=(j == KD - 1))
            ps.full("z0", last)
            ring.last_use("z0")
            w = cols_of(512)(ring.take(pe))
            tokens_out(ps, "z1", "act", hT, w, 512)
            ring.last_use("z1t1")
            for s_ in range(2, 6):
                wd = IN_SLOTS[s_][1]
                w = cols_of(wd)(ring.take(pe))
                channels_out(ps, f"xb{2 * (s_ - 2)}", "act", hT, w, 0)
                if s_ < 5:
                    channels_out(ps, f"xb{2 * (s_ - 2) + 1}", "act", hT, w, 256)
                    ring.last_use(f"xb{2 * (s_ - 2) + 1}")
                else:
                    bank = ps.fill(pe, "dt", "dve")
                    for t in range(TT):
                        for j in range(KD):
                            last = mm(bank[:, t * HEADS:(t + 1) * HEADS], hT[:, j, t * P:t * P + P],
                                      w[:, j, 256:256 + HEADS], start=(j == 0), stop=(j == KD - 1))
                    ps.full("dt", last)
                    ring.last_use("dt")
            for n in ADA2:
                ada(n)
                if n > ADA2[0]:
                    ada_spread(n - 1)
            ada_spread(ADA2[-1])
            pe.wait_ge(ev("pool_weights_loaded"), 64)
            pe.wait_ge(ev("pooled"), 1)
            bank = ps.fill(pe, "pool", "act")
            for b in range(2):
                last = mm(bank[:, b * T:b * T + T], wpool[:, b, :], diff[:, b, :], start=True, stop=True)
            ps.full("pool", last)
            pe.wait_ge(ev("decay_steps"), 1)
            bank = ps.fill(pe, "acs", "dve")
            for t in range(TT):
                mm(bank[:, t * HEADS:(t + 1) * HEADS], C["tri"], dta[:, t, :], start=True, stop=True)
            last = mm(bank[:, 2 * HEADS:3 * HEADS], ones, dta[:, 0, :], start=True, stop=True)
            ps.full("acs", last)
            pe.wait_ge(ev("conv_gated"), 4)
            for t in range(TT):
                lots = ((0, 4), (4, 8), (8, 10)) if t == 0 else ((0, 4), (4, 6))
                for lo, hi in lots:
                    transposes(ps, f"xs{t}_{lo}", "act",
                               [(xb[:, k, t * P:t * P + P], (k - lo) * P) for k in range(lo, hi)])
            def decays(t, g):
                bank = ps.fill(pe, f"row{t}{g}", "dve")
                for r in range(RPG):
                    h = RPG * g + r
                    last = mm(bank[:, r * P:r * P + P], dta[:, t, h:h + 1].to_broadcast([P, P]), C["tri"],
                              start=True, stop=True)
                ps.full(f"row{t}{g}", last)
                bank = ps.fill(pe, f"cb{t}{g}", "dve")
                last = mm(bank[:, 0:P], xb[:, 6 + g, t * P:t * P + P], xb[:, 10 + g, t * P:t * P + P],
                          start=True, stop=True)
                ps.full(f"cb{t}{g}", last)

            def diagonal(t, g):
                ps.wait_drained(pe, f"cb{t}{g}")
                pe.wait_ge(ev("xdt_ready"), 1)
                bank = ps.fill(pe, f"yd{t}{g}", "dve")
                for r in range(RPG):
                    h = RPG * g + r
                    last = mm(bank[:, r * HD:r * HD + HD], seg2[:, r, :], xdt[:, t, h * HD:h * HD + HD],
                              start=True, stop=True)
                ps.full(f"yd{t}{g}", last)
            for g in range(GROUPS):
                decays(0, g)
                diagonal(0, g)
            pe.wait_ge(ev("xcd_ready"), 1)
            for g in range(GROUPS):
                bank = ps.fill(pe, f"state{g}", "dve")
                last = mm(bank[:, 0:RPG * HD], xtok[:, 0, SSD_W + g * P:SSD_W + g * P + P],
                          xcd[:, g * RPG * HD:(g + 1) * RPG * HD], start=True, stop=True)
                ps.full(f"state{g}", last)
            for g in range(GROUPS):
                ps.wait_drained(pe, f"state{g}")
                decays(1, g)
                diagonal(1, g)
                bank = ps.fill(pe, f"yo{g}", "dve")
                last = mm(bank[:, 0:RPG * HD], xb[:, 10 + g, P:2 * P], prevT[:, g, :], start=True, stop=True)
                ps.full(f"yo{g}", last)
            pe.wait_ge(ev("ssd_normed"), 1)
            for j in range(3):
                transposes(ps, f"yT{j}", "act", [(yv[:, t, (2 * j + b) * P:(2 * j + b + 1) * P], b * T + t * P)
                                                for b in range(2) for t in range(TT)])
            for j in range(3):
                ps.wait_drained(pe, f"yT{j}")
            for n in range(2):
                w = cols_of(512)(ring.take(pe))
                tokens_out(ps, f"mix{n}", "dve", mixT, w, 512)
                ring.last_use(f"mix{n}t1")
            pe.wait_ge(ev("mem_normed"), 1)
            all_channels(ps, "memT", mem_x)
            for j in range(4):
                ps.wait_drained(pe, f"memT{j}")
            w = cols_of(512)(ring.take(pe))
            tokens_out(ps, "mk", "dve", memT, w, 256)
            tokens_out(ps, "mv0", "act", memT, w, 256, col=256)
            ring.last_use("mv0t1")
            w = cols_of(512)(ring.take(pe))
            tokens_out(ps, "mv1", "act", memT, w, 512)
            ring.last_use("mv1t1")
            w = cols_of(256)(ring.take(pe))
            tokens_out(ps, "mv2", "act", memT, w, 256)
            ring.last_use("mv2t1")
            pe.wait_ge(ev("mem_keys_normed"), 1)
            transposes(ps, "mkT", "act", [(mk[:, t, b * P:b * P + P], b * T + t * P)
                                          for b in range(2) for t in range(TT)])
            pe.wait_ge(ev("x_normed"), 2)
            all_channels(ps, "h2", xn)
            for j in range(4):
                ps.wait_drained(pe, f"h2{j}")
            pe.wait_ge(ev("router_loaded"), 32)
            tokens_out(ps, "router", "dve", hT, wr, EG + NE)
            pe.wait_ge(ev("chosen"), 1)
            bank = ps.fill(pe, "rank", "dve")
            mm(bank[:, 0:NE], C["strict"], sel[:, 0, :], start=True, stop=True)
            mm(bank[:, NE:2 * NE], ones, sel[:, 0, :], start=True, stop=False)
            mm(bank[:, NE:2 * NE], C["strict"], sel[:, 1, :], start=False, stop=True)
            mm(bank[:, 2 * NE:3 * NE], ones, sel[:, 0, :], start=True, stop=False)
            last = mm(bank[:, 2 * NE:3 * NE], ones, sel[:, 1, :], start=False, stop=True)
            ps.full("rank", last)
            pe.wait_ge(ev("block_experts"), 1)
            bank = ps.fill(pe, "experts", "dve")
            last = mm(bank[0:1, 0:P], be, ident, start=True, stop=True)
            ps.full("experts", last)

            pe.wait_ge(ev("routed"), 1)
            pairs = pe.value_load(meta[0:1, P:P + 1], min_val=4, max_val=MAXB // 2)
            last_pair = pe.value_load(meta[0:1, P + 1:P + 2], min_val=3, max_val=MAXB // 2 - 1)
            gA, gB, hA, hB, tA, tB, oA, oB = banks

            def gather(i):
                pe.wait_ge(ev("slots_picked"), i + 1)
                for k in range(KD):
                    dst = (gA, gB)[k // 4][:, (k % 4) * P:(k % 4) * P + P]
                    for t in range(TT):
                        last = mm(dst, xn[:, t, k * P:k * P + P], pick[:, t, :], start=(t == 0), stop=(t == TT - 1))
                    if k % 4 == 3:
                        last.then_inc(ev("gather_filled"), 1)

            def hidden(i, b):
                if b == 0:
                    pe.wait_ge(ev("slots_in_by_act"), i + 1)
                    pe.wait_ge(ev("slots_in_by_dve"), i + 1)
                    pe.wait_ge(ev("hidden_out_by_act"), i * 2)
                    pe.wait_ge(ev("hidden_out_by_dve"), i * 2)
                else:
                    pe.wait_ge(ev("hidden_out_by_act"), i * 2 + 1)
                    pe.wait_ge(ev("hidden_out_by_dve"), i * 2 + 1)
                for part in range(2):
                    pe.wait_ge(xw_landed[3 * b + part], i * 16 + 16)
                w = [slots[3 * b + part].rearrange("p (k n) -> p k n", k=4) for part in range(2)]
                for n, dst in enumerate((hA, hB)):
                    for k in range(4):
                        for part in range(2):
                            last = mm(dst[SLOTS * part:SLOTS * part + SLOTS, :],
                                      xeT[:, 4 * part + k, b * SLOTS:b * SLOTS + SLOTS],
                                      w[part][:, k, n * 512:n * 512 + 512], start=(k == 0), stop=(k == 3))
                    last.then_inc(ev("hidden_filled"), 1)

            def fold(i, b):
                pe.wait_ge(ev("hidden_out_by_act"), i * 2 + (b + 1))
                pe.wait_ge(ev("hidden_out_by_dve"), i * 2 + (b + 1))
                pe.wait_ge(ev("hidden_gated"), i * 2 + b)
                for f in range(8):
                    last = mm((tA, tB)[f // 4][:, (f % 4) * P:(f % 4) * P + 96], hs[:, f * P:f * P + P],
                              C["fold"][:, 0:96], start=True, stop=True)
                    if f % 4 == 3:
                        last.then_inc(ev("folded"), 1)

            def rows_out(m):
                pe.wait_ge(ev("hidden_gated"), m * 2 + 2)
                pe.wait_ge(ev("parts_added"), m * 4)
                for b in range(2):
                    pe.wait_ge(xw_landed[3 * b + 2], m * 16 + 16)
                w = [slots[3 * b + 2].rearrange("p (k n) -> p k n", k=4) for b in range(2)]
                for n_, dst in enumerate((oA, oB)):
                    for f in range(4):
                        for b in range(2):
                            last = mm(dst[SLOTS * b:SLOTS * b + SLOTS, :], sT[b][:, f, :],
                                      w[b][:, f, n_ * 512:n_ * 512 + 512], start=(f == 0), stop=(f == 3))
                    last.then_inc(ev(("rows_filled_for_act", "rows_filled_for_dve")[n_]), 1)

            def combine(m, t):
                if t == 0:
                    pe.wait_ge(ev("rows_out_by_act"), m + 1)
                    pe.wait_ge(ev("rows_out_by_dve"), m + 1)
                    pe.wait_ge(ev("shares_ready"), m + 1)
                else:
                    pe.wait_ge(ev("parts_added"), m * 4 + 2)
                for n_, dst in enumerate((oA, oB)):
                    mm(dst[:, :], share_f[:, t * P:t * P + P], osb[:, n_ * 512:n_ * 512 + 512], start=True,
                       stop=True).then_inc(ev("parts_filled"), 1)

            for n, name in enumerate(("slot_rows", "gate_rows")):
                pe.wait_ge(ev("columns_spread"), 4 * n + 4)
                bank = ps.fill(pe, name, ("dve", "act")[n])
                for m in range(4):
                    last = mm(bank[:, m * P:m * P + P], ones, diag[:, 4 * n + m, :], start=True, stop=True)
                ps.full(name, last)
            for r in ("dve", "act"):
                pe.wait_ge(ps.drained[r], ps.count[r])
            gather(0)
            hidden(0, 0)
            fold(0, 0)
            hidden(0, 1)
            gather(1)
            fold(0, 1)
            with pe.Fori(1, pairs) as i:
                hidden(i, 0)
                rows_out(i - 1)
                fold(i, 0)
                hidden(i, 1)
                combine(i - 1, 0)
                gather(i + 1)
                fold(i, 1)
                combine(i - 1, 1)
            rows_out(last_pair)
            combine(last_pair, 0)
            combine(last_pair, 1)

            def softmax_products(name, qs, ks):
                bank = ps2.fill(pe, f"s_{name}", "dve")
                for t in range(TT):
                    n = len(qs)
                    for m, (qa, ka) in enumerate(zip(qs, ks)):
                        last = mm(bank[:, t * T:t * T + T], qa[:, t * P:t * P + P], ka, start=(m == 0), stop=(m == n - 1))
                ps2.full(f"s_{name}", last)

            def softmax_transposes(name, idx):
                pe.wait_ge(ev("probs_ready"), idx + 1)
                transposes(ps2, f"pT_{name}", "act", [(pr[idx % 2][:, t, k * P:k * P + P], (t * 2 + k) * P)
                                                     for t in range(TT) for k in range(2)])

            def softmax_values(name, idx, value, width):
                ps2.wait_drained(pe, f"pT_{name}")
                bank = ps2.fill(pe, f"o_{name}", "dve")
                for t in range(TT):
                    for k in range(2):
                        last = mm(bank[:, t * width:t * width + width], pT[idx % 2][:, t * 2 + k, :], value(k),
                                  start=(k == 0), stop=(k == 1))
                ps2.full(f"o_{name}", last)

            def attention(heads, args, first, value, width):
                for h in range(heads + 1):
                    if h < heads:
                        softmax_products(f"{first + h}", *args(h))
                    if h:
                        softmax_transposes(f"{first + h - 1}", first + h - 1)
                        softmax_values(f"{first + h - 1}", first + h - 1, value(h - 1), width)

            def gates(br):
                for n in range(2):
                    w = cols_of(512)(ring2.take(pe))
                    tokens_out(ps2, f"gate{br}{n}", "dve", hT, w, 512)
                    ring2.last_use(f"gate{br}{n}t1")

            pe.wait_ge(ev("parts_added"), pairs * 4)
            pe.wait_ge(ev("x_normed"), 3)
            all_channels(ps2, "h3", xn)
            for j in range(4):
                ps2.wait_drained(pe, f"h3{j}")
            w = cols_of(256)(ring2.take(pe))
            tokens_out(ps2, "mq", "dve", hT, w, 256)
            ring2.last_use("mqt1")
            pe.wait_ge(ev("mem_q_normed"), 1)
            transposes(ps2, "mqT", "act", [(qm[:, t, b * P:b * P + P], b * T + t * P)
                                           for b in range(2) for t in range(TT)])
            ps2.wait_drained(pe, "mqT")
            attention(EH, lambda h: ([qmT[64 * (h % 2):64 * (h % 2) + 64, h // 2, :]],
                                     [kmT[64 * (h % 2):64 * (h % 2) + 64, h // 2, :]]), 0,
                      lambda h: lambda k: vm[:, k, h * EV:h * EV + EV], EV)
            gates(2)
            for nm in ("gq", "gk"):
                w = cols_of(512)(ring2.take(pe))
                for b in range(2):
                    channels_out(ps2, f"{nm}{b}", "act", hT, w, b * 256)
                ring2.last_use(f"{nm}1")
            w = cols_of(GRANK)(ring2.take(pe))
            bank = ps2.fill(pe, "ga", "act")
            for j in range(KD):
                last = mm(bank[0:GRANK, 0:T], w[:, j, :], hT[:, j, :], start=(j == 0), stop=(j == KD - 1))
            ps2.full("ga", last)
            ring2.last_use("ga")
            for nm in ("gv", "gr"):
                for n in range(2):
                    w = cols_of(512)(ring2.take(pe))
                    tokens_out(ps2, f"{nm}{n}", "act", hT, w, 512)
                    ring2.last_use(f"{nm}{n}t1")
                if nm == "gv":
                    ps2.wait_drained(pe, "ga")
                    pe.wait_ge(ev("gla_rows_loaded"), 48)
                    for t in range(TT):
                        bank = ps2.fill(pe, f"lg{t}", "dve")
                        last = mm(bank[:, :], gaT[0:GRANK, t * P:t * P + P], wgate[0:GRANK, :], start=True, stop=True)
                        ps2.full(f"lg{t}", last)
            pe.wait_ge(ev("log_decays"), 1)
            for j in range(2):
                bank = ps2.fill(pe, f"cum{j}", "act")
                for b in range(2):
                    for t in range(TT):
                        h = 2 * j + b
                        last = mm(bank[:, b * T + t * P:b * T + t * P + P], la[:, t, h * DK:h * DK + DK], C["tri"],
                                  start=True, stop=True)
                ps2.full(f"cum{j}", last)
            for lvl in range(LEVELS + 1):
                if lvl == 0:
                    ps2.wait_drained(pe, "gk1")
                else:
                    pe.wait_ge(ev("level_ready"), lvl)
                for t in range(TT):
                    bank = ps2.fill(pe, f"lvl{lvl}{t}", "dve")
                    for h in range(GH):
                        k_ = (gkT if lvl == 0 else qk)[:, h, t * P:t * P + P]
                        q_ = (gqT if lvl == 0 else qk)[:, h, t * P:t * P + P]
                        last = mm(bank[:, h * P:h * P + P], k_, q_, start=True, stop=True)
                    ps2.full(f"lvl{lvl}{t}", last)
            pe.wait_ge(ev("level_ready"), LEVELS + 1)
            bank = ps2.fill(pe, "cross", "act")
            for h in range(GH):
                last = mm(bank[:, h * P:h * P + P], qk[:, h, 0:P], qk[:, h, P:2 * P], start=True, stop=True)
            ps2.full("cross", last)
            ps2.wait_drained(pe, f"lvl{LEVELS}1")
            ps2.wait_drained(pe, "cross")
            for h in range(GH):
                bank = ps2.fill(pe, f"go{h}", "dve")
                mm(bank[:, 0:DV], att[0][:, h, :], gv[:, 0, h * DV:h * DV + DV], start=True, stop=True)
                mm(bank[:, DV:2 * DV], att[2][:, h, :], gv[:, 0, h * DV:h * DV + DV], start=True, stop=False)
                last = mm(bank[:, DV:2 * DV], att[1][:, h, :], gv[:, 1, h * DV:h * DV + DV], start=False, stop=True)
                ps2.full(f"go{h}", last)
            gates(1)
            pe.wait_ge(ev("gla_done"), 1)
            w = cols_of(320)(ring2.take(pe))
            tokens_out(ps2, "ckv", "dve", hT, w, 320)
            ring2.last_use("ckvt1")
            for n in range(3):
                w = cols_of(512)(ring2.take(pe))
                tokens_out(ps2, f"q{n}", "act", hT, w, 512)
                ring2.last_use(f"q{n}t1")
            pe.wait_ge(ev("ckv_normed"), 1)
            transposes(ps2, "ckT", "act", [(ckv[:, t, b * P:b * P + P], b * T + t * P)
                                           for b in range(2) for t in range(TT)])
            ps2.wait_drained(pe, "ckT")
            w = cols_of(2048, 2)(ring2.take(pe))
            for n in range(4):
                tokens_out(ps2, f"kv{n}", "act", ckT, w, 512, col=n * 512, k=2)
            ring2.last_use("kv3t1")
            pe.wait_ge(ev("rope_k_ready"), 1)
            transposes(ps2, "krT", "act", [(kr2[:, t, :], t * P) for t in range(TT)])
            pe.wait_ge(ev("mla_q_ready"), 1)
            for j in range(4):
                transposes(ps2, f"qnT{j}", "act", [(q[:, t, (2 * j + b) * 192:(2 * j + b) * 192 + P], b * T + t * P)
                                                  for b in range(2) for t in range(TT)])
            for j in range(2):
                transposes(ps2, f"qrT{j}", "act", [(ropeb[:, t, (2 * j + b) * P:(2 * j + b + 1) * P], b * T + t * P)
                                                  for b in range(2) for t in range(TT)])
            pe.wait_ge(ev("mla_k_ready"), 1)
            for j in range(4):
                transposes(ps2, f"knT{j}", "act",
                           [(kv[:, t, (2 * j + b) * 256:(2 * j + b) * 256 + P], b * T + t * P)
                            for b in range(2) for t in range(TT)])
            for j in range(4):
                ps2.wait_drained(pe, f"knT{j}")

            def mla_args(h):
                lo = 64 * (h % 2)
                return ([qnT[:, h, :], qrT[lo:lo + 64, h // 2, :]], [knT[:, h, :], krT[lo:lo + 64, :]])
            attention(MH, mla_args, EH, lambda h: lambda k: kv[:, k, h * 256 + P:h * 256 + 256], VD)
            gates(0)
            pe.wait_ge(ev("branches_summed"), 1)
            all_channels(ps2, "ysT", ysum)
            for j in range(4):
                ps2.wait_drained(pe, f"ysT{j}")
            for n in range(2):
                w = cols_of(512)(ring2.take(pe))
                tokens_out(ps2, f"wo{n}", "dve", hT, w, 512)
                ring2.last_use(f"wo{n}t1")
            pe.wait_ge(ev("x_normed"), 4)
            all_channels(ps2, "h4", xn)
            for j in range(4):
                ps2.wait_drained(pe, f"h4{j}")
            for n in range(8):
                w = cols_of(512)(ring2.take(pe))
                for b in range(2):
                    channels_out(ps2, f"up{n}{b}", "act", hT, w, b * 256)
                ring2.last_use(f"up{n}1")
            accs = [ps2.fill(pe, f"down{t}{n}", "dve") for t in range(TT) for n in range(2)]
            for g in range(8):
                w = cols_of(D, 4)(ring2.take(pe))
                pe.wait_ge(ev("ffn_squared"), 2 * g + 2)
                for m, acc in enumerate(accs):
                    t, n = m // 2, m % 2
                    for j in range(4):
                        last = mm(acc[:, :], aT[:, 4 * g + j, t * P:t * P + P], w[:, j, n * 512:n * 512 + 512],
                                  start=(g == 0 and j == 0), stop=(g == 7 and j == 3))
                    if g == 7:
                        ps2.full(f"down{t}{n}", last)
                    elif m == 3:
                        last.then_inc(ev("down_weights_used"), 1)
                ring2.last_use((ev("down_weights_used"), g + 1))
        @block.scalar
        def _(act):
            do = Chained(act, ev("act_step"))
            A = nc.scalar.activation

            def raise_(name):
                act.sem_inc(ev(name), 1)

            def drain(ps, name, pairs, scale=None, shift=None):
                bank = ps.read(act, name, "act")
                for n, (dst, src) in enumerate(pairs(bank)):
                    sc, sh = (scale[n] if scale else 1.0), (shift[n] if shift else 0.0)
                    ins = A(dst, src, ACT.Identity, bias=sh, scale=sc)
                    if n == len(pairs(bank)) - 1:
                        ps.release(name, ins, act)
                    else:
                        do(ins)

            def to_channels(ps, name, dst, scale, shift):
                for j in (1, 3):
                    drain(ps, f"{name}{j}", lambda bank: [(dst[:, 2 * j + b, :], bank[:, b * T:b * T + T]) for b in range(2)],
                          [scale if isinstance(scale, float) else scale[:, 2 * j + b:2 * j + b + 1] for b in range(2)],
                          [shift[:, 2 * j + b:2 * j + b + 1] for b in range(2)] if shift is not None else None)

            ps.wait_drained(act, "params")
            do(A(ctmp, prm[:, 0:8], ACT.Tanh, scale=0.5))
            raise_("c_tanh")
            act.wait_ge(ev("x_loaded"), 16)
            for t in range(TT):
                do(A(hT_sb[:, 0:D], x[:, t, :], ACT.Square, accum_out=ss[:, t:t + 1]))
            raise_("squares")
            ps.wait_drained(act, "adaT3")
            to_channels(ps, "h1", hT, modc[:, 8:16], modc[:, 0:8])
            act.wait_ge(ev("pads_zeroed"), 1)
            drain(ps, "u", lambda bank: [(uT[:, :, PAD:PAD + T], v3(bank[:, :], 2))])
            drain(ps, "z0", lambda bank: [(z[:, :, 0:256], v3(bank[:, :], 2))], [0.5])
            for t in range(TT):
                drain(ps, f"z1t{t}", lambda bank: [(z[:, t, 256:768], bank[:, :])], [0.5])
            for n in range(4):
                for j in (2 * n, 2 * n + 1):
                    if j < 7:
                        drain(ps, f"xb{j}", lambda bank: [(raw[:, 2 * j:2 * j + 2, 3:3 + T], v3(bank[:, :], 2))])
                act.wait_ge(ev("conv_batch"), n + 1)
                w = 4 if n < 3 else 2
                do(A(ce[:, 0:w, :], cv[:, 0:w, :], ACT.Tanh))
                raise_("conv_tanh")
            act.wait_ge(ev("dt_abs"), 1)
            do(A(flat(dta), flat(dta), ACT.Exp, scale=-1.0))
            do(A(flat(dta), flat(dta), ACT.Ln, bias=1.0))
            do(A(nega, alog_b, ACT.Exp))
            raise_("dt_log")
            for t in range(TT):
                act.wait_ge(ev("ce_free"), t + 1)
                do(A(ce_f[:, 0:SSD_W], z[:, t, :], ACT.Tanh))
                raise_("z_tanh")
            drain(ps, "pool", lambda bank: [(mixT[:, b, :], bank[:, b * T:b * T + T]) for b in range(2)],
                  [prm[:, ROWS["pool_scale"] + b:ROWS["pool_scale"] + b + 1] for b in range(2)])
            act.wait_ge(ev("decay_sums"), 1)
            do(A(dte, dte, ACT.Exp))
            do(A(eacs, acs[:, 1, :], ACT.Exp))
            raise_("decay_exps")
            act.wait_ge(ev("conv_gated"), 4)
            for t in range(TT):
                for lo, hi in (((0, 4), (4, 8), (8, 10)) if t == 0 else ((0, 4), (4, 6))):
                    drain(ps, f"xs{t}_{lo}", lambda bank: [(xtok[:, t, lo * P:hi * P], bank[:, 0:(hi - lo) * P])])
            for n in range(TT * GROUPS):
                act.wait_ge(ev("segment_sums"), n + 1)
                do(A(seg, seg, ACT.Exp))
                raise_("segment_exps")
            for j in range(3):
                drain(ps, f"yT{j}", lambda bank: [(mixT[:, 2 + 2 * j + b, :], bank[:, b * T:b * T + T]) for b in range(2)],
                      [prm[:, ROWS["ssd_norm_w"] + 2 * j + b:ROWS["ssd_norm_w"] + 2 * j + b + 1] for b in range(2)])
            act.wait_ge(ev("memory_loaded"), 16)
            for t in range(TT):
                do(A(ce_f, mem_x[:, t, :], ACT.Square, accum_out=ss[:, t:t + 1]))
            raise_("squares")
            to_channels(ps, "memT", memT, prm[:, ROWS["g_mem"]:ROWS["g_mem"] + 8], None)
            for t in range(TT):
                drain(ps, f"mv0t{t}", lambda bank: [(vm[:, t, 0:256], bank[:, 0:256])])
            for t in range(TT):
                drain(ps, f"mv1t{t}", lambda bank: [(vm[:, t, 256:768], bank[:, :])])
            for t in range(TT):
                drain(ps, f"mv2t{t}", lambda bank: [(vm[:, t, 768:1024], bank[:, 0:256])])
            drain(ps, "mkT", lambda bank: [(flat(kmT), bank[:, :])])
            act.wait_ge(ev("x_updated"), 1)
            for t in range(TT):
                do(A(hT_sb[:, 0:D], x[:, t, :], ACT.Square, accum_out=ss[:, t:t + 1]))
            raise_("squares")
            to_channels(ps, "h2", hT, modc[:, 32:40], modc[:, 24:32])
            act.wait_ge(ev("group_shifted"), 1)
            do(A(flat(gtm), flat(gtm), ACT.Exp))
            raise_("group_exps")
            act.wait_ge(ev("top_gap"), 1)
            do(A(e2, v2, ACT.Exp))
            raise_("top_exp")

            act.wait_ge(ev("routed"), 1)
            pairs = act.value_load(meta[0:1, P:P + 1], min_val=4, max_val=MAXB // 2)
            last_pair = act.value_load(meta[0:1, P + 1:P + 2], min_val=3, max_val=MAXB // 2 - 1)
            gA, gB, hA, hB, tA, tB, oA, oB = banks
            PER = 8

            def slots_in(i, lc):
                act.wait_ge(ev("gather_filled"), i * 2 + 1)
                for k in range(4):
                    ins = A(xeT[:, k, :], gA[:, k * P:k * P + P], ACT.Identity, scale=modc[:, 32 + k:33 + k],
                            bias=modc[:, 24 + k:25 + k])
                    if k < 3:
                        lc(ins)
                ins.then_inc(ev("slots_in_by_act"), 1)

            def hidden_out(i, b):
                act.wait_ge(ev("hidden_filled"), i * 4 + (2 * b + 1))
                A(hs[:, 0:512], hA[:, :], ACT.Identity).then_inc(ev("hidden_out_by_act"), 1)

            def gate_tanh(i, b, lc):
                act.wait_ge(ev("folded"), i * 4 + (2 * b + 1))
                A(ge, v3(tA[:, :], 4)[:, :, 0:SLOTS], ACT.Tanh, scale=0.5).then_inc(ev("gate_tanhs"), 1)

            def rows_out(m):
                act.wait_ge(ev("rows_filled_for_act"), m + 1)
                act.wait_ge(ev("parts_filled"), m * 4)
                A(osb[:, 0:512], oA[:, :], ACT.Identity).then_inc(ev("rows_out_by_act"), 1)

            def turn(i, lc, first):
                hidden_out(i, 0)
                if not first:
                    rows_out(i - 1)
                gate_tanh(i, 0, lc)
                hidden_out(i, 1)
                slots_in(i + 1, lc)
                gate_tanh(i, 1, lc)

            lead = Chained(act, ev("act_lead_step"))
            drain(ps, "gate_rows", lambda bank: [(gate_rows, bank[:, :])])
            slots_in(0, lead)
            turn(0, lead, True)
            with act.Fori(1, pairs) as i:
                lc = LoopChained(act, ev("act_expert_step"), i, 3)
                turn(i, lc, False)
                lc.end()
            rows_out(last_pair)

            act.wait_ge(ev("x_updated"), 2)
            for t in range(TT):
                do(A(hT_sb[:, 0:D], x[:, t, :], ACT.Square, accum_out=ss[:, t:t + 1]))
            raise_("squares")
            act.wait_ge(ev("x_updated"), 3)
            for t in range(TT):
                do(A(hT_sb[:, 0:D], x[:, t, :], ACT.Square, accum_out=ss[:, t:t + 1]))
            raise_("squares")
            to_channels(ps2, "h3", hT, prm[:, ROWS["g_mix"]:ROWS["g_mix"] + 8], None)
            act.wait_ge(ev("angles_ready"), 1)
            do(A(flat(sinv), flat(ang), ACT.Sin))
            do(A(flat(cosv), flat(rn), ACT.Sin))
            raise_("rope_tables")
            drain(ps2, "mqT", lambda bank: [(flat(qmT), bank[:, :])])

            def attention(heads, first, scale):
                for h in range(heads):
                    n = first + h
                    act.wait_ge(ev("scores_maxed"), n + 1)
                    for t in range(TT):
                        do(A(pr[n % 2][:, t, :], pr[n % 2][:, t, :], ACT.Exp, bias=mxs[n % 2][:, t:t + 1],
                             scale=scale, accum_out=sums[n % 2][:, t:t + 1]))
                    raise_("probs_ready")
                    drain(ps2, f"pT_{n}", lambda bank: [(flat(pT[n % 2]), bank[:, :])])
            attention(EH, 0, EQ ** -0.5)

            def gates(br):
                for n in range(2):
                    for t in range(TT):
                        k = gate_no[0]
                        act.wait_ge(ev("gate_logits"), k + 1)
                        do(A(gtmp, gtmp, ACT.Tanh, scale=0.5))
                        raise_("gate_tanh_done")
                        gate_no[0] += 1
            gate_no = [0]
            gates(2)
            drain(ps2, "gq0", lambda bank: [(flat(gqT)[:, 0:512], bank[:, :])], [DK ** -0.5])
            drain(ps2, "gq1", lambda bank: [(flat(gqT)[:, 512:1024], bank[:, :])], [DK ** -0.5])
            for b in range(2):
                drain(ps2, f"gk{b}", lambda bank: [(flat(gkT)[:, b * 512:b * 512 + 512], bank[:, :])])
            drain(ps2, "ga", lambda bank: [(gaT[0:GRANK, :], bank[0:GRANK, 0:T])])
            for n in range(2):
                for t in range(TT):
                    drain(ps2, f"gv{n}t{t}", lambda bank: [(gv[:, t, n * 512:n * 512 + 512], bank[:, :])])
            act.wait_ge(ev("log_arg"), 1)
            do(A(flat(lt), flat(lt), ACT.Exp, scale=-1.0))
            do(A(flat(lt), flat(lt), ACT.Ln, bias=1.0))
            raise_("log_done")
            for n in range(2):
                for t in range(TT):
                    drain(ps2, f"gr{n}t{t}", lambda bank: [(gr[:, t, n * 512:n * 512 + 512], bank[:, :])], [0.5])
            for j in range(2):
                drain(ps2, f"cum{j}", lambda bank: [(flat(gbT)[:, j * 512:j * 512 + 512], bank[:, :])])
            for lvl in range(1, LEVELS + 2):
                act.wait_ge(ev("level_differences"), lvl)
                do(A(flat(lev), flat(lev), ACT.Exp))
                raise_("level_exps")
            drain(ps2, "cross", lambda bank: [(flat(att[2]), bank[:, :])])
            act.wait_ge(ev("gla_normed"), 1)
            for t in range(TT):
                do(A(flat(la)[:, 0:D] if t == 0 else flat(lt)[:, 0:D], gr[:, t, :], ACT.Tanh))
            raise_("r_tanh")
            gates(1)
            for n in range(3):
                for t in range(TT):
                    drain(ps2, f"q{n}t{t}", lambda bank: [(q[:, t, n * 512:n * 512 + 512], bank[:, :])])
            drain(ps2, "ckT", lambda bank: [(ckT[:, b, :], bank[:, b * T:b * T + T]) for b in range(2)],
                  [prm[:, ROWS["g_ckv"] + b:ROWS["g_ckv"] + b + 1] for b in range(2)])
            for n in range(4):
                for t in range(TT):
                    drain(ps2, f"kv{n}t{t}", lambda bank: [(kv[:, t, n * 512:n * 512 + 512], bank[:, :])])
            drain(ps2, "krT", lambda bank: [(krT, bank[:, 0:T])])
            for j in range(4):
                drain(ps2, f"qnT{j}", lambda bank: [(flat(qnT)[:, j * 512:j * 512 + 512], bank[:, :])])
            for j in range(2):
                drain(ps2, f"qrT{j}", lambda bank: [(flat(qrT)[:, j * 512:j * 512 + 512], bank[:, :])])
            for j in range(4):
                drain(ps2, f"knT{j}", lambda bank: [(flat(knT)[:, j * 512:j * 512 + 512], bank[:, :])])
            attention(MH, EH, (NOPE + ROPE) ** -0.5)
            gates(0)
            to_channels(ps2, "ysT", hT, 0.5, None)
            act.wait_ge(ev("x_updated"), 4)
            for t in range(TT):
                do(A(flat(ysum)[:, 0:D], x[:, t, :], ACT.Square, accum_out=ss[:, t:t + 1]))
            raise_("squares")
            to_channels(ps2, "h4", hT, prm[:, ROWS["g_ffn"]:ROWS["g_ffn"] + 8], None)
            for n in range(8):
                for b in range(2):
                    bank = ps2.read(act, f"up{n}{b}", "act")
                    ins = A(flat(aT)[:, (2 * n + b) * 512:(2 * n + b) * 512 + 512], bank[:, :], ACT.Relu)
                    ps2.release(f"up{n}{b}", ins, act)
        @block.vector
        def _(dve):
            do = Chained(dve, ev("dve_step"))
            spread = Signal(ev("columns_spread"))
            V = nc.vector

            def raise_(name):
                dve.sem_inc(ev(name), 1)

            def ts(out_, in_, s1, op0, s2=None, op1=ALU.bypass):
                return V.tensor_scalar(out_, in_, s1, s2, op0, op1)

            def tt(out_, x_, y_, op):
                return V.tensor_tensor(out_, x_, y_, op)

            def stt(out_, x_, s_, y_, op0, op1):
                return V.scalar_tensor_tensor(out_, x_, s_, y_, op0, op1)

            def rsqrt(dst, n, sums_, width):
                v, w = rt[0][:, 0:n], rt[1][:, 0:n]
                do(ts(v, sums_, 1.0 / width, ALU.mult, EPS, ALU.add))
                do(ts(w.bitcast(I32), v.bitcast(I32), 1, ALU.logical_shift_right))
                do(ts(dst.bitcast(I32), w.bitcast(I32), -1.0, ALU.mult, 1597463007.0, ALU.add))
                for _ in range(3):
                    do(tt(w, dst, dst, ALU.mult))
                    do(stt(w, w, -0.5, v, ALU.mult, ALU.mult))
                    do(stt(dst, w, 1.5, dst, ALU.add, ALU.mult))

            def times_sigmoid(dst, tanh_half, y_):
                do(stt(dst, tanh_half, 1.0, y_, ALU.add, ALU.mult))

            def to_channels(ps, name, dst, scale, shift):
                for j in (0, 2):
                    bank = ps.read(dve, f"{name}{j}", "dve")
                    for b in range(2):
                        c = 2 * j + b
                        o_, i_ = dst[:, c, :], bank[:, b * T:b * T + T]
                        if shift is not None:
                            ins = ts(o_, i_, scale[:, c:c + 1], ALU.mult, shift[:, c:c + 1], ALU.add)
                        elif scale is not None:
                            ins = ts(o_, i_, scale if isinstance(scale, float) else scale[:, c:c + 1], ALU.mult)
                        else:
                            ins = V.tensor_copy(o_, i_)
                        if b:
                            ps.release(f"{name}{j}", ins, dve)
                        else:
                            do(ins)

            norm_no = [0]

            def normalize(dst, src):
                norm_no[0] += 1
                dve.wait_ge(ev("squares"), norm_no[0])
                rsqrt(rs[:, 0:TT], TT, ss, D)
                for t in range(TT):
                    do(ts(dst[:, t, :], src[:, t, :], rs[:, t:t + 1], ALU.mult))

            bank = ps.read(dve, "params", "dve")
            ps.release("params", V.tensor_copy(prm[:, :], bank[:, 0:NROWS + 48]), dve)
            do(ts(cs, prm[:, 0:8], 0.5, ALU.mult))
            dve.wait_ge(ev("c_tanh"), 1)
            times_sigmoid(cs, ctmp, cs)
            raise_("c_gated")
            halved = prm[:, ROWS["conv_w"]:ROWS["conv_b"] + NXB]
            do(ts(halved, halved, 0.5, ALU.mult))
            normalize(xn, x)
            raise_("x_normed")

            def ada_row(n):
                bank = ps.read(dve, f"ada{n}", "dve")
                ps.release(f"ada{n}", V.tensor_copy(mrow[n % 2], bank[0:1, :]), dve)

            def ada_place(n):
                bank = ps.read(dve, f"adaT{n}", "dve")
                part, half = n // 2, n % 2
                if part in (2, 5):
                    rows = (g1b if part == 2 else g2b)[:, half * 512:half * 512 + 512]
                    if n == 4:
                        dve.wait_ge(ev("gate_rows_loaded"), 32)
                    ins = tt(rows, bank[:, :], rows, ALU.add)
                else:
                    ins = stt(modc[:, 4 * n:4 * n + 4], bank[:, 0:4], 1.0 if part in (1, 4) else 0.0,
                              prm[:, BADA + 4 * n:BADA + 4 * n + 4], ALU.add, ALU.add)
                ps.release(f"adaT{n}", ins, dve)

            def ada(lot):
                for n in lot:
                    ada_row(n)
                    if n > lot[0]:
                        ada_place(n - 1)
                ada_place(lot[-1])
            ada(ADA1)
            to_channels(ps, "h1", hT, modc[:, 8:16], modc[:, 0:8])
            for n in range(4):
                blocks = range(4 * n, min(4 * n + 4, NXB))
                for k in blocks:
                    if k % 2 == 0:
                        ps.wait_drained(dve, f"xb{k // 2}")
                    dst = cv[:, k - 4 * n, :]
                    w = [prm[:, ROWS["conv_w"] + j * NXB + k:ROWS["conv_w"] + j * NXB + k + 1] for j in range(CONV)]
                    bias = prm[:, ROWS["conv_b"] + k:ROWS["conv_b"] + k + 1]
                    do(ts(dst, raw[:, k, 3:3 + T], w[3], ALU.mult, bias, ALU.add))
                    for j in range(3):
                        do(stt(dst, raw[:, k, j:j + T], w[j], dst, ALU.mult, ALU.add))
                raise_("conv_batch")
                dve.wait_ge(ev("conv_tanh"), n + 1)
                m = len(blocks)
                times_sigmoid(xb[:, 4 * n:4 * n + m, :], ce[:, 0:m, :], cv[:, 0:m, :])
                raise_("conv_gated")
            bank = ps.read(dve, "dt", "dve")
            dve.wait_ge(ev("head_rows_loaded"), 48)
            ps.release("dt", tt(dtr, v3(bank[:, 0:TT * HEADS], TT), over(dt_b, TT, 1), ALU.add), dve)
            do(stt(flat(dta), flat(dtr), -1.0, flat(dtr), ALU.mult, ALU.max))
            raise_("dt_abs")
            dve.wait_ge(ev("dt_log"), 1)
            do(ts(dtv, dtr, 0.0, ALU.max))
            do(tt(dtv, dtv, dta, ALU.add))
            do(ts(nega, nega, -1.0, ALU.mult))
            do(tt(dta, dtv, over(nega, TT, 1), ALU.mult))
            raise_("decay_steps")
            for t in range(TT):
                raise_("ce_free")
                dve.wait_ge(ev("z_tanh"), t + 1)
                times_sigmoid(z[:, t, :], ce_f[:, 0:SSD_W], z[:, t, :])
            ps.wait_drained(dve, "u")
            dve.wait_ge(ev("pool_table_loaded"), 16)

            def widen(dst, src, by, blocks):
                do(tt(dst[:, blocks, PAD:PAD + T], src[:, blocks, PAD:PAD + T], src[:, blocks, PAD - by:PAD - by + T],
                      ALU.add))

            def group_mean(g, src):
                p0, b = 64 * (g % 2), g // 2
                do(tt(diff[p0:p0 + 64, b, :], src[p0:p0 + 64, b, PAD:PAD + T], prc[p0:p0 + 64, b, :], ALU.mult))
            both, last_ = slice(0, 2), slice(1, 2)
            widen(sA, uT, 1, both)
            group_mean(0, sA)
            widen(sB, sA, 2, both)
            group_mean(1, sB)
            widen(sA, sB, 4, last_)
            group_mean(2, sA)
            widen(sB, sA, 8, last_)
            group_mean(3, sB)
            do(tt(diff, diff, uT[:, :, PAD:PAD + T], ALU.subtract))
            raise_("pooled")
            ada(ADA2)
            bank = ps.read(dve, "acs", "dve")
            ps.release("acs", V.tensor_copy(flat(acs), bank[:, 0:3 * HEADS]), dve)
            do(tt(dte, acs[:, 2, :], acs[:, 0, :], ALU.subtract))
            raise_("decay_sums")
            ps.wait_drained(dve, "xs1_4")
            dve.wait_ge(ev("decay_exps"), 1)

            def heads(v, n=HD):
                return v.rearrange("p (h c) -> p h c", c=n)
            for t in range(TT):
                do(tt(heads(xdt[:, t, :]), heads(xtok[:, t, 0:SSD_W]), over(dtv[:, t, :], HD, 2), ALU.mult))
            raise_("xdt_ready")
            do(tt(heads(xcd), heads(xdt[:, 0, :]), over(dte, HD, 2), ALU.mult))
            raise_("xcd_ready")
            for t in range(TT):
                do(tt(heads(yv[:, t, :]), heads(xtok[:, t, 0:SSD_W]), over(dskip_b, HD, 2), ALU.mult))
            GW = RPG * HD

            def decays(t, g):
                bank = ps.read(dve, f"row{t}{g}", "dve")
                cols = acs[:, t, RPG * g:RPG * g + RPG]
                ps.release(f"row{t}{g}", tt(seg, v3(bank[:, 0:RPG * P], RPG), over(cols, P, 2), ALU.subtract), dve)
                do(tt(seg, seg, over(C["seg_mask"], RPG, 1), ALU.add))
                raise_("segment_sums")
                dve.wait_ge(ev("segment_exps"), t * GROUPS + g + 1)
                bank = ps.read(dve, f"cb{t}{g}", "dve")
                ps.release(f"cb{t}{g}", tt(seg2, seg, over(bank[:, 0:P], RPG, 1), ALU.mult), dve)

            def diagonal(t, g):
                bank = ps.read(dve, f"yd{t}{g}", "dve")
                dst = yv[:, t, g * GW:g * GW + GW]
                ps.release(f"yd{t}{g}", tt(dst, bank[:, 0:GW], dst, ALU.add), dve)
            for g in range(GROUPS):
                decays(0, g)
                diagonal(0, g)
            for g in range(GROUPS):
                bank = ps.read(dve, f"state{g}", "dve")
                ps.release(f"state{g}", V.tensor_copy(prevT[:, g, :], bank[:, 0:GW]), dve)
            for g in range(GROUPS):
                decays(1, g)
                diagonal(1, g)
                bank = ps.read(dve, f"yo{g}", "dve")
                ps.release(f"yo{g}", tt(heads(ybuf), heads(bank[:, 0:GW]),
                                        over(eacs[:, RPG * g:RPG * g + RPG], HD, 2), ALU.mult), dve)
                dst = yv[:, 1, g * GW:g * GW + GW]
                do(tt(dst, dst, ybuf, ALU.add))
            sq = v3(cv_f[:, 0:SSD_W], GROUPS)
            for t in range(TT):
                do(tt(yv[:, t, :], yv[:, t, :], z[:, t, :], ALU.mult))
                do(tt(cv_f[:, 0:SSD_W], yv[:, t, :], yv[:, t, :], ALU.mult))
                do(V.tensor_reduce(gss[:, t * GROUPS:(t + 1) * GROUPS], sq, AX.X, ALU.add))
            rsqrt(rs[:, 0:TT * GROUPS], TT * GROUPS, gss, GW)
            for t in range(TT):
                yh = heads(yv[:, t, :], GW)
                do(tt(yh, yh, over(rs[:, t * GROUPS:(t + 1) * GROUPS], GW, 2), ALU.mult))
            raise_("ssd_normed")

            def add_gated(ps, names, gate_rows, buf):
                for n in range(2):
                    for t in range(TT):
                        bank = ps.read(dve, f"{names}{n}t{t}", "dve")
                        cols = slice(n * 512, n * 512 + 512)
                        ps.release(f"{names}{n}t{t}", tt(buf[:, 0:512], bank[:, :], gate_rows[:, cols], ALU.mult), dve)
                        do(tt(x[:, t, cols], x[:, t, cols], buf[:, 0:512], ALU.add))
            add_gated(ps, "mix", g1b, cv_f)
            raise_("x_updated")
            normalize(mem_x, mem_x)
            raise_("mem_normed")
            to_channels(ps, "memT", memT, prm[:, ROWS["g_mem"]:ROWS["g_mem"] + 8], None)

            def head_norm(src, n, width, gain, sq_, t=None):
                do(tt(sq_, src, src, ALU.mult))
                do(V.tensor_reduce(hss[:, 0:n], sq_, AX.X, ALU.add))
                rsqrt(rs[:, 0:n], n, hss[:, 0:n], width)
                do(tt(src, src, over(rs[:, 0:n], width, 2), ALU.mult))
                if gain is not None:
                    do(tt(src, src, over(gain, n, 1), ALU.mult))
            dve.wait_ge(ev("norm_rows_loaded"), 96)
            G_QN, G_KN = rows2[:, 0:128], rows2[:, 128:256]
            G_QR, G_KR, G_QM, G_KM = (rows2[:, 256 + 64 * n:320 + 64 * n] for n in range(4))
            for t in range(TT):
                bank = ps.read(dve, f"mkt{t}", "dve")
                ps.release(f"mkt{t}", V.tensor_copy(mk[:, t, :], bank[:, 0:256]), dve)
            for t in range(TT):
                head_norm(heads(mk[:, t, :], EQ), EH, EQ, G_KM, heads(msq[:, t, :], EQ))
            raise_("mem_keys_normed")
            normalize(xn, x)
            raise_("x_normed")
            to_channels(ps, "h2", hT, modc[:, 32:40], modc[:, 24:32])
            dve.wait_ge(ev("router_loaded"), 32)
            dve.wait_ge(ev("router_rows_loaded"), 32)
            for t in range(TT):
                bank = ps.read(dve, f"routert{t}", "dve")
                ps.release(f"routert{t}", tt(lg[:, t, :], bank[:, 0:EG + NE], rb, ALU.add), dve)

            def first_max(one_hot, values, top, rev, tmp):
                n = values.shape[2]
                do(V.tensor_reduce(top, values, AX.X, ALU.max))
                do(tt(tmp, values, over(top, n, 2), ALU.is_equal))
                do(tt(tmp, tmp, over(rev, TT, 1), ALU.mult))
                do(V.tensor_reduce(gsm, tmp, AX.X, ALU.max))
                do(tt(one_hot, over(gsm, n, 2), over(rev, TT, 1), ALU.is_equal))
            glog = lg[:, :, 0:EG]
            first_max(ohg, glog, gm, C["rev4"], gtm)
            do(tt(gtm, glog, over(gm, EG, 2), ALU.subtract))
            raise_("group_shifted")
            dve.wait_ge(ev("group_exps"), 1)
            do(V.tensor_reduce(gsm, gtm, AX.X, ALU.add))
            do(V.reciprocal(pg, gsm))
            w4 = wide.rearrange("p (t g e) -> p t g e", t=TT, g=EG)
            for t in range(TT):
                do(tt(w4[:, t], lg[:, t, EG:].rearrange("p (g e) -> p g e", g=EG), over(ohg[:, t, :], EPG, 2), ALU.mult))
                do(V.tensor_reduce(w8[:, t, :], w4[:, t].rearrange("p g e -> p e g"), AX.X, ALU.add))
            first_max(oh1, w8, v1, C["rev8"], t8)
            do(stt(w8, oh1, BIG, w8, ALU.mult, ALU.add))
            first_max(oh2, w8, v2, C["rev8"], t8)
            do(tt(v2, v2, v1, ALU.subtract))
            raise_("top_gap")
            dve.wait_ge(ev("top_exp"), 1)
            do(ts(v1, e2, 1.0, ALU.add))
            do(V.reciprocal(v1, v1))
            do(tt(gate1, pg, v1, ALU.mult))
            do(tt(gate2, gate1, e2, ALU.mult))
            for s_, oh in ((sel1, oh1), (sel2, oh2)):
                for t in range(TT):
                    do(tt(s_[:, t, :].rearrange("p (g e) -> p g e", g=EG), over(ohg[:, t, :], EPG, 2),
                          over(oh[:, t, :], EG, 1), ALU.mult))
            do(tt(sel, sel1, sel2, ALU.add))
            do(V.memset(cumA, 0.0))
            do(V.memset(cumB, 0.0))
            raise_("chosen")
            bank = ps.read(dve, "rank", "dve")
            do(V.tensor_copy(flat(slot_of), bank[:, 0:2 * NE]))
            ps.release("rank", V.tensor_copy(cnt, bank[:, 2 * NE:3 * NE]), dve)
            do(ts(nblk, cnt, 0.0, ALU.is_gt))
            for m in range(1, T // SLOTS):
                do(stt(nblk, cnt, float(m * SLOTS), nblk, ALU.is_gt, ALU.add))
            do(V.tensor_copy(cumA[:, NE:], nblk))
            cum = [cumA, cumB]
            for m in range(5):
                s_, d_ = cum[m % 2], cum[(m + 1) % 2]
                do(tt(d_[:, NE:], s_[:, NE:], s_[:, NE - 2 ** m:2 * NE - 2 ** m], ALU.add))
            ends = cumB[:, NE:]
            do(ts(wide[:, 0:NE], ends, C["row_id"], ALU.is_le))
            do(V.tensor_reduce(be, wide[:, 0:NE], AX.X, ALU.add))
            do(ts(be, be, float(NE - 1), ALU.min))
            raise_("block_experts")
            do(tt(cnt, ends, nblk, ALU.subtract))
            do(ts(cnt, cnt, float(SLOTS), ALU.mult))
            do(tt(slot_of, slot_of, over(cnt, TT, 1), ALU.add))
            for s_, dst in ((sel1, dest[0]), (sel2, dest[1])):
                do(tt(v3(wide, TT), s_, slot_of, ALU.mult))
                do(V.tensor_reduce(dst, v3(wide, TT), AX.X, ALU.add))
            do(ts(npf, ends[:, NE - 1:NE], 0.5, ALU.mult, 0.25, ALU.add))
            do(V.tensor_copy(meta[0:1, P:P + 1], npf[0:1, :]))
            do(ts(npf, npf, -1.0, ALU.add))
            do(V.tensor_copy(meta[0:1, P + 1:P + 2], npf[0:1, :]))
            do(V.tensor_copy(slot_id, C["iota"]))
            bank = ps.read(dve, "experts", "dve")
            ps.release("experts", V.tensor_copy(meta[0:1, 0:P], bank[0:1, 0:P]), dve)
            raise_("routed")

            pairs = dve.value_load(meta[0:1, P:P + 1], min_val=4, max_val=MAXB // 2)
            last_pair = dve.value_load(meta[0:1, P + 1:P + 2], min_val=3, max_val=MAXB // 2 - 1)
            gA, gB, hA, hB, tA, tB, oA, oB = banks

            def choose_slots(i, lc):
                if i is not None:
                    dve.wait_ge(ev("gather_filled"), i * 2)
                for t in range(TT):
                    lc(ts(pick[:, t, :], slot_id, dest[0][:, t:t + 1], ALU.is_equal))
                    ins = stt(pick[:, t, :], slot_id, dest[1][:, t:t + 1], pick[:, t, :], ALU.is_equal, ALU.add)
                    lc(ins)
                lc(ts(slot_id, slot_id, float(P), ALU.add))
                dve.sem_inc(ev("slots_picked"), 1)

            def slots_in(i, lc):
                dve.wait_ge(ev("gather_filled"), i * 2 + 2)
                for k in range(4, 8):
                    ins = ts(xeT[:, k, :], gB[:, (k - 4) * P:(k - 4) * P + P], modc[:, 32 + k:33 + k], ALU.mult,
                             modc[:, 24 + k:25 + k], ALU.add)
                    if k < 7:
                        lc(ins)
                ins.then_inc(ev("slots_in_by_dve"), 1)

            def hidden_out(i, b):
                dve.wait_ge(ev("hidden_filled"), i * 4 + (2 * b + 2))
                V.tensor_copy(hs[:, 512:1024], hB[:, :]).then_inc(ev("hidden_out_by_dve"), 1)

            def gate(i, b, lc):
                dve.wait_ge(ev("gate_tanhs"), i * 2 + (b + 1))
                lc(stt(gt, ge, 1.0, v3(tA[:, :], 4)[:, :, 0:SLOTS], ALU.add, ALU.mult))
                dve.wait_ge(ev("folded"), i * 4 + (2 * b + 2))
                stt(sT[b], gt, 0.5, v3(tB[:, :], 4)[:, :, 0:SLOTS], ALU.mult, ALU.mult).then_inc(ev("hidden_gated"), 1)

            def rows_out(m):
                dve.wait_ge(ev("rows_filled_for_dve"), m + 1)
                dve.wait_ge(ev("parts_filled"), m * 4)
                V.tensor_copy(osb[:, 512:1024], oB[:, :]).then_inc(ev("rows_out_by_dve"), 1)

            def shares(lc):
                lc(stt(share_f, slot_rows, slot_col, gate_rows, ALU.is_equal, ALU.mult))
                lc(ts(slot_col, slot_col, float(P), ALU.add))
                tt(share_f[:, 0:T], share_f[:, 0:T], share_f[:, T:2 * T], ALU.add).then_inc(ev("shares_ready"), 1)

            def add_parts(m, t):
                if t == 0:
                    dve.wait_ge(ev("parts_added"), m * 4)
                for n_, src in enumerate((oA, oB)):
                    dve.wait_ge(ev("parts_filled"), m * 4 + (2 * t + n_ + 1))
                    dst = acc[:, t, n_ * 512:n_ * 512 + 512]
                    tt(dst, src[:, :], dst, ALU.add).then_inc(ev("parts_added"), 1)

            def turn(i, lc, first):
                hidden_out(i, 0)
                if not first:
                    rows_out(i - 1)
                    shares(lc)
                choose_slots(i + 1, lc)
                gate(i, 0, lc)
                hidden_out(i, 1)
                if not first:
                    add_parts(i - 1, 0)
                slots_in(i + 1, lc)
                gate(i, 1, lc)
                if not first:
                    add_parts(i - 1, 1)
            lead = Chained(dve, ev("dve_lead_step"))
            choose_slots(None, lead)
            for n, col in enumerate([c_[:, t:t + 1] for c_ in (dest[0], dest[1], gate1, gate2) for t in range(TT)]):
                do(ts(diag[:, n, :], ident, col, ALU.mult), spread)
            do(V.tensor_copy(slot_col, C["row_id"]))
            bank = ps.read(dve, "slot_rows", "dve")
            ps.release("slot_rows", V.tensor_copy(slot_rows, bank[:, :]), dve)
            ps.wait_drained(dve, "gate_rows")
            do(V.memset(acc_f, 0.0))
            slots_in(0, lead)
            turn(0, lead, True)
            with dve.Fori(1, pairs) as i:
                lc = LoopChained(dve, ev("dve_expert_step"), i, 5 + 2 + 1 + 3 + 1)
                turn(i, lc, False)
                lc.end()
            rows_out(last_pair)
            shares(lead)
            add_parts(last_pair, 0)
            add_parts(last_pair, 1)

            dve.wait_ge(ev("parts_added"), pairs * 4)
            for t in range(TT):
                do(tt(acc[:, t, :], acc[:, t, :], g2b[:, :], ALU.mult))
                do(tt(x[:, t, :], x[:, t, :], acc[:, t, :], ALU.add))
            raise_("x_updated")
            dve.wait_ge(ev("final_rows_loaded"), 16)
            norm_no[0] += 1
            dve.wait_ge(ev("squares"), norm_no[0])
            rsqrt(rs[:, 0:TT], TT, ss, D)
            for t in range(TT):
                do(stt(x[:, t, :], x[:, t, :], rs[:, t:t + 1], fnw[:, :], ALU.mult, ALU.mult))
            raise_("x_updated")

            normalize(xn, x)
            raise_("x_normed")
            to_channels(ps2, "h3", hT, prm[:, ROWS["g_mix"]:ROWS["g_mix"] + 8], None)
            dve.wait_ge(ev("positions_loaded"), 16)
            do(V.tensor_copy(pos_f, pos_i))
            do(tt(ang, over(C["inv"], TT, 1), over(pos_f, NI, 2), ALU.mult))
            ROUND = float(1.5 * 2 ** 23)
            do(ts(rn, ang, float(1.0 / (2 * np.pi)), ALU.mult, ROUND, ALU.add))
            do(ts(rn, rn, -ROUND, ALU.add))
            c1 = 6.28125
            c2 = float(np.float32(np.floor((2 * np.pi - c1) * 2 ** 22) / 2 ** 22))
            c3 = float(2 * np.pi - c1 - c2)
            for c_ in (c1, c2, c3):
                do(stt(ang, rn, -c_, ang, ALU.mult, ALU.add))
            PI_ = 3.1415925
            do(ts(rn, ang, float(np.pi / 2), ALU.add))
            do(ts(sinv, rn, float(np.pi), ALU.is_gt))
            do(stt(rn, sinv, -float(2 * np.pi), rn, ALU.mult, ALU.add))
            do(ts(rn, rn, -PI_, ALU.max, PI_, ALU.min))
            do(ts(ang, ang, -PI_, ALU.max, PI_, ALU.min))
            raise_("angles_ready")
            dve.wait_ge(ev("rope_tables"), 1)

            for t in range(TT):
                bank = ps2.read(dve, f"mqt{t}", "dve")
                ps2.release(f"mqt{t}", V.tensor_copy(qm[:, t, :], bank[:, 0:256]), dve)
            for t in range(TT):
                head_norm(heads(qm[:, t, :], EQ), EH, EQ, G_QM, heads(qsq[:, t, :], EQ))
            raise_("mem_q_normed")

            def attention(n_heads, first, scale, causal, width):
                for h in range(n_heads + 1):
                    if h < n_heads:
                        n = first + h
                        bank = ps2.read(dve, f"s_{n}", "dve")
                        b_ = v3(bank[:, :], TT)
                        s_ = pr[n % 2]
                        if n >= 2:
                            ps2.wait_filled(dve, f"pT_{n - 2}")
                        if causal:
                            do(tt(s_[:, 0, 0:P], b_[:, 0, 0:P], C["causal"], ALU.add))
                            do(V.tensor_copy(s_[:, 1, 0:P], b_[:, 1, 0:P]))
                            do(V.memset(s_[:, 0, P:T], BIG))
                            ps2.release(f"s_{n}", tt(s_[:, 1, P:T], b_[:, 1, P:T], C["causal"], ALU.add), dve)
                        else:
                            ps2.release(f"s_{n}", V.tensor_copy(s_, b_), dve)
                        do(V.tensor_reduce(mxs[n % 2], s_, AX.X, ALU.max))
                        do(ts(mxs[n % 2], mxs[n % 2], -scale, ALU.mult))
                        raise_("scores_maxed")
                    if h:
                        n = first + h - 1
                        bank = ps2.read(dve, f"o_{n}", "dve")
                        do(V.reciprocal(rs[:, 0:TT], sums[n % 2]))
                        dst = obr[:, :, (h - 1) * width:h * width]
                        ps2.release(f"o_{n}", tt(dst, v3(bank[:, 0:TT * width], TT), over(rs[:, 0:TT], width, 2),
                                                 ALU.mult), dve)
            attention(EH, 0, EQ ** -0.5, False, EV)

            gate_no = [0]

            def gates(br, rows, first=False):
                dve.wait_ge(ev(f"gate_bias_loaded_{br}"), 16)
                for n in range(2):
                    for t in range(TT):
                        cols = slice(n * 512, n * 512 + 512)
                        bank = ps2.read(dve, f"gate{br}{n}t{t}", "dve")
                        ps2.release(f"gate{br}{n}t{t}", tt(gtmp, bank[:, :], rows[:, cols], ALU.add), dve)
                        raise_("gate_logits")
                        gate_no[0] += 1
                        dve.wait_ge(ev("gate_tanh_done"), gate_no[0])
                        if first:
                            times_sigmoid(ysum[:, t, cols], gtmp, obr[:, t, cols])
                        else:
                            times_sigmoid(gtmp, gtmp, obr[:, t, cols])
                            do(tt(ysum[:, t, cols], ysum[:, t, cols], gtmp, ALU.add))
            gates(2, g1b, True)
            dve.wait_ge(ev("gla_rows_loaded"), 48)
            for t in range(TT):
                bank = ps2.read(dve, f"lg{t}", "dve")
                ps2.release(f"lg{t}", tt(la[:, t, :], bank[:, :], bgla, ALU.add), dve)
            do(stt(flat(lt), flat(la), -1.0, flat(la), ALU.mult, ALU.max))
            raise_("log_arg")
            do(ts(flat(la), flat(la), 0.0, ALU.min))
            dve.wait_ge(ev("log_done"), 1)
            do(tt(flat(la), flat(la), flat(lt), ALU.subtract))
            do(ts(flat(la), flat(la), 1.0 / 16.0, ALU.mult))
            raise_("log_decays")
            for t in range(TT):
                bank = ps2.read(dve, f"lvl0{t}", "dve")
                ps2.release(f"lvl0{t}", tt(att[t], v3(bank[:, :], GH), over(ident, GH, 1), ALU.mult), dve)
            ps2.wait_drained(dve, "cum1")
            for lvl in range(1, LEVELS + 1):
                half = 2 ** (lvl - 1)

                def sides(v, side, half=half):
                    w = v.rearrange("p h (b s c) -> p (h b) s c", s=2, c=half)
                    return w[:, :, side, :]
                mid = gbT.rearrange("p h (b s c) -> p (h b) s c", s=2, c=half)[:, :, 0, half - 1:half]
                mid = mid.to_broadcast(list(sides(gbT, 0).shape))
                do(tt(sides(lev, 0), mid, sides(gbT, 0), ALU.subtract))
                do(tt(sides(lev, 1), sides(gbT, 1), mid, ALU.subtract))
                raise_("level_differences")
                dve.wait_ge(ev("level_exps"), lvl)
                if lvl > 1:
                    ps2.wait_filled(dve, f"lvl{lvl - 1}1")
                do(tt(sides(qk, 0), sides(lev, 0), sides(gkT, 0), ALU.mult))
                do(tt(sides(qk, 1), sides(lev, 1), sides(gqT, 1), ALU.mult))
                raise_("level_ready")
                mask = C["level"][:, (lvl - 1) * P:lvl * P]
                for t in range(TT):
                    bank = ps2.read(dve, f"lvl{lvl}{t}", "dve")
                    ps2.release(f"lvl{lvl}{t}", tt(lev.rearrange("p a b -> p (a b)")[:, 0:GH * P].rearrange("p (a b) -> p a b", a=GH),
                                                   v3(bank[:, :], GH), over(mask, GH, 1), ALU.mult), dve)
                    do(tt(att[t], att[t], v3(flat(lev)[:, 0:GH * P], GH), ALU.add))
            mid = gbT[:, :, P - 1:P].to_broadcast([P, GH, P])
            do(tt(lev[:, :, 0:P], mid, gbT[:, :, 0:P], ALU.subtract))
            do(V.tensor_copy(lev[:, :, P:T], gbT[:, :, P:T]))
            raise_("level_differences")
            dve.wait_ge(ev("level_exps"), LEVELS + 1)
            ps2.wait_filled(dve, f"lvl{LEVELS}1")
            do(tt(qk[:, :, 0:P], lev[:, :, 0:P], gkT[:, :, 0:P], ALU.mult))
            do(tt(qk[:, :, P:T], lev[:, :, P:T], gqT[:, :, P:T], ALU.mult))
            raise_("level_ready")
            for h in range(GH):
                bank = ps2.read(dve, f"go{h}", "dve")
                ps2.release(f"go{h}", V.tensor_copy(obr[:, :, h * DV:h * DV + DV], v3(bank[:, :], TT)), dve)
            raise_("gla_normed")
            sqv = v3(flat(qk)[:, 0:GH * DV], GH)
            for t in range(TT):
                head_norm(heads(obr[:, t, :], DV), GH, DV, ggla, sqv)
            dve.wait_ge(ev("r_tanh"), 1)
            for t, e_ in enumerate((flat(la), flat(lt))):
                times_sigmoid(gr[:, t, :], e_, gr[:, t, :])
                do(tt(obr[:, t, :], obr[:, t, :], gr[:, t, :], ALU.mult))
            gates(1, g2b)
            raise_("gla_done")
            for t in range(TT):
                bank = ps2.read(dve, f"ckvt{t}", "dve")
                ps2.release(f"ckvt{t}", V.tensor_copy(ckv[:, t, :], bank[:, 0:KVR + ROPE]), dve)
            for t in range(TT):
                head_norm(ckv[:, t:t + 1, 0:KVR], 1, KVR, None, nsq[:, 0:KVR].unsqueeze(1))
            raise_("ckv_normed")

            def rotate(dst, src, t, n):
                c_, s_ = over(cosv[:, t, :], n, 1), over(sinv[:, t, :], n, 1)
                tmp = nsq[:, 0:n * NI].rearrange("p (n c) -> p n c", n=n)
                a_, b_ = src[:, :, 0:NI], src[:, :, NI:ROPE]
                do(tt(dst[:, :, 0:NI], a_, c_, ALU.mult))
                do(tt(tmp, b_, s_, ALU.mult))
                do(tt(dst[:, :, 0:NI], dst[:, :, 0:NI], tmp, ALU.subtract))
                do(tt(dst[:, :, NI:ROPE], a_, s_, ALU.mult))
                do(tt(tmp, b_, c_, ALU.mult))
                do(tt(dst[:, :, NI:ROPE], dst[:, :, NI:ROPE], tmp, ALU.add))
            for t in range(TT):
                head_norm(ckv[:, t:t + 1, KVR:KVR + ROPE], 1, ROPE, G_KR, nsq[:, 0:ROPE].unsqueeze(1))
                rotate(kr2[:, t:t + 1, 0:ROPE], ckv[:, t:t + 1, KVR:KVR + ROPE], t, 1)
                do(V.tensor_copy(kr2[:, t, ROPE:2 * ROPE], kr2[:, t, 0:ROPE]))
            raise_("rope_k_ready")
            ps2.wait_drained(dve, "q2t1")
            for t in range(TT):
                qh = q[:, t, :].rearrange("p (h c) -> p h c", h=MH)
                head_norm(qh[:, :, 0:NOPE], MH, NOPE, G_QN, nsq.rearrange("p (h c) -> p h c", h=MH))
                head_norm(qh[:, :, NOPE:], MH, ROPE, G_QR, nsq[:, 0:MH * ROPE].rearrange("p (h c) -> p h c", h=MH))
                rotate(heads(ropeb[:, t, :], ROPE), qh[:, :, NOPE:], t, MH)
            raise_("mla_q_ready")
            ps2.wait_drained(dve, "kv3t1")
            for t in range(TT):
                kh = kv[:, t, :].rearrange("p (h c) -> p h c", h=MH)
                head_norm(kh[:, :, 0:NOPE], MH, NOPE, G_KN, nsq.rearrange("p (h c) -> p h c", h=MH))
            raise_("mla_k_ready")
            attention(MH, EH, (NOPE + ROPE) ** -0.5, True, VD)
            gates(0, fnw)
            raise_("branches_summed")
            to_channels(ps2, "ysT", hT, 0.5, None)
            for n in range(2):
                for t in range(TT):
                    bank = ps2.read(dve, f"wo{n}t{t}", "dve")
                    dst = x[:, t, n * 512:n * 512 + 512]
                    ps2.release(f"wo{n}t{t}", tt(dst, bank[:, :], dst, ALU.add), dve)
            raise_("x_updated")
            normalize(xn, x)
            raise_("x_normed")
            to_channels(ps2, "h4", hT, prm[:, ROWS["g_ffn"]:ROWS["g_ffn"] + 8], None)
            for m in range(16):
                ps2.wait_drained(dve, f"up{m // 2}{m % 2}")
                v_ = flat(aT)[:, m * 512:m * 512 + 512]
                do(tt(v_, v_, v_, ALU.mult))
                raise_("ffn_squared")
            for t in range(TT):
                for n in range(2):
                    bank = ps2.read(dve, f"down{t}{n}", "dve")
                    dst = x[:, t, n * 512:n * 512 + 512]
                    ps2.release(f"down{t}{n}", tt(dst, bank[:, :], dst, ALU.add), dve)
                    raise_("output_ready")
        @block.gpsimd
        def _(pool):
            def rows_of(dst, src, name):
                pool.dma_start(dst, src.partition_broadcast(P)).then_inc(ev(name), 16)
            pool.memset(raw[:, :, 0:3], 0.0).then_inc(ev("pool_step"), 1)
            for v in (uT, sA, sB):
                pool.memset(v[:, :, 0:PAD], 0.0).then_inc(ev("pool_step"), 1)
            pool.memset(wpool, 0.0).then_inc(ev("pool_step"), 1)
            pool.wait_ge(ev("pool_step"), 5)
            pool.sem_inc(ev("pads_zeroed"), 1)
            rows_of(dt_b, a["dt_bias"][0], "head_rows_loaded")
            rows_of(alog_b, a["a_log"][0], "head_rows_loaded")
            rows_of(dskip_b, a["d_skip"][0], "head_rows_loaded")
            rows_of(g1b[:, :], a["b_ada"][0][2 * D:3 * D], "gate_rows_loaded")
            rows_of(g2b[:, :], a["b_ada"][0][5 * D:6 * D], "gate_rows_loaded")
            for g in range(4):
                lo = 64 * (g % 2)
                pool.dma_start(wpool[lo:lo + 64, g // 2, lo:lo + 64], a["w_pool"][0][g]).then_inc(ev("pool_weights_loaded"), 16)
            pool.dma_start(flat(prc), a["pool_table"]).then_inc(ev("pool_table_loaded"), 16)
            for n, (nm, w) in enumerate((("g_q_nope_2", 128), ("g_k_nope_2", 128), ("g_q_rope_2", 64),
                                         ("g_k_rope_2", 64), ("g_q_mem_2", 64), ("g_k_mem_2", 64))):
                lo = (0, 128, 256, 320, 384, 448)[n]
                rows_of(rows2[:, lo:lo + w], a[nm][0], "norm_rows_loaded")
            rows_of(rb[:, 0:EG], a["b_group"][0], "router_rows_loaded")
            rows_of(rb[:, EG:], a["b_router"][0], "router_rows_loaded")
            rows_of(fnw[:, :], a["final_norm_w"], "final_rows_loaded")
            pool.dma_start(pos_i, a["positions_2"][0].rearrange("(t p) -> p t", p=P),
                           allow_slow_non_contiguous=True).then_inc(ev("positions_loaded"), 16)
            pool.wait_ge(ev("ssd_normed"), 1)
            pool.dma_start(mem_x, a["mem_2"][0].rearrange("(t p) d -> p t d", p=P)).then_inc(ev("memory_loaded"), 16)
            pool.wait_ge(ev("mem_keys_normed"), 1)
            ps.wait_filled(pool, "mkT")
            pool.dma_start(wr[:, :, 0:EG], a["w_group"][0].rearrange("(k p) n -> p k n", p=P)).then_inc(ev("router_loaded"), 16)
            pool.dma_start(wr[:, :, EG:], a["w_router"][0].rearrange("(k p) n -> p k n", p=P)).then_inc(ev("router_loaded"), 16)
            pool.wait_ge(ev("x_updated"), 1)
            rows_of(g1b[:, :], a["b_gate_2"][0][2 * D:3 * D], "gate_bias_loaded_2")
            pool.wait_ge(ev("x_updated"), 2)
            rows_of(g2b[:, :], a["b_gate_2"][0][D:2 * D], "gate_bias_loaded_1")
            pool.wait_ge(ev("x_updated"), 3)
            rows_of(fnw[:, :], a["b_gate_2"][0][0:D], "gate_bias_loaded_0")
            pool.dma_start(wgate[0:GRANK, :], a["w_gla_gate_2"][0]).then_inc(ev("gla_rows_loaded"), 16)
            rows_of(bgla, a["b_gla_gate_2"][0], "gla_rows_loaded")
            rows_of(ggla, a["g_gla_out_2"][0], "gla_rows_loaded")
        @block.sync
        def _(sp):
            sp.dma_start(cst[:, :], a["const"]).then_inc(ev("constants_loaded"), 16)

            def load_rows(name, src, rows):
                sp.dma_start(prm_rows[ROWS[name]:ROWS[name] + rows, 0:P], src).then_inc(ev("param_rows_loaded"), 16)
            load_rows("c", a["c"][0].rearrange("(k p) -> k p", p=P), 8)
            load_rows("conv_w", a["conv_w"][0].rearrange("t (k p) -> (t k) p", p=P), CONV * NXB)
            load_rows("conv_b", a["conv_b"][0].rearrange("(k p) -> k p", p=P), NXB)
            load_rows("ssd_norm_w", a["ssd_norm_w"][0].rearrange("(k p) -> k p", p=P), 6)
            load_rows("pool_scale", a["pool_scale"][0].rearrange("(k p) -> k p", p=P), 2)
            load_rows("g_mix", a["g_mix_2"][0].rearrange("(k p) -> k p", p=P), 8)
            load_rows("g_mem", a["g_mem_2"][0].rearrange("(k p) -> k p", p=P), 8)
            load_rows("g_ffn", a["g_ffn_2"][0].rearrange("(k p) -> k p", p=P), 8)
            load_rows("g_ckv", a["g_ckv_2"][0].rearrange("(k p) -> k p", p=P), 2)
            sp.dma_start(prm_rows[0:48, P:2 * P],
                         a["b_ada"][0].rearrange("(k p) -> k p", p=P)).then_inc(ev("param_rows_loaded"), 16)
            sp.dma_start(x, a["x"][0].rearrange("(t p) d -> p t d", p=P)).then_inc(ev("x_loaded"), 16)
            for n in ADA1:
                ring.load(sp, cols_of(512), k_rows(w_ada, slice(n * 512, n * 512 + 512)))
            for c0, w in IN_SLOTS:
                ring.load(sp, cols_of(w), k_rows(w_in, slice(c0, c0 + w)))
            for n in ADA2:
                ring.load(sp, cols_of(512), k_rows(w_ada, slice(n * 512, n * 512 + 512)))
            for n in range(2):
                ring.load(sp, cols_of(512), k_rows(w_out, slice(n * 512, n * 512 + 512)))
            for c0, w in MEM_SLOTS:
                ring.load(sp, cols_of(w), k_rows(w_mkv, slice(c0, c0 + w)))
            sp.wait_ge(ev("routed"), 1)
            pairs = sp.value_load(meta[0:1, P:P + 1], min_val=4, max_val=MAXB // 2)
            last = sp.value_load(meta[0:1, P + 1:P + 2], min_val=3, max_val=MAXB // 2 - 1)

            def load_w13(b, e, wait):
                for part in range(2):
                    wait(3 * b + part)
                    src = w13[bass.ds(e, 1), part * 512:part * 512 + 512, :]
                    sp.dma_start(slots[3 * b + part].rearrange("p (k n) -> p k n", k=4),
                                 src.rearrange("e (k p) n -> (e p) k n", p=P)).then_inc(xw_landed[3 * b + part], 16)

            def load_w2(b, e, wait):
                wait(3 * b + 2)
                src = w2[bass.ds(e, 1), :, :]
                sp.dma_start(slots[3 * b + 2].rearrange("p (k n) -> p k n", k=4),
                             src.rearrange("e (k p) n -> (e p) k n", p=P)).then_inc(xw_landed[3 * b + 2], 16)

            def expert_of(block):
                return sp.value_load(meta[0:1, block:block + 1] if isinstance(block, int)
                                     else meta[0:1, bass.ds(block, 1)], min_val=0, max_val=NE - 1)
            last_of = {k % 6: name for k, name in enumerate(ring.free_at)}

            def ring_free(slot):
                ps.wait_filled(sp, last_of[slot])
            ea, eb = expert_of(0), expert_of(1)
            load_w13(0, ea, ring_free)
            load_w13(1, eb, ring_free)
            load_w2(0, ea, ring_free)
            load_w2(1, eb, ring_free)
            load_w13(0, expert_of(2), lambda s_: sp.wait_ge(ev("hidden_filled"), 2))
            load_w13(1, expert_of(3), lambda s_: sp.wait_ge(ev("hidden_filled"), 4))
            with sp.Fori(2, pairs) as i:
                olda, oldb, ea, eb = (expert_of(i * 2 + n) for n in (-2, -1, 0, 1))
                load_w13(0, ea, lambda s_: sp.wait_ge(ev("hidden_filled"), i * 4 - 2))
                load_w2(0, olda, lambda s_: sp.wait_ge(ev("rows_filled_for_dve"), i - 1))
                load_w2(1, oldb, lambda s_: sp.wait_ge(ev("rows_filled_for_dve"), i - 1))
                load_w13(1, eb, lambda s_: sp.wait_ge(ev("hidden_filled"), i * 4))
            for b in range(2):
                load_w2(b, expert_of(last * 2 + b), lambda s_: sp.wait_ge(ev("rows_filled_for_dve"), last))
            for n, (name, c0, w) in enumerate(LATE_A):
                need = None
                if n < 4:
                    need = [(ev("hidden_filled"), last * 4 + 2), (ev("hidden_filled"), last * 4 + 2),
                            (ev("rows_filled_for_dve"), pairs), (ev("hidden_filled"), pairs * 4)][n]
                ring2.load(sp, cols_of(w), k_rows(w_in2, slice(c0, c0 + w)), need)
            ring2.load(sp, cols_of(2048, 2), w_ukv.rearrange("(k p) n -> p k n", p=P))
            for name, c0, w in LATE_B:
                ring2.load(sp, cols_of(w), k_rows(w_in2, slice(c0, c0 + w)))
            for n in range(2):
                ring2.load(sp, cols_of(512), k_rows(w_o2, slice(n * 512, n * 512 + 512)))
            for n in range(8):
                ring2.load(sp, cols_of(512), k_rows(w_up, slice(n * 512, n * 512 + 512)))
            for n in range(8):
                ring2.load(sp, cols_of(D, 4), w_down[n * 512:n * 512 + 512, :].rearrange("(k p) n -> p k n", p=P))
            sp.wait_ge(ev("output_ready"), 4)
            sp.dma_start(out[0].rearrange("(t p) d -> p t d", p=P), x).then_inc(ev("output_written"), 16)
            sp.wait_ge(ev("output_written"), 16)


_INS = ["x", "c", "w_ada", "b_ada", "w_in", "w_pool", "pool_scale", "conv_w", "conv_b", "dt_bias", "a_log",
        "d_skip", "ssd_norm_w", "w_out", "w_group", "b_group", "w_router", "b_router", "w13", "w2",
        "final_norm_w", "mem_2", "positions_2", "g_mix_2", "w_in_2", "b_gate_2", "g_ckv_2", "w_ukv_2",
        "g_q_nope_2", "g_k_nope_2", "g_q_rope_2", "g_k_rope_2", "w_gla_gate_2", "b_gla_gate_2", "g_gla_out_2",
        "g_mem_2", "w_mem_kv_2", "g_q_mem_2", "g_k_mem_2", "w_o_2", "g_ffn_2", "w_up_2", "w_down_2"]


def program(nc, arrays):
    args = {}
    for name, v in arrays.items():
        args[name] = nc.dram_tensor(f"in_{name}_dram", v.shape, mybir.dt.from_np(v.dtype), kind="ExternalInput").ap()
    out = nc.dram_tensor("out_0_dram", (1, T, D), F32, kind="ExternalOutput").ap()
    build(nc, args, out)


def kernel(**inputs):
    import concourse.bacc as _bacc
    from concourse.bass_utils import run_bass_kernel_spmd as _run

    nc = _bacc.Bacc("TRN2", target_bir_lowering=False, num_devices=1)
    arrays = {name: np.ascontiguousarray(inputs[name]) for name in _INS}
    arrays["const"], arrays["pool_table"] = constants()
    program(nc, arrays)
    r = _run(nc, [{f"in_{k}_dram": v for k, v in arrays.items()}], core_ids=[0])
    return r.results[0]["out_0_dram"]
```

```python
from contextlib import ExitStack

import numpy as np

import concourse.bass as bass
from concourse import mybir

ALU = mybir.AluOpType
ACT = mybir.ActivationFunctionType
AX = mybir.AxisListType
F32 = mybir.dt.float32
F32R = mybir.dt.float32r
I32 = mybir.dt.int32
U32 = mybir.dt.uint32

P = 128
D = 1024
T = 256
TT = T // P
KD = D // P
EPS = 1e-6

POOL_W, SSD_W, HEADS, HD, GROUPS, STATE, CONV = 256, 768, 12, 64, 4, 128, 4
RPG = HEADS // GROUPS
XBC = SSD_W + 2 * GROUPS * STATE
NXB = XBC // P
IN1 = POOL_W + SSD_W + XBC + HEADS
EG, EPG, FF = 4, 8, 512
NE = EG * EPG
SLOTS = 64
MAXB = NE + 2 * T // SLOTS
MH, NOPE, ROPE, VD, KVR = 8, 128, 64, 128, 256
GH, DK, DV, GRANK = 4, 128, 256, 16
EH, EQ, EV = 4, 64, 256
DFF = 4 * D
O_Q, O_CKV, O_KR = 0, 1536, 1792
O_GQ, O_GK, O_GV, O_GA, O_GR = 1856, 2368, 2880, 3904, 3920
O_MQ, O_GATE = 4944, 5200
LEVELS = 7
BIG = -1e30

ROWS = {}
_r = 0
for _n, _c in (("c", 8), ("conv_w", CONV * NXB), ("conv_b", NXB), ("ssd_norm_w", 6), ("pool_scale", 2),
               ("g_mix", 8), ("g_mem", 8), ("g_ffn", 8), ("g_ckv", 2),
               ("g_q_nope", 1), ("g_k_nope", 1)):
    ROWS[_n] = _r
    _r += _c
NROWS = _r
BADA = NROWS
assert NROWS <= P

CONST_COLS = {}
_r = 0
for _n, _c in (("ident", P), ("tri", P), ("strict", P), ("ones", P), ("seg_mask", P), ("causal", 3 * P),
               ("fold", P), ("iota", P), ("level", LEVELS * P), ("inv", ROPE // 2), ("row_id", 1), ("quarters", 1),
               ("rev4", EG), ("rev8", EPG)):
    CONST_COLS[_n] = (_r, _c)
    _r += _c
NCONST = _r


def constants():
    c = np.zeros((P, NCONST), np.float32)
    p, f = np.arange(P)[:, None], np.arange(P)[None, :]

    def put(name, value):
        a, n = CONST_COLS[name]
        c[:, a:a + n] = value
    put("ident", p == f)
    put("tri", p <= f)
    put("strict", p < f)
    put("ones", 1.0)
    put("seg_mask", np.where(p <= f, 0.0, BIG))
    causal = np.where(f <= p, 0.0, BIG)
    put("causal", np.concatenate([causal, np.zeros((P, P)), causal], 1))
    put("fold", (f < SLOTS) & (p % SLOTS == f))
    put("iota", np.broadcast_to(f, (P, P)))
    x = p ^ f
    put("level", np.concatenate([(x >= 2 ** l) & (x < 2 ** (l + 1)) & (p < f) for l in range(LEVELS)], 1))
    put("inv", (1.0 / (np.float32(10000.0) ** (np.arange(0, ROPE, 2, dtype=np.float32) / np.float32(ROPE))))[None, :])
    put("row_id", p)
    put("quarters", p % 32 == 0)
    put("rev4", np.arange(EG, 0, -1)[None, :])
    put("rev8", np.arange(EPG, 0, -1)[None, :])
    pool = np.zeros((P, 2, T), np.float32)
    for g, w in enumerate((2, 4, 8, 16)):
        cnt = np.minimum(np.arange(1, T + 1, dtype=np.float32), np.float32(w))
        pool[64 * (g % 2):64 * (g % 2) + 64, g // 2] = np.float32(1.0) / cnt
    return c, pool.reshape(P, 2 * T)


class Signal:

    def __init__(self, sem):
        self.sem, self.n = sem, 0


class Chained:

    def __init__(self, eng, sem):
        self.eng, self.done = eng, Signal(sem)

    def __call__(self, ins, signal=None):
        s = signal or self.done
        s.n += 1
        ins.then_inc(s.sem, 1)
        self.eng.wait_ge(s.sem, s.n)


class LoopChained:

    def __init__(self, eng, sem, i, per):
        self.eng, self.sem, self.i, self.per, self.n = eng, sem, i, per, 0

    def __call__(self, ins):
        self.n += 1
        ins.then_inc(self.sem, 1)
        self.eng.wait_ge(self.sem, self.i * self.per + (self.n - self.per))

    def end(self):
        assert self.n == self.per, (self.n, self.per)


class PsumBanks:

    def __init__(self, banks, filled, drained):
        self.banks, self.filled, self.drained = banks, filled, drained
        self.order, self.by = [], {}
        self.count = {"dve": 0, "act": 0}
        self.seen = {"dve": 0, "act": 0}

    def fill(self, pe, name, reader):
        n = len(self.order)
        if n >= 8:
            r, k = self.order[n - 8]
            pe.wait_ge(self.drained[r], k + 1)
        assert name not in self.by, name
        self.by[name] = (n % 8, reader, self.count[reader])
        self.order.append((reader, self.count[reader]))
        self.count[reader] += 1
        return self.banks[n % 8]

    def full(self, name, ins):
        ins.then_inc(self.filled[self.by[name][1]], 1)

    def wait_drained(self, pe, name):
        _, r, k = self.by[name]
        pe.wait_ge(self.drained[r], k + 1)

    def wait_filled(self, eng, name):
        _, r, k = self.by[name]
        eng.wait_ge(self.filled[r], k + 1)

    def read(self, eng, name, reader):
        b, r, k = self.by[name]
        assert r == reader and k == self.seen[reader], (name, r, k, self.seen[reader])
        eng.wait_ge(self.filled[r], k + 1)
        return self.banks[b]

    def release(self, name, ins, eng):
        _, r, k = self.by[name]
        self.seen[r] += 1
        ins.then_inc(self.drained[r], 1)
        eng.wait_ge(self.drained[r], k + 1)


class WeightRing:

    def __init__(self, ps, slots, landed):
        self.ps, self.slots, self.landed = ps, slots, landed
        self.n, self.loads, self.taken, self.free_at = len(slots), 0, 0, {}

    def take(self, pe):
        k = self.taken
        self.taken += 1
        pe.wait_ge(self.landed[k % self.n], 16 * (k // self.n + 1))
        return self.slots[k % self.n]

    def last_use(self, bank_name, k=None):
        self.free_at[self.taken - 1 if k is None else k] = bank_name

    def wait_used(self, eng, k):
        at = self.free_at[k]
        if isinstance(at, tuple):
            eng.wait_ge(*at)
        else:
            self.ps.wait_filled(eng, at)

    def load(self, sp, view, src, need=None):
        k = self.loads
        self.loads += 1
        if k >= self.n:
            self.wait_used(sp, k - self.n)
        if need:
            sp.wait_ge(*need)
        s = k % self.n
        sp.dma_start(view(self.slots[s]), src).then_inc(self.landed[s], 16)


def build(nc, a, out):
    ctx = ExitStack()
    with ctx:
        def sb(name, cols, dt=F32, parts=P):
            return ctx.enter_context(nc.sbuf_tensor(name, [parts, cols], dt))

        def twin(name, cols):
            with nc.sbuf_tensor(f"{name}_parts", [P, cols], F32R) as parts:
                pass
            whole = sb(name, cols)
            return whole, parts

        def sem(name):
            return ctx.enter_context(nc.semaphore(name))

        def v3(ap, n):
            return ap.rearrange("p (a b) -> p a b", a=n)

        def over(ap, n, axis):
            x = ap.unsqueeze(axis)
            shape = list(x.shape)
            shape[axis] = n
            return x.to_broadcast(shape)

        ring_mem, ring_mem_r = twin("weight_ring", 6 * 4096)
        cst = sb("constants", NCONST)
        C = {n: cst[:, x:x + w] for n, (x, w) in CONST_COLS.items()}
        ident, ones = C["ident"], C["ones"]
        prm = sb("param_cols", NROWS + 48)
        x = v3(sb("x_tokens", TT * D)[:, :], TT)
        hT_sb, hT_r = twin("hT", KD * T)
        hT = v3(hT_sb[:, :], KD)
        g1b, g1b_r = twin("gate1_rows", D)
        g2b, g2b_r = twin("gate2_rows", D)
        fnw = sb("final_norm_rows", D)
        rows2 = sb("norm_gain_rows", 512)
        kmT = v3(sb("mem_keysT", 2 * T)[:, :], 2)
        vm_sb, vm_r = twin("mem_values", TT * D)
        vm = v3(vm_sb[:, :], TT)
        small = sb("small", 1100)
        small_at = [0]

        def tiny(n, dt=F32):
            v = small[:, small_at[0]:small_at[0] + n]
            small_at[0] += n
            assert small_at[0] <= 1100, small_at
            return v if dt == F32 else v.bitcast(dt)

        work, work_r = twin("work", 14840)
        extra = ring_mem[:, 4 * 4096:6 * 4096]

        def area(*bases):
            left = [[b, 0] for b in bases]

            def alloc(n):
                for e in left:
                    if e[1] + n <= e[0].shape[1]:
                        e[1] += n
                        return e[0][:, e[1] - n:e[1]]
                raise AssertionError((n, [(b.shape, u) for b, u in left]))
            return alloc

        banks = [ctx.enter_context(nc.psum_tensor(f"bank{i}", [P, 512], F32)) for i in range(8)]

        def flat(v):
            return v.rearrange("p a b -> p (a b)")

        m1 = area(work[:, :])
        xn_f = m1(TT * D)
        xn = v3(xn_f, TT)
        mixT = v3(xn_f, KD)
        raw_f = m1(NXB * (T + 3))
        raw = v3(raw_f, NXB)
        xb_f = m1(NXB * T)
        xb = v3(xb_f, NXB)
        cv_f, ce_f = m1(4 * T), m1(4 * T)
        cv, ce = v3(cv_f, 4), v3(ce_f, 4)
        z = v3(m1(TT * SSD_W), TT)
        wpool = v3(m1(2 * P), 2)
        y_f = m1(TT * SSD_W)
        yv = v3(y_f, TT)
        prc = v3(y_f[:, 0:2 * T], 2)
        prm_rows = cv_f[:, 0:2 * P]
        u_mem = area(vm_sb[:, :])
        PAD = 16
        uT, sA, sB = (v3(u_mem(2 * (T + PAD)), 2) for _ in range(3))
        diff = kmT
        r_mem = area(raw_f)
        xtok = v3(r_mem(TT * 1280), TT)
        prevT = v3(r_mem(GROUPS * RPG * HD), GROUPS)
        xdt = v3(hT_sb[:, 0:TT * SSD_W], TT)
        seg2 = [v3(cv_f[:, n * RPG * P:(n + 1) * RPG * P], RPG) for n in range(2)]
        s_mem = area(ring_mem[:, 4 * 4096:5 * 4096])
        segs = [v3(s_mem(RPG * P), RPG) for _ in range(TT * GROUPS)]
        mrow = [s_mem(512) for _ in range(2)]
        t_mem = area(ring_mem[:, 5 * 4096:6 * 4096])
        mem_x = v3(t_mem(TT * D), TT)
        memT = v3(t_mem(KD * T), KD)
        zt = [mem_x[:, t, 0:SSD_W] for t in range(TT)]
        xcd = ce_f[:, 0:SSD_W]
        ybuf = ce_f[:, SSD_W:SSD_W + RPG * HD]
        m3 = area(work[:, TT * D:])
        xeT = v3(m3(KD * P), KD)
        hs = m3(D)
        ge = v3(m3(4 * SLOTS), 4)
        gt = v3(m3(4 * SLOTS), 4)
        sT = [v3(m3(4 * SLOTS), 4) for _ in range(2)]
        osb = m3(D)
        mk, msq = flat(kmT), osb[:, 0:TT * EH * EQ]
        pick = v3(m3(TT * P), TT)
        wr = v3(m3(KD * (EG + NE)), KD)
        acc_f = m3(TT * D)
        acc = v3(acc_f, TT)
        diag = v3(acc_f[:, D:2 * D], 8)
        slot_rows, gate_rows = m3(2 * T), m3(2 * T)
        share_f = m3(2 * T)
        slot_id = m3(P)
        m2 = area(work[:, :], extra)
        ysum, obr = v3(m2(TT * D), TT), v3(m2(TT * D), TT)
        pr_f, pT_f = m2(3 * TT * T), m2(2 * TT * T)
        pr, pT = ([f_[:, n * TT * T:(n + 1) * TT * T] for n in range(m)] for f_, m in ((pr_f, 3), (pT_f, 2)))
        QW = MH * (NOPE + ROPE)
        q = [vm_sb[:, 0:QW], m2(QW)]
        ckv = [v3(c_, 1) for c_ in (vm_sb[:, QW:QW + KVR + ROPE], flat(kmT)[:, 0:KVR + ROPE])]
        used2 = 2 * TT * D + 5 * TT * T + QW

        def branch_area():
            return area(work[:, used2:], extra)
        b1 = branch_area()
        gv, gr = v3(b1(TT * D), TT), v3(b1(TT * D), TT)
        gates1 = b1(2 * GH * T)
        gbT, lev = (v3(gates1[:, n * GH * T:(n + 1) * GH * T], GH) for n in range(2))
        gates1 = v3(gates1, TT)
        gqT, gkT = v3(b1(GH * T), GH), v3(b1(GH * T), GH)
        qk = v3(b1(GH * T), GH)
        att = [v3(b1(GH * P), GH) for _ in range(3)]
        la, lt = v3(b1(TT * GH * DK), TT), v3(b1(TT * GH * DK), TT)
        gaT = b1(T)
        wgate = b1(GH * DK)
        bgla = b1(GH * DK)
        ggla = b1(DV)
        b0 = area(flat(gv))
        qm = v3(b0(TT * EH * EQ), TT)
        qmT = v3(b0(2 * T), 2)
        qsq = v3(b0(TT * EH * EQ), TT)
        gates2 = gr
        b2 = branch_area()
        gates0 = v3(b2(TT * D), TT)
        kv = v3(b2(TT * MH * (NOPE + VD)), TT)
        qnT, qrT = v3(b2(MH * T), MH), v3(b2(4 * T), 4)
        knT, krT = v3(b2(MH * T), MH), b2(T)
        qsqs = [flat(qnT)[:, 0:QW], flat(knT)[:, 0:QW]]
        ksqs = [pr_f[:, 0:MH * NOPE], pT_f]
        ckT = v3(b2(2 * T), 2)
        ropeb = v3(b2(TT * MH * ROPE), TT)
        kr2 = v3(b2(TT * 2 * ROPE), TT)
        nsq = b2(MH * ROPE)
        csq = pr_f[:, 0:KVR]
        pieces_ = [work_r[:, n * 4 * T:(n + 1) * 4 * T] for n in range(14)] + [g1b_r[:, :], g2b_r[:, :]]
        aH, aL = ([v3(pieces_[2 * n + m], 4) for n in range(8)] for m in range(2))
        relu = [fnw[:, n * 2 * T:(n + 1) * 2 * T] for n in range(2)]
        hH, hL = (v3(v_, KD) for v_ in (vm_r[:, :], hT_r[:, :]))

        S = {}

        def ev(name):
            if name not in S:
                S[name] = sem(name)
            return S[name]
        ps = PsumBanks(banks, {r: ev(f"bank_filled_for_{r}") for r in ("dve", "act")},
                       {r: ev(f"bank_drained_by_{r}") for r in ("dve", "act")})
        ps2 = PsumBanks(banks, {r: ev(f"late_bank_filled_for_{r}") for r in ("dve", "act")},
                        {r: ev(f"late_bank_drained_by_{r}") for r in ("dve", "act")})
        slots = [ring_mem[:, i * 4096:(i + 1) * 4096] for i in range(6)]
        ring = WeightRing(ps, slots[:4], [ev(f"weights_landed_{i}") for i in range(4)])
        low_slots = [ring_mem_r[:, i * 4096:(i + 1) * 4096] for i in range(4)]
        high_slots = [ring_mem_r[:, i * 4096:(i + 1) * 4096] for i in (4, 5)]
        ring2 = WeightRing(ps2, slots[:4], [ev(f"late_weights_landed_{i}") for i in range(4)])
        xw_landed = [ev(f"expert_weights_landed_{i}") for i in range(6)]

        cs = tiny(KD)
        ctmp = tiny(KD)
        modc = tiny(48)
        ss = tiny(2)
        rs = tiny(40)
        rt = [tiny(40) for _ in range(2)]
        dt_b, alog_b, dskip_b = tiny(HEADS), tiny(HEADS), tiny(HEADS)
        dtr, dta, dtv = (v3(tiny(TT * HEADS), TT) for _ in range(3))
        nega = tiny(HEADS)
        acs = v3(tiny(3 * HEADS), 3)
        eacs, dte = tiny(HEADS), tiny(HEADS)
        gss = tiny(TT * GROUPS)
        rb = tiny(EG + NE)
        lg = v3(tiny(TT * (EG + NE)), TT)
        gm, pg, gsm = tiny(TT), tiny(TT), tiny(TT)
        ohg = v3(tiny(TT * EG), TT)
        gtm = v3(tiny(TT * EG), TT)
        w8, oh1, oh2, t8 = (v3(tiny(TT * EPG), TT) for _ in range(4))
        v1, v2, e2, gate1, gate2 = (tiny(TT) for _ in range(5))
        route_area = area(acc_f[:, 0:D])
        wide = route_area(TT * NE)
        sel1, sel2, sel = (v3(route_area(TT * NE), TT) for _ in range(3))
        cnt, nblk = route_area(NE), route_area(NE)
        cumA, cumB = route_area(2 * NE), route_area(2 * NE)
        slot_of = v3(route_area(TT * NE), TT)
        dest = [tiny(TT) for _ in range(2)]
        be, slot_col = tiny(1), tiny(1)
        meta = tiny(P + 2, I32)
        npf = tiny(1)
        pos_i, pos_f = tiny(TT, I32), tiny(TT)
        NI = ROPE // 2
        ang, rn, cosv, sinv = (v3(tiny(TT * NI), TT) for _ in range(4))
        mxs, sums = [tiny(TT) for _ in range(3)], [tiny(TT) for _ in range(3)]
        hss = tiny(40)

        def k_rows(w, cols):
            return w.rearrange("(k p) n -> p k n", p=P)[:, :, cols]

        w_ada, w_in, w_out = a["w_ada"][0], a["w_in"][0], a["w_out"][0]
        w13, w2 = a["w13"][0], a["w2"][0]
        w_in2, w_ukv, w_mkv = a["w_in_2"][0], a["w_ukv_2"][0], a["w_mem_kv_2"][0]
        w_o2, w_up, w_down = a["w_o_2"][0], a["w_up_2"][0], a["w_down_2"][0]

        def cols_of(n, k=KD):
            return lambda s: s[:, 0:k * n].rearrange("p (k n) -> p k n", k=k)

        block = ctx.enter_context(nc.Block())
        ADA1, ADA2 = range(0, 4), range(4, 12)
        IN_SLOTS = [(i * 512, min(512, IN1 - i * 512)) for i in range(6)]
        IN_ORDER = (2, 3, 4, 5, 0, 1)
        MEM_SLOTS = [(0, 512), (512, 512), (1024, 256)]
        BESIDE = [[("ada", 4), ("mk", 0), ("mk", 1), ("adaT", 4)], [("mv", 0, 0), ("mv", 0, 1), ("ada", 5), ("adaT", 5)],
                  [("ada", 6), ("mv", 1, 0), ("adaT", 6)], [("mv", 1, 1), ("ada", 7), ("adaT", 7)],
                  [("ada", 8), ("mv", 2, 0), ("adaT", 8)], [("mv", 2, 1), ("ada", 9), ("adaT", 9)],
                  [("ada", 10), ("adaT", 10)], [("ada", 11), ("adaT", 11)]]
        LATE_A = [(O_MQ, 256), (O_GATE + 2048, 512), (O_GATE + 2560, 512), (O_GQ, 512), (O_GK, 512), (O_GA, 16),
                  (O_GV, 512), (O_GV + 512, 512), (O_GR, 512), (O_GR + 512, 512), (O_Q, 512), (O_Q + 512, 512),
                  (O_Q + 1024, 512), (O_CKV, 320), (O_GATE + 1024, 512), (O_GATE + 1536, 512), (O_GATE, 512)]
        LATE_B = [(O_GATE + 512, 512)]
        FFN_LOAD = len(LATE_A) + 1 + len(LATE_B) + 2
        FILL = [("gr", 0, 0), ("gr", 0, 1), ("gr", 1, 0), ("gr", 1, 1)] + [("q", n, t) for n in range(3) for t in range(2)] + [
            ("ckv", 0, 0), ("ckv", 0, 1)]
        SHARE = (1, 1, 2, 1, 1, 2, 1, 1, 2)
        FILLS = [FILL[sum(SHARE[:n]):sum(SHARE[:n + 1])] for n in range(LEVELS + 2)]
        @block.tensor
        def _(pe):
            mm = nc.tensor.matmul

            def transposes(ps, name, reader, pieces):
                bank = ps.fill(pe, name, reader)
                for src, col in pieces:
                    n, w = src.shape[0], src.shape[1]
                    last = nc.tensor.transpose(bank[0:w, col:col + n], src, ident[0:n, 0:n])
                ps.full(name, last)

            def all_channels(ps, name, src):
                for j in range(4):
                    transposes(ps, f"{name}{j}", ("dve", "act")[j % 2],
                               [(src[:, t, (2 * j + b) * P:(2 * j + b + 1) * P], b * T + t * P)
                                for b in range(2) for t in range(TT)])

            def tokens_out(ps, name, reader, lhs, w, width, col=0, k=KD):
                for t in range(TT):
                    bank = ps.fill(pe, f"{name}t{t}", reader)
                    for j in range(k):
                        last = mm(bank[:, 0:width], lhs[:, j, t * P:t * P + P], w[:, j, col:col + width],
                                  start=(j == 0), stop=(j == k - 1))
                    ps.full(f"{name}t{t}", last)

            def channels_out(ps, name, reader, lhs, w, col):
                bank = ps.fill(pe, name, reader)
                for b in range(2):
                    for j in range(KD):
                        last = mm(bank[:, b * T:b * T + T], w[:, j, col + b * P:col + b * P + P], lhs[:, j, :],
                                  start=(j == 0), stop=(j == KD - 1))
                ps.full(name, last)

            pe.wait_ge(ev("constants_loaded"), 16)
            pe.wait_ge(ev("param_rows_loaded"), 192)
            transposes(ps, "params", "dve", [(prm_rows[0:NROWS, 0:P], 0), (prm_rows[0:48, P:2 * P], NROWS)])

            def ada(n):
                w = cols_of(512)(ring.take(pe))
                if n == 0:
                    pe.wait_ge(ev("c_gated"), 1)
                bank = ps.fill(pe, f"ada{n}", "act")
                for k in range(KD):
                    g = k % 4
                    last = mm(bank[32 * g:32 * g + 32, :], cs[:, k:k + 1].to_broadcast([P, 32]), w[:, k, :],
                              start=(k < 4), stop=(k >= 4), tile_position=(0, 32 * g))
                ps.full(f"ada{n}", last)
                ring.last_use(f"ada{n}")

            def ada_spread(n):
                ps.wait_drained(pe, f"ada{n}")
                bank = ps.fill(pe, f"adaT{n}", "dve")
                if n // 2 in (2, 5):
                    last = mm(bank[:, :], C["quarters"].to_broadcast([P, P]), mrow[n % 2], start=True, stop=True)
                else:
                    for j in range(4):
                        last = mm(bank[:, j:j + 1], mrow[n % 2][:, j * P:j * P + P], C["quarters"],
                                  start=True, stop=True)
                ps.full(f"adaT{n}", last)

            for n in ADA1:
                ada(n)
                if n:
                    ada_spread(n - 1)
            ada_spread(ADA1[-1])

            pe.wait_ge(ev("x_normed"), 1)
            all_channels(ps, "h1", xn)
            for j in range(4):
                ps.wait_drained(pe, f"h1{j}")
            for s_ in range(2, 6):
                wd = IN_SLOTS[s_][1]
                w = cols_of(wd)(ring.take(pe))
                channels_out(ps, f"xb{2 * (s_ - 2)}", "act", hT, w, 0)
                if s_ < 5:
                    channels_out(ps, f"xb{2 * (s_ - 2) + 1}", "act", hT, w, 256)
                    ring.last_use(f"xb{2 * (s_ - 2) + 1}")
                else:
                    bank = ps.fill(pe, "dt", "dve")
                    for t in range(TT):
                        for j in range(KD):
                            last = mm(bank[:, t * HEADS:(t + 1) * HEADS], hT[:, j, t * P:t * P + P],
                                      w[:, j, 256:256 + HEADS], start=(j == 0), stop=(j == KD - 1))
                    ps.full("dt", last)
                    ring.last_use("dt")
            pe.wait_ge(ev("mem_normed"), 1)
            all_channels(ps, "memT", mem_x)
            w = cols_of(512)(ring.take(pe))
            channels_out(ps, "u", "act", hT, w, 0)
            bank = ps.fill(pe, "z0", "act")
            for t in range(TT):
                for j in range(KD):
                    last = mm(bank[:, t * 256:t * 256 + 256], hT[:, j, t * P:t * P + P], w[:, j, 256:512],
                              start=(j == 0), stop=(j == KD - 1))
            ps.full("z0", last)
            ring.last_use("z0")
            pe.wait_ge(ev("decay_steps"), 1)
            bank = ps.fill(pe, "acs", "dve")
            for t in range(TT):
                mm(bank[:, t * HEADS:(t + 1) * HEADS], C["tri"], dta[:, t, :], start=True, stop=True)
            last = mm(bank[:, 2 * HEADS:3 * HEADS], ones, dta[:, 0, :], start=True, stop=True)
            ps.full("acs", last)

            def decay_rows(t):
                for g in range(GROUPS):
                    bank = ps.fill(pe, f"row{t}{g}", "dve")
                    for r in range(RPG):
                        h = RPG * g + r
                        last = mm(bank[:, r * P:r * P + P], dta[:, t, h:h + 1].to_broadcast([P, P]), C["tri"],
                                  start=True, stop=True)
                    ps.full(f"row{t}{g}", last)
            decay_rows(0)
            w = cols_of(512)(ring.take(pe))
            tokens_out(ps, "z1", "act", hT, w, 512)
            ring.last_use("z1t1")
            decay_rows(1)
            pe.wait_ge(ev("conv_gated"), 4)
            for t in range(TT):
                lots = ((0, 4), (4, 8), (8, 10)) if t == 0 else ((0, 4), (4, 6))
                for lo, hi in lots:
                    transposes(ps, f"xs{t}_{lo}", "act",
                               [(xb[:, k, t * P:t * P + P], (k - lo) * P) for k in range(lo, hi)])
            pe.wait_ge(ev("pool_weights_loaded"), 64)
            pe.wait_ge(ev("pooled"), 1)
            bank = ps.fill(pe, "pool", "act")
            for b in range(2):
                last = mm(bank[:, b * T:b * T + T], wpool[:, b, :], diff[:, b, :], start=True, stop=True)
            ps.full("pool", last)

            def beside(step):
                for what, n, *t in BESIDE[step]:
                    if what == "ada":
                        ada(n)
                    elif what == "adaT":
                        ada_spread(n)
                    else:
                        t, part, width, col = (n, 0, 256, 0) if what == "mk" else (
                            t[0], n, (256, 512, 256)[n], 256 if n == 0 else 0)
                        if t == 0 and (what == "mk" or n):
                            mem_w[part] = (cols_of(MEM_SLOTS[part][1])(ring.take(pe)), ring.taken - 1)
                        w, k = mem_w[part]
                        name = f"mk{t}" if what == "mk" else f"mv{n}{t}"
                        bank = ps.fill(pe, name, "dve" if what == "mk" else "act")
                        for j in range(KD):
                            last = mm(bank[:, 0:width], memT[:, j, t * P:t * P + P], w[:, j, col:col + width],
                                      start=(j == 0), stop=(j == KD - 1))
                        ps.full(name, last)
                        if t and what == "mv":
                            ring.last_use(name, k)
            mem_w = {}
            for j in range(4):
                ps.wait_drained(pe, f"memT{j}")
            pe.wait_ge(ev("xcd_ready"), 1)
            for g in range(GROUPS):
                bank = ps.fill(pe, f"state{g}", "dve")
                last = mm(bank[:, 0:RPG * HD], xtok[:, 0, SSD_W + g * P:SSD_W + g * P + P],
                          xcd[:, g * RPG * HD:(g + 1) * RPG * HD], start=True, stop=True)
                ps.full(f"state{g}", last)

            def pair_products(n):
                t, g = divmod(n, GROUPS)
                bank = ps.fill(pe, f"cb{n}", "dve")
                last = mm(bank[:, 0:P], xb[:, 6 + g, t * P:t * P + P], xb[:, 10 + g, t * P:t * P + P],
                          start=True, stop=True)
                ps.full(f"cb{n}", last)
            pair_products(0)
            for n in range(TT * GROUPS):
                t, g = divmod(n, GROUPS)
                if n + 1 < TT * GROUPS:
                    pair_products(n + 1)
                beside(n)
                ps.wait_drained(pe, f"cb{n}")
                bank = ps.fill(pe, f"yd{n}", "dve")
                for r in range(RPG):
                    h = RPG * g + r
                    last = mm(bank[:, r * HD:r * HD + HD], seg2[n % 2][:, r, :], xdt[:, t, h * HD:h * HD + HD],
                              start=True, stop=True)
                ps.full(f"yd{n}", last)
                if t:
                    bank = ps.fill(pe, f"yo{g}", "dve")
                    last = mm(bank[:, 0:RPG * HD], xb[:, 10 + g, P:2 * P], prevT[:, g, :], start=True, stop=True)
                    ps.full(f"yo{g}", last)
            pe.wait_ge(ev("ssd_normed"), 1)
            for j in range(3):
                transposes(ps, f"yT{j}", "act", [(yv[:, t, (2 * j + b) * P:(2 * j + b + 1) * P], b * T + t * P)
                                                for b in range(2) for t in range(TT)])
            for j in range(3):
                ps.wait_drained(pe, f"yT{j}")
            for n in range(2):
                w = cols_of(512)(ring.take(pe))
                tokens_out(ps, f"mix{n}", "dve", mixT, w, 512)
                ring.last_use(f"mix{n}t1")
            pe.wait_ge(ev("x_normed"), 2)
            all_channels(ps, "h2", xn)
            for j in range(4):
                ps.wait_drained(pe, f"h2{j}")
            pe.wait_ge(ev("router_loaded"), 32)
            tokens_out(ps, "router", "dve", hT, wr, EG + NE)
            pe.wait_ge(ev("chosen"), 1)
            bank = ps.fill(pe, "rank", "dve")
            mm(bank[:, 0:NE], C["strict"], sel[:, 0, :], start=True, stop=True)
            mm(bank[:, NE:2 * NE], ones, sel[:, 0, :], start=True, stop=False)
            mm(bank[:, NE:2 * NE], C["strict"], sel[:, 1, :], start=False, stop=True)
            mm(bank[:, 2 * NE:3 * NE], ones, sel[:, 0, :], start=True, stop=False)
            last = mm(bank[:, 2 * NE:3 * NE], ones, sel[:, 1, :], start=False, stop=True)
            ps.full("rank", last)
            pe.wait_ge(ev("block_experts"), 1)
            bank = ps.fill(pe, "experts", "dve")
            last = mm(bank[0:1, 0:P], be, ident, start=True, stop=True)
            ps.full("experts", last)

            pe.wait_ge(ev("routed"), 1)
            pairs = pe.value_load(meta[0:1, P:P + 1], min_val=4, max_val=MAXB // 2)
            last_pair = pe.value_load(meta[0:1, P + 1:P + 2], min_val=3, max_val=MAXB // 2 - 1)
            gA, gB, hA, hB, tA, tB, oA, oB = banks

            def gather(i):
                pe.wait_ge(ev("slots_picked"), i + 1)
                for k in range(KD):
                    dst = (gA, gB)[k // 4][:, (k % 4) * P:(k % 4) * P + P]
                    for t in range(TT):
                        last = mm(dst, xn[:, t, k * P:k * P + P], pick[:, t, :], start=(t == 0), stop=(t == TT - 1))
                    if k % 4 == 3:
                        last.then_inc(ev("gather_filled"), 1)

            def hidden(i, b):
                if b == 0:
                    pe.wait_ge(ev("slots_in_by_act"), i + 1)
                    pe.wait_ge(ev("slots_in_by_dve"), i + 1)
                    pe.wait_ge(ev("hidden_out_by_act"), i * 2)
                    pe.wait_ge(ev("hidden_out_by_dve"), i * 2)
                else:
                    pe.wait_ge(ev("hidden_out_by_act"), i * 2 + 1)
                    pe.wait_ge(ev("hidden_out_by_dve"), i * 2 + 1)
                for part in range(2):
                    pe.wait_ge(xw_landed[3 * b + part], i * 16 + 16)
                w = [slots[3 * b + part].rearrange("p (k n) -> p k n", k=4) for part in range(2)]
                for n, dst in enumerate((hA, hB)):
                    for k in range(4):
                        for part in range(2):
                            last = mm(dst[SLOTS * part:SLOTS * part + SLOTS, :],
                                      xeT[:, 4 * part + k, b * SLOTS:b * SLOTS + SLOTS],
                                      w[part][:, k, n * 512:n * 512 + 512], start=(k == 0), stop=(k == 3))
                    last.then_inc(ev("hidden_filled"), 1)

            def fold(i, b):
                pe.wait_ge(ev("hidden_out_by_act"), i * 2 + (b + 1))
                pe.wait_ge(ev("hidden_out_by_dve"), i * 2 + (b + 1))
                pe.wait_ge(ev("hidden_gated"), i * 2 + b)
                for f in range(8):
                    last = mm((tA, tB)[f // 4][:, (f % 4) * P:(f % 4) * P + 96], hs[:, f * P:f * P + P],
                              C["fold"][:, 0:96], start=True, stop=True)
                    if f % 4 == 3:
                        last.then_inc(ev("folded"), 1)

            def rows_out(m):
                pe.wait_ge(ev("hidden_gated"), m * 2 + 2)
                pe.wait_ge(ev("parts_added"), m * 4 + 1)
                for b in range(2):
                    pe.wait_ge(xw_landed[3 * b + 2], m * 16 + 16)
                w = [slots[3 * b + 2].rearrange("p (k n) -> p k n", k=4) for b in range(2)]
                for n_, dst in enumerate((oA, oB)):
                    for f in range(4):
                        for b in range(2):
                            last = mm(dst[SLOTS * b:SLOTS * b + SLOTS, :], sT[b][:, f, :],
                                      w[b][:, f, n_ * 512:n_ * 512 + 512], start=(f == 0), stop=(f == 3))
                    last.then_inc(ev(("rows_filled_for_act", "rows_filled_for_dve")[n_]), 1)

            def combine(m, t):
                if t == 0:
                    pe.wait_ge(ev("rows_out_by_act"), m + 1)
                    pe.wait_ge(ev("rows_out_by_dve"), m + 1)
                    pe.wait_ge(ev("shares_ready"), m + 1)
                else:
                    pe.wait_ge(ev("parts_added"), m * 4 + 3)
                for n_, dst in enumerate((oA, oB)):
                    mm(dst[:, :], share_f[:, t * P:t * P + P], osb[:, n_ * 512:n_ * 512 + 512], start=True,
                       stop=True).then_inc(ev("parts_filled"), 1)

            for n, name in enumerate(("slot_rows", "gate_rows")):
                pe.wait_ge(ev("columns_spread"), 4 * n + 4)
                bank = ps.fill(pe, name, ("dve", "act")[n])
                for m in range(4):
                    last = mm(bank[:, m * P:m * P + P], ones, diag[:, 4 * n + m, :], start=True, stop=True)
                ps.full(name, last)
            pe.wait_ge(ev("mem_keys_normed"), 1)
            transposes(ps, "mkT", "act", [(mk[:, t * EH * EQ + b * P:t * EH * EQ + b * P + P], b * T + t * P)
                                          for b in range(2) for t in range(TT)])
            for r in ("dve", "act"):
                pe.wait_ge(ps.drained[r], ps.count[r])
            pe.sem_inc(ev("parts_filled"), 1)
            gather(0)
            hidden(0, 0)
            fold(0, 0)
            hidden(0, 1)
            gather(1)
            fold(0, 1)
            with pe.Fori(1, pairs) as i:
                hidden(i, 0)
                rows_out(i - 1)
                fold(i, 0)
                hidden(i, 1)
                combine(i - 1, 0)
                gather(i + 1)
                fold(i, 1)
                combine(i - 1, 1)
            rows_out(last_pair)
            combine(last_pair, 0)
            combine(last_pair, 1)

            def softmax_products(name, qs, ks, causal):
                bank = ps2.fill(pe, f"s_{name}", "dve")
                for t in range(TT):
                    at, w = ((0, P), (P, T))[t] if causal else (t * T, T)
                    n = len(qs)
                    for m, (qa, ka) in enumerate(zip(qs, ks)):
                        last = mm(bank[:, at:at + w], qa[:, t * P:t * P + P], ka[:, 0:w], start=(m == 0), stop=(m == n - 1))
                ps2.full(f"s_{name}", last)

            def pieces(causal):
                return ((0, 0), (1, 0), (1, 1)) if causal else ((0, 0), (0, 1), (1, 0), (1, 1))

            def softmax_transposes(name, idx, causal):
                pe.wait_ge(ev("probs_ready"), idx + 1)
                transposes(ps2, f"pT_{name}", "act", [(pr[idx % 3][:, n * P:n * P + P], n * P)
                                                     for n in range(len(pieces(causal)))])

            def softmax_values(name, idx, value, width, causal):
                ps2.wait_drained(pe, f"pT_{name}")
                bank = ps2.fill(pe, f"o_{name}", "dve")
                for n, (t, k) in enumerate(pieces(causal)):
                    last = mm(bank[:, t * width:t * width + width], pT[idx % 2][:, n * P:n * P + P], value(k),
                              start=(k == 0), stop=(k == 1 or (causal and t == 0)))
                ps2.full(f"o_{name}", last)

            def attention(heads, args, first, value, width, causal, fill=()):
                for h in range(heads + 2):
                    if h < heads:
                        softmax_products(f"{first + h}", *args(h), causal)
                    if h < len(fill):
                        fill[h]()
                    if h >= 2:
                        softmax_transposes(f"{first + h - 2}", first + h - 2, causal)
                        softmax_values(f"{first + h - 2}", first + h - 2, value(h - 2), width, causal)

            def gate(br, n):
                w = cols_of(512)(ring2.take(pe))
                tokens_out(ps2, f"gate{br}{n}", "dve", hT, w, 512)
                ring2.last_use(f"gate{br}{n}t1")

            pe.wait_ge(ev("parts_added"), pairs * 4 + 1)
            pe.wait_ge(ev("x_normed"), 3)
            all_channels(ps2, "h3", xn)
            for j in range(4):
                ps2.wait_drained(pe, f"h3{j}")
            w = cols_of(256)(ring2.take(pe))
            tokens_out(ps2, "mq", "dve", hT, w, 256)
            ring2.last_use("mqt1")
            for n in range(2):
                gate(2, n)
            pe.wait_ge(ev("mem_q_normed"), 1)
            transposes(ps2, "mqT", "act", [(qm[:, t, b * P:b * P + P], b * T + t * P)
                                           for b in range(2) for t in range(TT)])
            ps2.wait_drained(pe, "mqT")

            def gla_channels(nm, b):
                if b == 0:
                    taken[0] = cols_of(512)(ring2.take(pe))
                channels_out(ps2, f"{nm}{b}", "act", hT, taken[0], b * 256)
                if b:
                    ring2.last_use(f"{nm}1")
            taken = [None]
            attention(EH, lambda h: ([qmT[64 * (h % 2):64 * (h % 2) + 64, h // 2, :]],
                                     [kmT[64 * (h % 2):64 * (h % 2) + 64, h // 2, :]]), 0,
                      lambda h: lambda k: vm[:, k, h * EV:h * EV + EV], EV, False,
                      [lambda nm=nm, b=b: gla_channels(nm, b) for nm in ("gq", "gk") for b in range(2)])
            w = cols_of(GRANK)(ring2.take(pe))
            bank = ps2.fill(pe, "ga", "act")
            for j in range(KD):
                last = mm(bank[0:GRANK, 0:T], w[:, j, :], hT[:, j, :], start=(j == 0), stop=(j == KD - 1))
            ps2.full("ga", last)
            ring2.last_use("ga")
            for n in range(2):
                w = cols_of(512)(ring2.take(pe))
                tokens_out(ps2, f"gv{n}", "act", hT, w, 512)
                ring2.last_use(f"gv{n}t1")
                if n == 0:
                    ps2.wait_drained(pe, "ga")
                    pe.wait_ge(ev("gla_rows_loaded"), 48)
                    for t in range(TT):
                        bank = ps2.fill(pe, f"lg{t}", "dve")
                        last = mm(bank[:, :], gaT[0:GRANK, t * P:t * P + P], wgate[0:GRANK, :], start=True, stop=True)
                        ps2.full(f"lg{t}", last)
            def fill(lvl):
                for nm, n, t in FILLS[lvl]:
                    width = 320 if nm == "ckv" else 512
                    if t == 0:
                        taken[0] = cols_of(width)(ring2.take(pe))
                    bank = ps2.fill(pe, f"{nm}{n}t{t}", "act")
                    for j in range(KD):
                        last = mm(bank[:, 0:width], hT[:, j, t * P:t * P + P], taken[0][:, j, :], start=(j == 0),
                                  stop=(j == KD - 1))
                    ps2.full(f"{nm}{n}t{t}", last)
                    if t:
                        ring2.last_use(f"{nm}{n}t1")
            fill(0)
            pe.wait_ge(ev("log_decays"), 1)
            for j in range(2):
                bank = ps2.fill(pe, f"cum{j}", "act")
                for b in range(2):
                    for t in range(TT):
                        h = 2 * j + b
                        last = mm(bank[:, b * T + t * P:b * T + t * P + P], la[:, t, h * DK:h * DK + DK], C["tri"],
                                  start=True, stop=True)
                ps2.full(f"cum{j}", last)
            for lvl in range(LEVELS + 1):
                if lvl == 0:
                    ps2.wait_drained(pe, "gk1")
                else:
                    fill(lvl)
                    pe.wait_ge(ev("level_ready"), lvl)
                for t in range(TT):
                    bank = ps2.fill(pe, f"lvl{lvl}{t}", "dve")
                    for h in range(GH):
                        k_ = (gkT if lvl == 0 else qk)[:, h, t * P:t * P + P]
                        q_ = (gqT if lvl == 0 else qk)[:, h, t * P:t * P + P]
                        last = mm(bank[:, h * P:h * P + P], k_, q_, start=True, stop=True)
                    ps2.full(f"lvl{lvl}{t}", last)
            fill(LEVELS + 1)
            pe.wait_ge(ev("level_ready"), LEVELS + 1)
            bank = ps2.fill(pe, "cross", "act")
            for h in range(GH):
                last = mm(bank[:, h * P:h * P + P], qk[:, h, 0:P], qk[:, h, P:2 * P], start=True, stop=True)
            ps2.full("cross", last)
            ps2.wait_drained(pe, f"lvl{LEVELS}1")
            ps2.wait_drained(pe, "cross")
            for h in range(GH):
                bank = ps2.fill(pe, f"go{h}", "dve")
                mm(bank[:, 0:DV], att[0][:, h, :], gv[:, 0, h * DV:h * DV + DV], start=True, stop=True)
                mm(bank[:, DV:2 * DV], att[2][:, h, :], gv[:, 0, h * DV:h * DV + DV], start=True, stop=False)
                last = mm(bank[:, DV:2 * DV], att[1][:, h, :], gv[:, 1, h * DV:h * DV + DV], start=False, stop=True)
                ps2.full(f"go{h}", last)
            gate(1, 0)
            gate(1, 1)
            gate(0, 0)
            pe.wait_ge(ev("ckv_normed"), 1)
            transposes(ps2, "ckT", "act", [(ckv[t][:, 0, b * P:b * P + P], b * T + t * P)
                                           for b in range(2) for t in range(TT)])
            ps2.wait_drained(pe, "ckT")
            w = cols_of(2048, 2)(ring2.take(pe))
            for n in range(4):
                tokens_out(ps2, f"kv{n}", "act", ckT, w, 512, col=n * 512, k=2)
            ring2.last_use("kv3t1")
            gate(0, 1)
            pe.wait_ge(ev("rope_k_ready"), 1)
            transposes(ps2, "krT", "act", [(kr2[:, t, :], t * P) for t in range(TT)])
            pe.wait_ge(ev("mla_q_ready"), 1)
            for j in range(4):
                transposes(ps2, f"qnT{j}", "act", [(q[t][:, (2 * j + b) * 192:(2 * j + b) * 192 + P], b * T + t * P)
                                                  for b in range(2) for t in range(TT)])
            for j in range(2):
                transposes(ps2, f"qrT{j}", "act", [(ropeb[:, t, (2 * j + b) * P:(2 * j + b + 1) * P], b * T + t * P)
                                                  for b in range(2) for t in range(TT)])
            pe.wait_ge(ev("mla_k_ready"), 1)
            for j in range(4):
                transposes(ps2, f"knT{j}", "act",
                           [(kv[:, t, (2 * j + b) * 256:(2 * j + b) * 256 + P], b * T + t * P)
                            for b in range(2) for t in range(TT)])
            for j in range(4):
                ps2.wait_drained(pe, f"knT{j}")

            def mla_args(h):
                lo = 64 * (h % 2)
                return ([qnT[:, h, :], qrT[lo:lo + 64, h // 2, :]], [knT[:, h, :], krT[lo:lo + 64, :]])
            attention(MH, mla_args, EH, lambda h: lambda k: kv[:, k, h * 256 + P:h * 256 + 256], VD, True)
            pe.wait_ge(ev("branches_summed"), 1)
            all_channels(ps2, "ysT", ysum)
            for j in range(4):
                ps2.wait_drained(pe, f"ysT{j}")
            for n in range(2):
                w = cols_of(512)(ring2.take(pe))
                tokens_out(ps2, f"wo{n}", "dve", hT, w, 512)
                ring2.last_use(f"wo{n}t1")
            pe.wait_ge(ev("x_normed"), 4)
            all_channels(ps2, "h4", xn)
            for j in range(4):
                ps2.wait_drained(pe, f"h4{j}")
            pe.wait_ge(ev("ffn_input_split"), 1)

            def parts(n, k, width):
                ring2.take(pe)
                low = low_slots[(FFN_LOAD + n) % 4]
                pe.wait_ge(ev("low_parts"), n + 1)
                return cols_of(width, k)(high_slots[n % 2]), cols_of(width, k)(low)

            for n in range(8):
                wH, wL = parts(n, KD, 512)
                for b in range(2):
                    bank = ps2.fill(pe, f"up{n}{b}", "act")
                    for c in range(2):
                        for j in range(KD):
                            at = (2 * b + c) * P
                            for m, (w_, h_) in enumerate(((wH, hH), (wH, hL), (wL, hH))):
                                last = mm(bank[:, c * T:c * T + T], w_[:, j, at:at + P], h_[:, j, :],
                                          start=(j == 0 and m == 0), stop=(j == KD - 1 and m == 2))
                    ps2.full(f"up{n}{b}", last)
                ring2.last_use(f"up{n}1")
            accs = [ps2.fill(pe, f"down{t}{n}", "dve") for t in range(TT) for n in range(2)]
            for g in range(8):
                wH, wL = parts(8 + g, 4, D)
                pe.wait_ge(ev("ffn_squared"), 2 * g + 2)
                for m, acc_ in enumerate(accs):
                    t, n = m // 2, m % 2
                    for j in range(4):
                        for i_, (a_, w_) in enumerate(((aH, wH), (aH, wL), (aL, wH))):
                            last = mm(acc_[:, :], a_[g][:, j, t * P:t * P + P], w_[:, j, n * 512:n * 512 + 512],
                                      start=(g == 0 and j == 0 and i_ == 0), stop=(g == 7 and j == 3 and i_ == 2))
                    if g == 7:
                        ps2.full(f"down{t}{n}", last)
                    elif m == 3:
                        last.then_inc(ev("down_weights_used"), 1)
                ring2.last_use((ev("down_weights_used"), g + 1))
        @block.scalar
        def _(act):
            do = Chained(act, ev("act_step"))
            A = nc.scalar.activation

            def raise_(name):
                act.sem_inc(ev(name), 1)

            def drain(ps, name, pairs, scale=None, shift=None):
                bank = ps.read(act, name, "act")
                for n, (dst, src) in enumerate(pairs(bank)):
                    sc, sh = (scale[n] if scale else 1.0), (shift[n] if shift else 0.0)
                    ins = A(dst, src, ACT.Identity, bias=sh, scale=sc)
                    if n == len(pairs(bank)) - 1:
                        ps.release(name, ins, act)
                    else:
                        do(ins)

            def to_channels(ps, name, dst, scale, shift):
                for j in (1, 3):
                    drain(ps, f"{name}{j}", lambda bank: [(dst[:, 2 * j + b, :], bank[:, b * T:b * T + T]) for b in range(2)],
                          [scale if isinstance(scale, float) else scale[:, 2 * j + b:2 * j + b + 1] for b in range(2)],
                          [shift[:, 2 * j + b:2 * j + b + 1] for b in range(2)] if shift is not None else None)

            ps.wait_drained(act, "params")
            do(A(ctmp, prm[:, 0:8], ACT.Tanh, scale=0.5))
            raise_("c_tanh")
            act.wait_ge(ev("x_loaded"), 16)
            for t in range(TT):
                do(A(hT_sb[:, 0:D], x[:, t, :], ACT.Square, accum_out=ss[:, t:t + 1]))
            raise_("squares")
            def ada_row(n):
                drain(ps, f"ada{n}", lambda bank: [(mrow[n % 2], bank[:, :])])
            for n in ADA1:
                ada_row(n)
            ps.wait_drained(act, "adaT3")
            to_channels(ps, "h1", hT, modc[:, 8:16], modc[:, 0:8])
            act.wait_ge(ev("memory_loaded"), 16)
            act.wait_ge(ev("x_normed"), 1)
            for t in range(TT):
                do(A(ring_mem[:, 4 * 4096:4 * 4096 + D], mem_x[:, t, :], ACT.Square, accum_out=ss[:, t:t + 1]))
            raise_("squares")
            act.wait_ge(ev("pads_zeroed"), 1)
            for n in range(4):
                for j in (2 * n, 2 * n + 1):
                    if j < 7:
                        drain(ps, f"xb{j}", lambda bank: [(raw[:, 2 * j:2 * j + 2, 3:3 + T], v3(bank[:, :], 2))])
                act.wait_ge(ev("conv_batch"), n + 1)
                w = 4 if n < 3 else 2
                do(A(ce[:, 0:w, :], cv[:, 0:w, :], ACT.Tanh))
                raise_("conv_tanh")
            act.wait_ge(ev("dt_abs"), 1)
            do(A(flat(dta), flat(dta), ACT.Exp, scale=-1.0))
            do(A(flat(dta), flat(dta), ACT.Ln, bias=1.0))
            do(A(nega, alog_b, ACT.Exp))
            raise_("dt_log")
            to_channels(ps, "memT", memT, prm[:, ROWS["g_mem"]:ROWS["g_mem"] + 8], None)
            drain(ps, "u", lambda bank: [(uT[:, :, PAD:PAD + T], v3(bank[:, :], 2))])
            drain(ps, "z0", lambda bank: [(z[:, :, 0:256], v3(bank[:, :], 2))], [0.5])
            act.wait_ge(ev("decay_sums"), 1)
            do(A(dte, dte, ACT.Exp))
            do(A(eacs, acs[:, 1, :], ACT.Exp))
            raise_("decay_exps")

            def segment_exps(t):
                for g in range(GROUPS):
                    n = t * GROUPS + g
                    act.wait_ge(ev("segment_sums"), n + 1)
                    do(A(segs[n], segs[n], ACT.Exp))
                    raise_("segment_exps")
            segment_exps(0)
            for t in range(TT):
                drain(ps, f"z1t{t}", lambda bank: [(z[:, t, 256:768], bank[:, :])], [0.5])
            act.wait_ge(ev("conv_gated"), 4)
            for t in range(TT):
                if t:
                    segment_exps(1)
                for lo, hi in (((0, 4), (4, 8), (8, 10)) if t == 0 else ((0, 4), (4, 6))):
                    drain(ps, f"xs{t}_{lo}", lambda bank: [(xtok[:, t, lo * P:hi * P], bank[:, 0:(hi - lo) * P])])
            for t in range(TT):
                do(A(zt[t], z[:, t, :], ACT.Tanh))
            raise_("z_tanh")
            drain(ps, "pool", lambda bank: [(mixT[:, b, :], bank[:, b * T:b * T + T]) for b in range(2)],
                  [prm[:, ROWS["pool_scale"] + b:ROWS["pool_scale"] + b + 1] for b in range(2)])
            for step in BESIDE:
                for what, n, *t in step:
                    if what == "ada":
                        ada_row(n)
                    elif what == "mv":
                        lo, w = ((0, 256), (256, 512), (768, 256))[n]
                        drain(ps, f"mv{n}{t[0]}", lambda bank: [(vm[:, t[0], lo:lo + w], bank[:, 0:w])])
            for j in range(3):
                drain(ps, f"yT{j}", lambda bank: [(mixT[:, 2 + 2 * j + b, :], bank[:, b * T:b * T + T]) for b in range(2)],
                      [prm[:, ROWS["ssd_norm_w"] + 2 * j + b:ROWS["ssd_norm_w"] + 2 * j + b + 1] for b in range(2)])
            for t in range(TT):
                act.wait_ge(ev("x_updated"), 0 + t + 1)
                do(A(hT_sb[:, 0:D], x[:, t, :], ACT.Square, accum_out=ss[:, t:t + 1]))
            raise_("squares")
            to_channels(ps, "h2", hT, modc[:, 32:40], modc[:, 24:32])
            act.wait_ge(ev("group_shifted"), 1)
            do(A(flat(gtm), flat(gtm), ACT.Exp))
            raise_("group_exps")
            act.wait_ge(ev("top_gap"), 1)
            do(A(e2, v2, ACT.Exp))
            raise_("top_exp")

            act.wait_ge(ev("routed"), 1)
            pairs = act.value_load(meta[0:1, P:P + 1], min_val=4, max_val=MAXB // 2)
            last_pair = act.value_load(meta[0:1, P + 1:P + 2], min_val=3, max_val=MAXB // 2 - 1)
            gA, gB, hA, hB, tA, tB, oA, oB = banks
            PER = 8

            def slots_in(i, lc):
                act.wait_ge(ev("gather_filled"), i * 2 + 1)
                for k in range(4):
                    ins = A(xeT[:, k, :], gA[:, k * P:k * P + P], ACT.Identity, scale=modc[:, 32 + k:33 + k],
                            bias=modc[:, 24 + k:25 + k])
                    if k < 3:
                        lc(ins)
                ins.then_inc(ev("slots_in_by_act"), 1)

            def hidden_out(i, b):
                act.wait_ge(ev("hidden_filled"), i * 4 + (2 * b + 1))
                A(hs[:, 0:512], hA[:, :], ACT.Identity).then_inc(ev("hidden_out_by_act"), 1)

            def gate_tanh(i, b, lc):
                act.wait_ge(ev("folded"), i * 4 + (2 * b + 1))
                A(ge, v3(tA[:, :], 4)[:, :, 0:SLOTS], ACT.Tanh, scale=0.5).then_inc(ev("gate_tanhs"), 1)

            def rows_out(m):
                act.wait_ge(ev("rows_filled_for_act"), m + 1)
                act.wait_ge(ev("parts_filled"), m * 4 + 1)
                A(osb[:, 0:512], oA[:, :], ACT.Identity).then_inc(ev("rows_out_by_act"), 1)

            def turn(i, lc, first):
                hidden_out(i, 0)
                if not first:
                    rows_out(i - 1)
                gate_tanh(i, 0, lc)
                hidden_out(i, 1)
                slots_in(i + 1, lc)
                gate_tanh(i, 1, lc)

            lead = Chained(act, ev("act_lead_step"))
            drain(ps, "gate_rows", lambda bank: [(gate_rows, bank[:, :])])
            drain(ps, "mkT", lambda bank: [(flat(kmT), bank[:, :])])
            slots_in(0, lead)
            turn(0, lead, True)
            with act.Fori(1, pairs) as i:
                lc = LoopChained(act, ev("act_expert_step"), i, 3)
                turn(i, lc, False)
                lc.end()
            rows_out(last_pair)

            for t in range(TT):
                act.wait_ge(ev("x_updated"), 2 + t + 1)
                do(A(hT_sb[:, 0:D], x[:, t, :], ACT.Square, accum_out=ss[:, t:t + 1]))
            raise_("squares")
            for t in range(TT):
                act.wait_ge(ev("x_updated"), 4 + t + 1)
                do(A(hT_sb[:, 0:D], x[:, t, :], ACT.Square, accum_out=ss[:, t:t + 1]))
            raise_("squares")
            to_channels(ps2, "h3", hT, prm[:, ROWS["g_mix"]:ROWS["g_mix"] + 8], None)
            act.wait_ge(ev("angles_ready"), 1)
            do(A(flat(sinv), flat(ang), ACT.Sin))
            do(A(flat(cosv), flat(rn), ACT.Sin))
            raise_("rope_tables")
            def gate_tanhs(name, buf, cols=None):
                act.wait_ge(ev(f"gate_logits_{name}"), 1)
                for t in range(TT):
                    v_ = buf[:, t, :] if cols is None else buf[:, t, cols]
                    do(A(v_, v_, ACT.Tanh, scale=0.5))
                raise_(f"gate_tanhs_{name}")
            gate_tanhs("2", gates2)
            drain(ps2, "mqT", lambda bank: [(flat(qmT), bank[:, :])])

            def attention(heads, first, scale, causal, fill=()):
                for h in range(heads + 2):
                    if h < len(fill):
                        fill[h]()
                    if h >= 2:
                        w = 3 * P if causal else 4 * P
                        drain(ps2, f"pT_{first + h - 2}", lambda bank: [(pT[(first + h - 2) % 2][:, 0:w], bank[:, 0:w])])
                    if h < heads:
                        n = first + h
                        act.wait_ge(ev("scores_maxed"), n + 1)
                        for t in range(TT):
                            at, w = ((0, P), (P, T))[t] if causal else (t * T, T)
                            v_ = pr[n % 3][:, at:at + w]
                            do(A(v_, v_, ACT.Exp, bias=mxs[n % 3][:, t:t + 1], scale=scale,
                                 accum_out=sums[n % 3][:, t:t + 1]))
                        raise_("probs_ready")

            def gla_channels(nm, dst, b, scale):
                drain(ps2, f"{nm}{b}", lambda bank: [(flat(dst)[:, b * 512:b * 512 + 512], bank[:, :])], [scale])
            attention(EH, 0, EQ ** -0.5, False,
                      [lambda nm=nm, dst=dst, b=b, s_=s_: gla_channels(nm, dst, b, s_)
                       for nm, dst, s_ in (("gq", gqT, DK ** -0.5), ("gk", gkT, 1.0)) for b in range(2)])
            drain(ps2, "ga", lambda bank: [(gaT[0:GRANK, :], bank[0:GRANK, 0:T])])
            for n in range(2):
                for t in range(TT):
                    drain(ps2, f"gv{n}t{t}", lambda bank: [(gv[:, t, n * 512:n * 512 + 512], bank[:, :])])
            act.wait_ge(ev("log_arg"), 1)
            do(A(flat(lt), flat(lt), ACT.Exp, scale=-1.0))
            do(A(flat(lt), flat(lt), ACT.Ln, bias=1.0))
            raise_("log_done")
            def fill_drains(lvl):
                for nm, n, t in FILLS[lvl]:
                    if nm == "gr":
                        drain(ps2, f"gr{n}t{t}", lambda bank: [(gr[:, t, n * 512:n * 512 + 512], bank[:, :])], [0.5])
                    elif nm == "q":
                        drain(ps2, f"q{n}t{t}", lambda bank: [(q[t][:, n * 512:n * 512 + 512], bank[:, :])])
                    else:
                        drain(ps2, f"ckv0t{t}", lambda bank: [(ckv[t][:, 0, :], bank[:, 0:KVR + ROPE])])
            act.wait_ge(ev("gate_2_added"), 1)
            fill_drains(0)
            for j in range(2):
                drain(ps2, f"cum{j}", lambda bank: [(flat(gbT)[:, j * 512:j * 512 + 512], bank[:, :])])
            for lvl in range(1, LEVELS + 2):
                act.wait_ge(ev("level_differences"), lvl)
                do(A(flat(lev), flat(lev), ACT.Exp))
                raise_("level_exps")
                fill_drains(lvl)
            raise_("latents_out")
            for t, e_ in enumerate((flat(la), flat(lt))):
                do(A(e_, gr[:, t, :], ACT.Tanh))
            raise_("r_tanh")
            drain(ps2, "cross", lambda bank: [(flat(att[2]), bank[:, :])])
            act.wait_ge(ev("gla_summed"), 1)
            for t, sq_ in enumerate((gqT, gkT)):
                do(A(flat(sq_), obr[:, t, :], ACT.Square))
            raise_("gla_squares")
            gate_tanhs("1", gates1)
            act.wait_ge(ev("gla_done"), 1)
            for t in range(TT):
                do(A(qsqs[t], q[t], ACT.Square))
            raise_("q_squares")
            drain(ps2, "ckT", lambda bank: [(ckT[:, b, :], bank[:, b * T:b * T + T]) for b in range(2)],
                  [prm[:, ROWS["g_ckv"] + b:ROWS["g_ckv"] + b + 1] for b in range(2)])
            for n in range(4):
                for t in range(TT):
                    drain(ps2, f"kv{n}t{t}", lambda bank: [(kv[:, t, n * 512:n * 512 + 512], bank[:, :])])
            for t in range(TT):
                do(A(v3(ksqs[t], MH), v3(kv[:, t, :], MH)[:, :, 0:NOPE], ACT.Square))
            raise_("k_squares")
            gate_tanhs("0a", gates0, slice(0, 512))
            drain(ps2, "krT", lambda bank: [(krT, bank[:, 0:T])])
            for j in range(4):
                drain(ps2, f"qnT{j}", lambda bank: [(flat(qnT)[:, j * 512:j * 512 + 512], bank[:, :])],
                      [prm[:, ROWS["g_q_nope"]:ROWS["g_q_nope"] + 1]])
            for j in range(2):
                drain(ps2, f"qrT{j}", lambda bank: [(flat(qrT)[:, j * 512:j * 512 + 512], bank[:, :])])
            for j in range(4):
                drain(ps2, f"knT{j}", lambda bank: [(flat(knT)[:, j * 512:j * 512 + 512], bank[:, :])],
                      [prm[:, ROWS["g_k_nope"]:ROWS["g_k_nope"] + 1]])
            attention(MH, EH, (NOPE + ROPE) ** -0.5, True)
            gate_tanhs("0b", gates0, slice(512, 1024))
            to_channels(ps2, "ysT", hT, 0.5, None)
            def high_part(n):
                k = FFN_LOAD + n
                act.wait_ge(ring2.landed[k % 4], 16 * (k // 4 + 1))
                if n >= 2:
                    ring2.wait_used(act, k - 2)
                do(A(high_slots[n % 2], slots[k % 4], ACT.Identity))
                raise_("high_parts")
            high_part(0)
            high_part(1)
            for t in range(TT):
                act.wait_ge(ev("x_updated"), 6 + t + 1)
                do(A(flat(ysum)[:, 0:D], x[:, t, :], ACT.Square, accum_out=ss[:, t:t + 1]))
            raise_("squares")
            to_channels(ps2, "h4", hT, prm[:, ROWS["g_ffn"]:ROWS["g_ffn"] + 8], None)
            for j in (0, 2):
                ps2.wait_drained(act, f"h4{j}")
            do(A(flat(hH), hT_sb[:, :], ACT.Identity))
            raise_("ffn_input_high")
            for n in range(8):
                for b in range(2):
                    m = 2 * n + b
                    if m >= 2:
                        act.wait_ge(ev("ffn_squared"), m - 1)
                    bank = ps2.read(act, f"up{n}{b}", "act")
                    ps2.release(f"up{n}{b}", A(relu[b], bank[:, :], ACT.Relu), act)
                    do(A(flat(aH[n])[:, b * 512:b * 512 + 512], relu[b], ACT.Square))
                    raise_("ffn_high")
                high_part(n + 2)
            for n in range(10, 16):
                high_part(n)
        @block.vector
        def _(dve):
            do = Chained(dve, ev("dve_step"))
            spread = Signal(ev("columns_spread"))
            V = nc.vector

            def raise_(name):
                dve.sem_inc(ev(name), 1)

            def ts(out_, in_, s1, op0, s2=None, op1=ALU.bypass):
                return V.tensor_scalar(out_, in_, s1, s2, op0, op1)

            def tt(out_, x_, y_, op):
                return V.tensor_tensor(out_, x_, y_, op)

            def stt(out_, x_, s_, y_, op0, op1):
                return V.scalar_tensor_tensor(out_, x_, s_, y_, op0, op1)

            def rsqrt(dst, n, sums_, width):
                v, w = rt[0][:, 0:n], rt[1][:, 0:n]
                at = 0
                for m, wd in (width if isinstance(width, list) else [(n, width)]):
                    do(ts(v[:, at:at + m], sums_[:, at:at + m], 1.0 / wd, ALU.mult, EPS, ALU.add))
                    at += m
                do(ts(w.bitcast(I32), v.bitcast(I32), 1, ALU.logical_shift_right))
                do(ts(dst.bitcast(I32), w.bitcast(I32), -1.0, ALU.mult, 1597463007.0, ALU.add))
                for _ in range(3):
                    do(tt(w, dst, dst, ALU.mult))
                    do(stt(w, w, -0.5, v, ALU.mult, ALU.mult))
                    do(stt(dst, w, 1.5, dst, ALU.add, ALU.mult))

            def times_sigmoid(dst, tanh_half, y_):
                do(stt(dst, tanh_half, 1.0, y_, ALU.add, ALU.mult))

            def to_channels(ps, name, dst, scale, shift):
                for j in (0, 2):
                    bank = ps.read(dve, f"{name}{j}", "dve")
                    for b in range(2):
                        c = 2 * j + b
                        o_, i_ = dst[:, c, :], bank[:, b * T:b * T + T]
                        if shift is not None:
                            ins = ts(o_, i_, scale[:, c:c + 1], ALU.mult, shift[:, c:c + 1], ALU.add)
                        elif scale is not None:
                            ins = ts(o_, i_, scale if isinstance(scale, float) else scale[:, c:c + 1], ALU.mult)
                        else:
                            ins = V.tensor_copy(o_, i_)
                        if b:
                            ps.release(f"{name}{j}", ins, dve)
                        else:
                            do(ins)

            norm_no = [0]

            def normalize(dst, src):
                norm_no[0] += 1
                dve.wait_ge(ev("squares"), norm_no[0])
                rsqrt(rs[:, 0:TT], TT, ss, D)
                for t in range(TT):
                    do(ts(dst[:, t, :], src[:, t, :], rs[:, t:t + 1], ALU.mult))

            bank = ps.read(dve, "params", "dve")
            ps.release("params", V.tensor_copy(prm[:, :], bank[:, 0:NROWS + 48]), dve)
            do(ts(cs, prm[:, 0:8], 0.5, ALU.mult))
            dve.wait_ge(ev("c_tanh"), 1)
            times_sigmoid(cs, ctmp, cs)
            raise_("c_gated")
            halved = prm[:, ROWS["conv_w"]:ROWS["conv_b"] + NXB]
            do(ts(halved, halved, 0.5, ALU.mult))
            normalize(xn, x)
            raise_("x_normed")

            def ada_place(n):
                bank = ps.read(dve, f"adaT{n}", "dve")
                part, half = n // 2, n % 2
                if part in (2, 5):
                    rows = (g1b if part == 2 else g2b)[:, half * 512:half * 512 + 512]
                    if n == 4:
                        dve.wait_ge(ev("gate_rows_loaded"), 32)
                    ins = tt(rows, bank[:, :], rows, ALU.add)
                else:
                    ins = stt(modc[:, 4 * n:4 * n + 4], bank[:, 0:4], 1.0 if part in (1, 4) else 0.0,
                              prm[:, BADA + 4 * n:BADA + 4 * n + 4], ALU.add, ALU.add)
                ps.release(f"adaT{n}", ins, dve)
            for n in ADA1:
                ada_place(n)
            to_channels(ps, "h1", hT, modc[:, 8:16], modc[:, 0:8])
            normalize(mem_x, mem_x)
            raise_("mem_normed")
            for n in range(4):
                blocks = range(4 * n, min(4 * n + 4, NXB))
                for k in blocks:
                    if k % 2 == 0:
                        ps.wait_drained(dve, f"xb{k // 2}")
                    dst = cv[:, k - 4 * n, :]
                    w = [prm[:, ROWS["conv_w"] + j * NXB + k:ROWS["conv_w"] + j * NXB + k + 1] for j in range(CONV)]
                    bias = prm[:, ROWS["conv_b"] + k:ROWS["conv_b"] + k + 1]
                    do(ts(dst, raw[:, k, 3:3 + T], w[3], ALU.mult, bias, ALU.add))
                    for j in range(3):
                        do(stt(dst, raw[:, k, j:j + T], w[j], dst, ALU.mult, ALU.add))
                raise_("conv_batch")
                dve.wait_ge(ev("conv_tanh"), n + 1)
                m = len(blocks)
                times_sigmoid(xb[:, 4 * n:4 * n + m, :], ce[:, 0:m, :], cv[:, 0:m, :])
                raise_("conv_gated")
            bank = ps.read(dve, "dt", "dve")
            dve.wait_ge(ev("head_rows_loaded"), 48)
            ps.release("dt", tt(dtr, v3(bank[:, 0:TT * HEADS], TT), over(dt_b, TT, 1), ALU.add), dve)
            do(stt(flat(dta), flat(dtr), -1.0, flat(dtr), ALU.mult, ALU.max))
            raise_("dt_abs")
            dve.wait_ge(ev("dt_log"), 1)
            do(ts(dtv, dtr, 0.0, ALU.max))
            do(tt(dtv, dtv, dta, ALU.add))
            do(ts(nega, nega, -1.0, ALU.mult))
            do(tt(dta, dtv, over(nega, TT, 1), ALU.mult))
            raise_("decay_steps")
            to_channels(ps, "memT", memT, prm[:, ROWS["g_mem"]:ROWS["g_mem"] + 8], None)
            bank = ps.read(dve, "acs", "dve")
            ps.release("acs", V.tensor_copy(flat(acs), bank[:, 0:3 * HEADS]), dve)
            do(tt(dte, acs[:, 2, :], acs[:, 0, :], ALU.subtract))
            raise_("decay_sums")

            def segment_sums(t):
                for g in range(GROUPS):
                    bank = ps.read(dve, f"row{t}{g}", "dve")
                    for r in range(RPG):
                        h = RPG * g + r
                        ins = stt(segs[t * GROUPS + g][:, r, :], bank[:, r * P:r * P + P], acs[:, t, h:h + 1],
                                  C["seg_mask"], ALU.subtract, ALU.add)
                        if r < RPG - 1:
                            do(ins)
                    ps.release(f"row{t}{g}", ins, dve)
                    raise_("segment_sums")
            segment_sums(0)
            ps.wait_drained(dve, "u")
            dve.wait_ge(ev("pool_table_loaded"), 16)

            def widen(dst, src, by, blocks):
                do(tt(dst[:, blocks, PAD:PAD + T], src[:, blocks, PAD:PAD + T], src[:, blocks, PAD - by:PAD - by + T],
                      ALU.add))

            def group_mean(g, src):
                p0, b = 64 * (g % 2), g // 2
                do(tt(diff[p0:p0 + 64, b, :], src[p0:p0 + 64, b, PAD:PAD + T], prc[p0:p0 + 64, b, :], ALU.mult))
            both, last_ = slice(0, 2), slice(1, 2)
            widen(sA, uT, 1, both)
            group_mean(0, sA)
            widen(sB, sA, 2, both)
            group_mean(1, sB)
            widen(sA, sB, 4, last_)
            group_mean(2, sA)
            widen(sB, sA, 8, last_)
            group_mean(3, sB)
            do(tt(diff, diff, uT[:, :, PAD:PAD + T], ALU.subtract))
            raise_("pooled")
            segment_sums(1)
            ps.wait_drained(dve, "xs1_4")
            dve.wait_ge(ev("decay_exps"), 1)

            def heads(v, n=HD):
                return v.rearrange("p (h c) -> p h c", c=n)
            for t in range(TT):
                do(tt(heads(xdt[:, t, :]), heads(xtok[:, t, 0:SSD_W]), over(dtv[:, t, :], HD, 2), ALU.mult))
            do(tt(heads(xcd), heads(xdt[:, 0, :]), over(dte, HD, 2), ALU.mult))
            raise_("xcd_ready")
            for t in range(TT):
                do(tt(heads(yv[:, t, :]), heads(xtok[:, t, 0:SSD_W]), over(dskip_b, HD, 2), ALU.mult))
            GW = RPG * HD
            for g in range(GROUPS):
                bank = ps.read(dve, f"state{g}", "dve")
                ps.release(f"state{g}", V.tensor_copy(prevT[:, g, :], bank[:, 0:GW]), dve)

            def decayed_products(n):
                dve.wait_ge(ev("segment_exps"), n + 1)
                bank = ps.read(dve, f"cb{n}", "dve")
                ps.release(f"cb{n}", tt(seg2[n % 2], segs[n], over(bank[:, 0:P], RPG, 1), ALU.mult), dve)

            def beside(step):
                for what, n, *t in BESIDE[step]:
                    if what == "adaT":
                        ada_place(n)
                    elif what == "mk":
                        bank = ps.read(dve, f"mk{n}", "dve")
                        ps.release(f"mk{n}", V.tensor_copy(mk[:, n * EH * EQ:(n + 1) * EH * EQ], bank[:, 0:256]), dve)
            sq = ce_f[:, 0:SSD_W]

            def gate_tile(t):
                do(tt(yv[:, t, :], yv[:, t, :], z[:, t, :], ALU.mult))
                do(tt(sq, yv[:, t, :], yv[:, t, :], ALU.mult))
                do(V.tensor_reduce(gss[:, t * GROUPS:(t + 1) * GROUPS], v3(sq, GROUPS), AX.X, ALU.add))
            decayed_products(0)
            for n in range(TT * GROUPS):
                t, g = divmod(n, GROUPS)
                if n + 1 < TT * GROUPS:
                    decayed_products(n + 1)
                beside(n)
                dst = yv[:, t, g * GW:g * GW + GW]
                bank = ps.read(dve, f"yd{n}", "dve")
                ps.release(f"yd{n}", tt(dst, bank[:, 0:GW], dst, ALU.add), dve)
                if n == 1:
                    dve.wait_ge(ev("z_tanh"), 1)
                    for t_ in range(TT):
                        times_sigmoid(z[:, t_, :], zt[t_], z[:, t_, :])
                if n == GROUPS:
                    gate_tile(0)
                if t:
                    bank = ps.read(dve, f"yo{g}", "dve")
                    ps.release(f"yo{g}", tt(heads(ybuf), heads(bank[:, 0:GW]),
                                            over(eacs[:, RPG * g:RPG * g + RPG], HD, 2), ALU.mult), dve)
                    do(tt(dst, dst, ybuf, ALU.add))
            gate_tile(1)
            rsqrt(rs[:, 0:TT * GROUPS], TT * GROUPS, gss, GW)
            for t in range(TT):
                yh = heads(yv[:, t, :], GW)
                do(tt(yh, yh, over(rs[:, t * GROUPS:(t + 1) * GROUPS], GW, 2), ALU.mult))
            raise_("ssd_normed")

            def add_gated(ps, names, gate_rows, buf):
                for n in range(2):
                    for t in range(TT):
                        bank = ps.read(dve, f"{names}{n}t{t}", "dve")
                        cols = slice(n * 512, n * 512 + 512)
                        ps.release(f"{names}{n}t{t}", tt(buf[:, 0:512], bank[:, :], gate_rows[:, cols], ALU.mult), dve)
                        do(tt(x[:, t, cols], x[:, t, cols], buf[:, 0:512], ALU.add))
                        if n:
                            raise_("x_updated")
            add_gated(ps, "mix", g1b, cv_f)
            def head_norm(src, n, width, gain, sq_, t=None):
                do(tt(sq_, src, src, ALU.mult))
                do(V.tensor_reduce(hss[:, 0:n], sq_, AX.X, ALU.add))
                rsqrt(rs[:, 0:n], n, hss[:, 0:n], width)
                do(tt(src, src, over(rs[:, 0:n], width, 2), ALU.mult))
                if gain is not None:
                    do(tt(src, src, over(gain, n, 1), ALU.mult))
            normalize(xn, x)
            raise_("x_normed")
            to_channels(ps, "h2", hT, modc[:, 32:40], modc[:, 24:32])
            dve.wait_ge(ev("router_loaded"), 32)
            dve.wait_ge(ev("router_rows_loaded"), 32)
            for t in range(TT):
                bank = ps.read(dve, f"routert{t}", "dve")
                ps.release(f"routert{t}", tt(lg[:, t, :], bank[:, 0:EG + NE], rb, ALU.add), dve)

            def first_max(one_hot, values, top, rev, tmp):
                n = values.shape[2]
                do(V.tensor_reduce(top, values, AX.X, ALU.max))
                do(tt(tmp, values, over(top, n, 2), ALU.is_equal))
                do(tt(tmp, tmp, over(rev, TT, 1), ALU.mult))
                do(V.tensor_reduce(gsm, tmp, AX.X, ALU.max))
                do(tt(one_hot, over(gsm, n, 2), over(rev, TT, 1), ALU.is_equal))
            glog = lg[:, :, 0:EG]
            first_max(ohg, glog, gm, C["rev4"], gtm)
            do(tt(gtm, glog, over(gm, EG, 2), ALU.subtract))
            raise_("group_shifted")
            dve.wait_ge(ev("group_exps"), 1)
            do(V.tensor_reduce(gsm, gtm, AX.X, ALU.add))
            do(V.reciprocal(pg, gsm))
            w4 = wide.rearrange("p (t g e) -> p t g e", t=TT, g=EG)
            for t in range(TT):
                do(tt(w4[:, t], lg[:, t, EG:].rearrange("p (g e) -> p g e", g=EG), over(ohg[:, t, :], EPG, 2), ALU.mult))
                do(V.tensor_reduce(w8[:, t, :], w4[:, t].rearrange("p g e -> p e g"), AX.X, ALU.add))
            first_max(oh1, w8, v1, C["rev8"], t8)
            do(stt(w8, oh1, BIG, w8, ALU.mult, ALU.add))
            first_max(oh2, w8, v2, C["rev8"], t8)
            do(tt(v2, v2, v1, ALU.subtract))
            raise_("top_gap")
            dve.wait_ge(ev("top_exp"), 1)
            do(ts(v1, e2, 1.0, ALU.add))
            do(V.reciprocal(v1, v1))
            do(tt(gate1, pg, v1, ALU.mult))
            do(tt(gate2, gate1, e2, ALU.mult))
            for s_, oh in ((sel1, oh1), (sel2, oh2)):
                for t in range(TT):
                    do(tt(s_[:, t, :].rearrange("p (g e) -> p g e", g=EG), over(ohg[:, t, :], EPG, 2),
                          over(oh[:, t, :], EG, 1), ALU.mult))
            do(tt(sel, sel1, sel2, ALU.add))
            do(V.memset(cumA, 0.0))
            do(V.memset(cumB, 0.0))
            raise_("chosen")
            bank = ps.read(dve, "rank", "dve")
            do(V.tensor_copy(flat(slot_of), bank[:, 0:2 * NE]))
            ps.release("rank", V.tensor_copy(cnt, bank[:, 2 * NE:3 * NE]), dve)
            do(ts(nblk, cnt, 0.0, ALU.is_gt))
            for m in range(1, T // SLOTS):
                do(stt(nblk, cnt, float(m * SLOTS), nblk, ALU.is_gt, ALU.add))
            do(ts(nblk[:, 0:1], nblk[:, 0:1], 1.0, ALU.max))
            do(V.tensor_copy(cumA[:, NE:], nblk))
            cum = [cumA, cumB]
            for m in range(5):
                s_, d_ = cum[m % 2], cum[(m + 1) % 2]
                do(tt(d_[:, NE:], s_[:, NE:], s_[:, NE - 2 ** m:2 * NE - 2 ** m], ALU.add))
            ends = cumB[:, NE:]
            do(ts(wide[:, 0:NE], ends, C["row_id"], ALU.is_le))
            do(V.tensor_reduce(be, wide[:, 0:NE], AX.X, ALU.add))
            do(ts(be, be, float(NE - 1), ALU.min))
            raise_("block_experts")
            do(tt(cnt, ends, nblk, ALU.subtract))
            do(ts(cnt, cnt, float(SLOTS), ALU.mult))
            do(tt(slot_of, slot_of, over(cnt, TT, 1), ALU.add))
            for s_, dst in ((sel1, dest[0]), (sel2, dest[1])):
                do(tt(v3(wide, TT), s_, slot_of, ALU.mult))
                do(V.tensor_reduce(dst, v3(wide, TT), AX.X, ALU.add))
            do(ts(npf, ends[:, NE - 1:NE], 0.5, ALU.mult, 0.25, ALU.add))
            do(V.tensor_copy(meta[0:1, P:P + 1], npf[0:1, :]))
            do(ts(npf, npf, -1.0, ALU.add))
            do(V.tensor_copy(meta[0:1, P + 1:P + 2], npf[0:1, :]))
            do(V.tensor_copy(slot_id, C["iota"]))
            bank = ps.read(dve, "experts", "dve")
            ps.release("experts", V.tensor_copy(meta[0:1, 0:P], bank[0:1, 0:P]), dve)
            raise_("routed")

            pairs = dve.value_load(meta[0:1, P:P + 1], min_val=4, max_val=MAXB // 2)
            last_pair = dve.value_load(meta[0:1, P + 1:P + 2], min_val=3, max_val=MAXB // 2 - 1)
            gA, gB, hA, hB, tA, tB, oA, oB = banks

            def choose_slots(i, lc):
                if i is not None:
                    dve.wait_ge(ev("gather_filled"), i * 2)
                for t in range(TT):
                    lc(ts(pick[:, t, :], slot_id, dest[0][:, t:t + 1], ALU.is_equal))
                    ins = stt(pick[:, t, :], slot_id, dest[1][:, t:t + 1], pick[:, t, :], ALU.is_equal, ALU.add)
                    lc(ins)
                lc(ts(slot_id, slot_id, float(P), ALU.add))
                dve.sem_inc(ev("slots_picked"), 1)

            def slots_in(i, lc):
                dve.wait_ge(ev("gather_filled"), i * 2 + 2)
                for k in range(4, 8):
                    ins = ts(xeT[:, k, :], gB[:, (k - 4) * P:(k - 4) * P + P], modc[:, 32 + k:33 + k], ALU.mult,
                             modc[:, 24 + k:25 + k], ALU.add)
                    if k < 7:
                        lc(ins)
                ins.then_inc(ev("slots_in_by_dve"), 1)

            def hidden_out(i, b):
                dve.wait_ge(ev("hidden_filled"), i * 4 + (2 * b + 2))
                V.tensor_copy(hs[:, 512:1024], hB[:, :]).then_inc(ev("hidden_out_by_dve"), 1)

            def gate(i, b, lc):
                dve.wait_ge(ev("gate_tanhs"), i * 2 + (b + 1))
                lc(stt(gt, ge, 1.0, v3(tA[:, :], 4)[:, :, 0:SLOTS], ALU.add, ALU.mult))
                dve.wait_ge(ev("folded"), i * 4 + (2 * b + 2))
                stt(sT[b], gt, 0.5, v3(tB[:, :], 4)[:, :, 0:SLOTS], ALU.mult, ALU.mult).then_inc(ev("hidden_gated"), 1)

            def rows_out(m):
                dve.wait_ge(ev("rows_filled_for_dve"), m + 1)
                dve.wait_ge(ev("parts_filled"), m * 4 + 1)
                V.tensor_copy(osb[:, 512:1024], oB[:, :]).then_inc(ev("rows_out_by_dve"), 1)

            def shares(lc):
                lc(stt(share_f, slot_rows, slot_col, gate_rows, ALU.is_equal, ALU.mult))
                lc(ts(slot_col, slot_col, float(P), ALU.add))
                tt(share_f[:, 0:T], share_f[:, 0:T], share_f[:, T:2 * T], ALU.add).then_inc(ev("shares_ready"), 1)

            def add_parts(m, t):
                if t == 0:
                    dve.wait_ge(ev("parts_added"), m * 4 + 1)
                for n_, src in enumerate((oA, oB)):
                    dve.wait_ge(ev("parts_filled"), m * 4 + (2 * t + n_ + 2))
                    dst = acc[:, t, n_ * 512:n_ * 512 + 512]
                    tt(dst, src[:, :], dst, ALU.add).then_inc(ev("parts_added"), 1)

            def turn(i, lc, first):
                hidden_out(i, 0)
                if not first:
                    rows_out(i - 1)
                    shares(lc)
                choose_slots(i + 1, lc)
                gate(i, 0, lc)
                hidden_out(i, 1)
                if not first:
                    add_parts(i - 1, 0)
                slots_in(i + 1, lc)
                gate(i, 1, lc)
                if not first:
                    add_parts(i - 1, 1)
            lead = Chained(dve, ev("dve_lead_step"))
            dve.sem_inc(ev("parts_added"), 1)
            choose_slots(None, lead)
            for n, col in enumerate([c_[:, t:t + 1] for c_ in (dest[0], dest[1], gate1, gate2) for t in range(TT)]):
                do(ts(diag[:, n, :], ident, col, ALU.mult), spread)
            do(V.tensor_copy(slot_col, C["row_id"]))
            dve.wait_ge(ev("norm_rows_loaded"), 96)
            G_QR, G_KR, G_QM, G_KM = (rows2[:, 256 + 64 * n:320 + 64 * n] for n in range(4))
            head_norm(heads(mk, EQ), TT * EH, EQ, G_KM, heads(msq, EQ))
            raise_("mem_keys_normed")
            bank = ps.read(dve, "slot_rows", "dve")
            ps.release("slot_rows", V.tensor_copy(slot_rows, bank[:, :]), dve)
            ps.wait_drained(dve, "gate_rows")
            do(V.memset(acc_f, 0.0))
            slots_in(0, lead)
            turn(0, lead, True)
            with dve.Fori(1, pairs) as i:
                lc = LoopChained(dve, ev("dve_expert_step"), i, 5 + 2 + 1 + 3 + 1)
                turn(i, lc, False)
                lc.end()
            rows_out(last_pair)
            shares(lead)
            add_parts(last_pair, 0)
            add_parts(last_pair, 1)

            dve.wait_ge(ev("parts_added"), pairs * 4 + 1)
            for t in range(TT):
                do(tt(acc[:, t, :], acc[:, t, :], g2b[:, :], ALU.mult))
                do(tt(x[:, t, :], x[:, t, :], acc[:, t, :], ALU.add))
                raise_("x_updated")
            dve.wait_ge(ev("final_rows_loaded"), 16)
            norm_no[0] += 1
            dve.wait_ge(ev("squares"), norm_no[0])
            rsqrt(rs[:, 0:TT], TT, ss, D)
            for t in range(TT):
                do(stt(x[:, t, :], x[:, t, :], rs[:, t:t + 1], fnw[:, :], ALU.mult, ALU.mult))
                raise_("x_updated")

            normalize(xn, x)
            raise_("x_normed")
            to_channels(ps2, "h3", hT, prm[:, ROWS["g_mix"]:ROWS["g_mix"] + 8], None)
            dve.wait_ge(ev("positions_loaded"), 16)
            do(V.tensor_copy(pos_f, pos_i))
            do(tt(ang, over(C["inv"], TT, 1), over(pos_f, NI, 2), ALU.mult))
            ROUND = float(1.5 * 2 ** 23)
            do(ts(rn, ang, float(1.0 / (2 * np.pi)), ALU.mult, ROUND, ALU.add))
            do(ts(rn, rn, -ROUND, ALU.add))
            c1 = 6.28125
            c2 = float(np.float32(np.floor((2 * np.pi - c1) * 2 ** 22) / 2 ** 22))
            c3 = float(2 * np.pi - c1 - c2)
            for c_ in (c1, c2, c3):
                do(stt(ang, rn, -c_, ang, ALU.mult, ALU.add))
            PI_ = 3.1415925
            do(ts(rn, ang, float(np.pi / 2), ALU.add))
            do(ts(sinv, rn, float(np.pi), ALU.is_gt))
            do(stt(rn, sinv, -float(2 * np.pi), rn, ALU.mult, ALU.add))
            do(ts(rn, rn, -PI_, ALU.max, PI_, ALU.min))
            do(ts(ang, ang, -PI_, ALU.max, PI_, ALU.min))
            raise_("angles_ready")
            dve.wait_ge(ev("rope_tables"), 1)

            for t in range(TT):
                bank = ps2.read(dve, f"mqt{t}", "dve")
                ps2.release(f"mqt{t}", V.tensor_copy(qm[:, t, :], bank[:, 0:256]), dve)
            head_norm(heads(flat(qm), EQ), TT * EH, EQ, G_QM, heads(flat(qsq), EQ))
            raise_("mem_q_normed")

            def gate_logits(br, name, buf, rows, halves=(0, 1)):
                dve.wait_ge(ev(f"gate_bias_loaded_{br}"), 16)
                for n in halves:
                    for t in range(TT):
                        cols = slice(n * 512, n * 512 + 512)
                        bank = ps2.read(dve, f"gate{br}{n}t{t}", "dve")
                        ps2.release(f"gate{br}{n}t{t}", tt(buf[:, t, cols], bank[:, :], rows[:, cols], ALU.add), dve)
                raise_(f"gate_logits_{name}")

            def add_gated_branch(buf, first=False):
                for t in range(TT):
                    if first:
                        times_sigmoid(ysum[:, t, :], buf[:, t, :], obr[:, t, :])
                    else:
                        times_sigmoid(buf[:, t, :], buf[:, t, :], obr[:, t, :])
                        do(tt(ysum[:, t, :], ysum[:, t, :], buf[:, t, :], ALU.add))
            gate_logits(2, "2", gates2, g1b)

            def attention(n_heads, first, scale, causal, width):
                for h in range(n_heads + 2):
                    if h < n_heads:
                        n = first + h
                        bank = ps2.read(dve, f"s_{n}", "dve")
                        if n >= 3:
                            ps2.wait_filled(dve, f"pT_{n - 3}")
                        if causal:
                            ps2.release(f"s_{n}", tt(pr[n % 3][:, 0:3 * P], bank[:, 0:3 * P], C["causal"], ALU.add), dve)
                            do(V.tensor_reduce(mxs[n % 3][:, 0:1], pr[n % 3][:, 0:P], AX.X, ALU.max))
                            do(V.tensor_reduce(mxs[n % 3][:, 1:2], pr[n % 3][:, P:3 * P], AX.X, ALU.max))
                        else:
                            ps2.release(f"s_{n}", V.tensor_copy(pr[n % 3], bank[:, :]), dve)
                            do(V.tensor_reduce(mxs[n % 3], v3(pr[n % 3], TT), AX.X, ALU.max))
                        do(ts(mxs[n % 3], mxs[n % 3], -scale, ALU.mult))
                        raise_("scores_maxed")
                    if h >= 2:
                        n = first + h - 2
                        bank = ps2.read(dve, f"o_{n}", "dve")
                        do(V.reciprocal(rs[:, 0:TT], sums[n % 3]))
                        dst = obr[:, :, (h - 2) * width:(h - 1) * width]
                        ps2.release(f"o_{n}", tt(dst, v3(bank[:, 0:TT * width], TT), over(rs[:, 0:TT], width, 2),
                                                 ALU.mult), dve)
            attention(EH, 0, EQ ** -0.5, False, EV)
            dve.wait_ge(ev("gate_tanhs_2"), 1)
            add_gated_branch(gates2, True)
            raise_("gate_2_added")
            dve.wait_ge(ev("gla_rows_loaded"), 48)
            for t in range(TT):
                bank = ps2.read(dve, f"lg{t}", "dve")
                ps2.release(f"lg{t}", tt(la[:, t, :], bank[:, :], bgla, ALU.add), dve)
            do(stt(flat(lt), flat(la), -1.0, flat(la), ALU.mult, ALU.max))
            raise_("log_arg")
            do(ts(flat(la), flat(la), 0.0, ALU.min))
            dve.wait_ge(ev("log_done"), 1)
            do(tt(flat(la), flat(la), flat(lt), ALU.subtract))
            do(ts(flat(la), flat(la), 1.0 / 16.0, ALU.mult))
            raise_("log_decays")
            for t in range(TT):
                bank = ps2.read(dve, f"lvl0{t}", "dve")
                ps2.release(f"lvl0{t}", tt(att[t], v3(bank[:, :], GH), over(ident, GH, 1), ALU.mult), dve)
            ps2.wait_drained(dve, "cum1")
            def sides(v, side, half):
                w = v.rearrange("p h (b s c) -> p (h b) s c", s=2, c=half)
                return w[:, :, side, :]

            def level_differences(lvl):
                if lvl <= LEVELS:
                    half = 2 ** (lvl - 1)
                    mid = gbT.rearrange("p h (b s c) -> p (h b) s c", s=2, c=half)[:, :, 0, half - 1:half]
                    mid = mid.to_broadcast(list(sides(gbT, 0, half).shape))
                    do(tt(sides(lev, 0, half), mid, sides(gbT, 0, half), ALU.subtract))
                    do(tt(sides(lev, 1, half), sides(gbT, 1, half), mid, ALU.subtract))
                else:
                    mid = gbT[:, :, P - 1:P].to_broadcast([P, GH, P])
                    do(tt(lev[:, :, 0:P], mid, gbT[:, :, 0:P], ALU.subtract))
                    do(V.tensor_copy(lev[:, :, P:T], gbT[:, :, P:T]))
                raise_("level_differences")
            level_differences(1)
            for lvl in range(1, LEVELS + 2):
                half = 2 ** (lvl - 1)
                dve.wait_ge(ev("level_exps"), lvl)
                if lvl > 1:
                    ps2.wait_filled(dve, f"lvl{lvl - 1}1")
                do(tt(sides(qk, 0, half), sides(lev, 0, half), sides(gkT, 0, half), ALU.mult))
                do(tt(sides(qk, 1, half), sides(lev, 1, half), sides(gqT, 1, half), ALU.mult))
                raise_("level_ready")
                if lvl <= LEVELS:
                    level_differences(lvl + 1)
                    mask = C["level"][:, (lvl - 1) * P:lvl * P]
                    for t in range(TT):
                        bank = ps2.read(dve, f"lvl{lvl}{t}", "dve")
                        ps2.release(f"lvl{lvl}{t}", V.copy_predicated(att[t], over(mask, GH, 1).bitcast(I32),
                                                                      v3(bank[:, :], GH)), dve)
            dve.wait_ge(ev("latents_out"), 1)
            for t in range(TT):
                head_norm(ckv[t][:, :, 0:KVR], 1, KVR, None, csq.unsqueeze(1))
            raise_("ckv_normed")
            dve.wait_ge(ev("r_tanh"), 1)
            for t, e_ in enumerate((flat(la), flat(lt))):
                times_sigmoid(gr[:, t, :], e_, gr[:, t, :])
                do(tt(heads(gr[:, t, :], DV), heads(gr[:, t, :], DV), over(ggla, GH, 1), ALU.mult))
            for h in range(GH):
                bank = ps2.read(dve, f"go{h}", "dve")
                ps2.release(f"go{h}", V.tensor_copy(obr[:, :, h * DV:h * DV + DV], v3(bank[:, :], TT)), dve)
            raise_("gla_summed")
            dve.wait_ge(ev("gla_squares"), 1)
            for t, sq_ in enumerate((gqT, gkT)):
                do(V.tensor_reduce(hss[:, t * GH:(t + 1) * GH], heads(flat(sq_), DV), AX.X, ALU.add))
            rsqrt(rs[:, 0:TT * GH], TT * GH, hss[:, 0:TT * GH], DV)
            for t in range(TT):
                oh = heads(obr[:, t, :], DV)
                do(tt(oh, oh, over(rs[:, t * GH:(t + 1) * GH], DV, 2), ALU.mult))
                do(tt(obr[:, t, :], obr[:, t, :], gr[:, t, :], ALU.mult))
            gate_logits(1, "1", gates1, g2b)
            dve.wait_ge(ev("gate_tanhs_1"), 1)
            add_gated_branch(gates1)
            raise_("gla_done")

            def rotate(dst, src, t, n):
                c_, s_ = over(cosv[:, t, :], n, 1), over(sinv[:, t, :], n, 1)
                tmp = nsq[:, 0:n * NI].rearrange("p (n c) -> p n c", n=n)
                a_, b_ = src[:, :, 0:NI], src[:, :, NI:ROPE]
                do(tt(dst[:, :, 0:NI], a_, c_, ALU.mult))
                do(tt(tmp, b_, s_, ALU.mult))
                do(tt(dst[:, :, 0:NI], dst[:, :, 0:NI], tmp, ALU.subtract))
                do(tt(dst[:, :, NI:ROPE], a_, s_, ALU.mult))
                do(tt(tmp, b_, c_, ALU.mult))
                do(tt(dst[:, :, NI:ROPE], dst[:, :, NI:ROPE], tmp, ALU.add))
            for t in range(TT):
                head_norm(ckv[t][:, :, KVR:KVR + ROPE], 1, ROPE, G_KR, nsq[:, 0:ROPE].unsqueeze(1))
                rotate(kr2[:, t:t + 1, 0:ROPE], ckv[t][:, :, KVR:KVR + ROPE], t, 1)
                do(V.tensor_copy(kr2[:, t, ROPE:2 * ROPE], kr2[:, t, 0:ROPE]))
            raise_("rope_k_ready")
            gate_logits(0, "0a", gates0, fnw, (0,))
            dve.wait_ge(ev("q_squares"), 1)
            for part, (lo, w) in enumerate(((0, NOPE), (NOPE, ROPE))):
                for t in range(TT):
                    at = (part * TT + t) * MH
                    do(V.tensor_reduce(hss[:, at:at + MH], v3(qsqs[t], MH)[:, :, lo:lo + w], AX.X, ALU.add))
            rsqrt(rs[:, 0:2 * TT * MH], 2 * TT * MH, hss, [(TT * MH, NOPE), (TT * MH, ROPE)])
            for t in range(TT):
                qh = v3(q[t], MH)
                do(tt(qh[:, :, 0:NOPE], qh[:, :, 0:NOPE], over(rs[:, t * MH:(t + 1) * MH], NOPE, 2), ALU.mult))
                do(tt(qh[:, :, NOPE:], qh[:, :, NOPE:], over(rs[:, (TT + t) * MH:(TT + t + 1) * MH], ROPE, 2), ALU.mult))
                do(tt(qh[:, :, NOPE:], qh[:, :, NOPE:], over(G_QR, MH, 1), ALU.mult))
                rotate(heads(ropeb[:, t, :], ROPE), qh[:, :, NOPE:], t, MH)
            raise_("mla_q_ready")
            dve.wait_ge(ev("k_squares"), 1)
            for t in range(TT):
                do(V.tensor_reduce(hss[:, t * MH:(t + 1) * MH], v3(ksqs[t], MH), AX.X, ALU.add))
            rsqrt(rs[:, 0:TT * MH], TT * MH, hss, NOPE)
            for t in range(TT):
                kh = v3(kv[:, t, :], MH)[:, :, 0:NOPE]
                do(tt(kh, kh, over(rs[:, t * MH:(t + 1) * MH], NOPE, 2), ALU.mult))
            raise_("mla_k_ready")
            gate_logits(0, "0b", gates0, fnw, (1,))
            attention(MH, EH, (NOPE + ROPE) ** -0.5, True, VD)
            for name in ("0a", "0b"):
                dve.wait_ge(ev(f"gate_tanhs_{name}"), 1)
            add_gated_branch(gates0)
            raise_("branches_summed")
            to_channels(ps2, "ysT", hT, 0.5, None)

            def low_part(n):
                dve.wait_ge(ev("high_parts"), n + 1)
                at = (FFN_LOAD + n) % 4
                do(tt(low_slots[at], slots[at], high_slots[n % 2].bitcast(F32), ALU.subtract))
                raise_("low_parts")
            low_part(0)
            low_part(1)
            for n in range(2):
                for t in range(TT):
                    bank = ps2.read(dve, f"wo{n}t{t}", "dve")
                    dst = x[:, t, n * 512:n * 512 + 512]
                    ps2.release(f"wo{n}t{t}", tt(dst, bank[:, :], dst, ALU.add), dve)
                    if n:
                        raise_("x_updated")
            normalize(xn, x)
            raise_("x_normed")
            to_channels(ps2, "h4", hT, prm[:, ROWS["g_ffn"]:ROWS["g_ffn"] + 8], None)
            dve.wait_ge(ev("ffn_input_high"), 1)
            do(tt(flat(hL), hT_sb[:, :], flat(hH).bitcast(F32), ALU.subtract))
            raise_("ffn_input_split")
            for n in range(8):
                for b in range(2):
                    dve.wait_ge(ev("ffn_high"), 2 * n + b + 1)
                    do(tt(relu[b], relu[b], relu[b], ALU.mult))
                    high = flat(aH[n])[:, b * 512:b * 512 + 512].bitcast(F32)
                    do(tt(flat(aL[n])[:, b * 512:b * 512 + 512], relu[b], high, ALU.subtract))
                    raise_("ffn_squared")
                low_part(n + 2)
            for n in range(10, 16):
                low_part(n)
            for t in range(TT):
                for n in range(2):
                    bank = ps2.read(dve, f"down{t}{n}", "dve")
                    dst = x[:, t, n * 512:n * 512 + 512]
                    ps2.release(f"down{t}{n}", tt(dst, bank[:, :], dst, ALU.add), dve)
                    raise_("output_ready")
        @block.gpsimd
        def _(pool):
            def rows_of(dst, src, name):
                pool.dma_start(dst, src.partition_broadcast(P)).then_inc(ev(name), 16)
            pool.memset(raw[:, :, 0:3], 0.0).then_inc(ev("pool_step"), 1)
            for v in (uT, sA, sB):
                pool.memset(v[:, :, 0:PAD], 0.0).then_inc(ev("pool_step"), 1)
            pool.memset(wpool, 0.0).then_inc(ev("pool_step"), 1)
            pool.wait_ge(ev("pool_step"), 5)
            pool.sem_inc(ev("pads_zeroed"), 1)
            rows_of(dt_b, a["dt_bias"][0], "head_rows_loaded")
            rows_of(alog_b, a["a_log"][0], "head_rows_loaded")
            rows_of(dskip_b, a["d_skip"][0], "head_rows_loaded")
            for g in range(4):
                lo = 64 * (g % 2)
                pool.dma_start(wpool[lo:lo + 64, g // 2, lo:lo + 64], a["w_pool"][0][g]).then_inc(ev("pool_weights_loaded"), 16)
            pool.dma_start(flat(prc), a["pool_table"]).then_inc(ev("pool_table_loaded"), 16)
            pool.dma_start(mem_x, a["mem_2"][0].rearrange("(t p) d -> p t d", p=P)).then_inc(ev("memory_loaded"), 16)
            for n, (nm, w) in enumerate((("g_q_nope_2", 128), ("g_k_nope_2", 128), ("g_q_rope_2", 64),
                                         ("g_k_rope_2", 64), ("g_q_mem_2", 64), ("g_k_mem_2", 64))):
                lo = (0, 128, 256, 320, 384, 448)[n]
                rows_of(rows2[:, lo:lo + w], a[nm][0], "norm_rows_loaded")
            rows_of(rb[:, 0:EG], a["b_group"][0], "router_rows_loaded")
            rows_of(rb[:, EG:], a["b_router"][0], "router_rows_loaded")
            pool.dma_start(pos_i, a["positions_2"][0].rearrange("(t p) -> p t", p=P),
                           allow_slow_non_contiguous=True).then_inc(ev("positions_loaded"), 16)
            ps.wait_drained(pool, "adaT3")
            rows_of(g1b[:, :], a["b_ada"][0][2 * D:3 * D], "gate_rows_loaded")
            rows_of(g2b[:, :], a["b_ada"][0][5 * D:6 * D], "gate_rows_loaded")
            rows_of(fnw[:, :], a["final_norm_w"], "final_rows_loaded")
            pool.wait_ge(ev("ssd_normed"), 1)
            pool.dma_start(wr[:, :, 0:EG], a["w_group"][0].rearrange("(k p) n -> p k n", p=P)).then_inc(ev("router_loaded"), 16)
            pool.dma_start(wr[:, :, EG:], a["w_router"][0].rearrange("(k p) n -> p k n", p=P)).then_inc(ev("router_loaded"), 16)
            pool.wait_ge(ev("x_updated"), 2)
            rows_of(g1b[:, :], a["b_gate_2"][0][2 * D:3 * D], "gate_bias_loaded_2")
            pool.wait_ge(ev("x_updated"), 4)
            rows_of(g2b[:, :], a["b_gate_2"][0][D:2 * D], "gate_bias_loaded_1")
            pool.wait_ge(ev("x_updated"), 6)
            rows_of(fnw[:, :], a["b_gate_2"][0][0:D], "gate_bias_loaded_0")
            pool.dma_start(wgate[0:GRANK, :], a["w_gla_gate_2"][0]).then_inc(ev("gla_rows_loaded"), 16)
            rows_of(bgla, a["b_gla_gate_2"][0], "gla_rows_loaded")
            rows_of(ggla, a["g_gla_out_2"][0], "gla_rows_loaded")
        @block.sync
        def _(sp):
            sp.dma_start(cst[:, :], a["const"]).then_inc(ev("constants_loaded"), 16)

            def load_rows(name, src, rows):
                sp.dma_start(prm_rows[ROWS[name]:ROWS[name] + rows, 0:P], src).then_inc(ev("param_rows_loaded"), 16)
            load_rows("c", a["c"][0].rearrange("(k p) -> k p", p=P), 8)
            load_rows("conv_w", a["conv_w"][0].rearrange("t (k p) -> (t k) p", p=P), CONV * NXB)
            load_rows("conv_b", a["conv_b"][0].rearrange("(k p) -> k p", p=P), NXB)
            load_rows("ssd_norm_w", a["ssd_norm_w"][0].rearrange("(k p) -> k p", p=P), 6)
            load_rows("pool_scale", a["pool_scale"][0].rearrange("(k p) -> k p", p=P), 2)
            load_rows("g_mix", a["g_mix_2"][0].rearrange("(k p) -> k p", p=P), 8)
            load_rows("g_mem", a["g_mem_2"][0].rearrange("(k p) -> k p", p=P), 8)
            load_rows("g_ffn", a["g_ffn_2"][0].rearrange("(k p) -> k p", p=P), 8)
            load_rows("g_ckv", a["g_ckv_2"][0].rearrange("(k p) -> k p", p=P), 2)
            load_rows("g_q_nope", a["g_q_nope_2"], 1)
            load_rows("g_k_nope", a["g_k_nope_2"], 1)
            sp.dma_start(prm_rows[0:48, P:2 * P],
                         a["b_ada"][0].rearrange("(k p) -> k p", p=P)).then_inc(ev("param_rows_loaded"), 16)
            sp.dma_start(x, a["x"][0].rearrange("(t p) d -> p t d", p=P)).then_inc(ev("x_loaded"), 16)
            for n in ADA1:
                ring.load(sp, cols_of(512), k_rows(w_ada, slice(n * 512, n * 512 + 512)))
            for n in IN_ORDER:
                c0, w = IN_SLOTS[n]
                ring.load(sp, cols_of(w), k_rows(w_in, slice(c0, c0 + w)))
            for step in BESIDE:
                for what, n, *t in step:
                    if what == "ada":
                        ring.load(sp, cols_of(512), k_rows(w_ada, slice(n * 512, n * 512 + 512)))
                    elif (what, n) == ("mk", 0) or (what == "mv" and n and t == [0]):
                        c0, w = MEM_SLOTS[n]
                        ring.load(sp, cols_of(w), k_rows(w_mkv, slice(c0, c0 + w)))
            for n in range(2):
                ring.load(sp, cols_of(512), k_rows(w_out, slice(n * 512, n * 512 + 512)))
            def load_w13(b, e, wait):
                for part in range(2):
                    wait(3 * b + part)
                    src = w13[bass.ds(e, 1), part * 512:part * 512 + 512, :]
                    sp.dma_start(slots[3 * b + part].rearrange("p (k n) -> p k n", k=4),
                                 src.rearrange("e (k p) n -> (e p) k n", p=P)).then_inc(xw_landed[3 * b + part], 16)

            def load_w2(b, e, wait):
                wait(3 * b + 2)
                src = w2[bass.ds(e, 1), :, :]
                sp.dma_start(slots[3 * b + 2].rearrange("p (k n) -> p k n", k=4),
                             src.rearrange("e (k p) n -> (e p) k n", p=P)).then_inc(xw_landed[3 * b + 2], 16)

            last_of = {n % 4: name for n, name in sorted(ring.free_at.items())}

            def ring_free(slot):
                if slot in last_of:
                    ps.wait_filled(sp, last_of[slot])
            load_w13(0, 0, ring_free)
            load_w2(0, 0, ring_free)
            sp.wait_ge(ev("routed"), 1)
            pairs = sp.value_load(meta[0:1, P:P + 1], min_val=4, max_val=MAXB // 2)
            last = sp.value_load(meta[0:1, P + 1:P + 2], min_val=3, max_val=MAXB // 2 - 1)

            def expert_of(block):
                return sp.value_load(meta[0:1, block:block + 1] if isinstance(block, int)
                                     else meta[0:1, bass.ds(block, 1)], min_val=0, max_val=NE - 1)
            eb = expert_of(1)
            load_w13(1, eb, ring_free)
            load_w2(1, eb, lambda s_: None)
            load_w13(0, expert_of(2), lambda s_: sp.wait_ge(ev("hidden_filled"), 2))
            load_w13(1, expert_of(3), lambda s_: sp.wait_ge(ev("hidden_filled"), 4))
            with sp.Fori(2, pairs) as i:
                olda, oldb, ea, eb = (expert_of(i * 2 + n) for n in (-2, -1, 0, 1))
                load_w13(0, ea, lambda s_: sp.wait_ge(ev("hidden_filled"), i * 4 - 2))
                load_w2(0, olda, lambda s_: sp.wait_ge(ev("rows_filled_for_dve"), i - 1))
                load_w2(1, oldb, lambda s_: sp.wait_ge(ev("rows_filled_for_dve"), i - 1))
                load_w13(1, eb, lambda s_: sp.wait_ge(ev("hidden_filled"), i * 4))
            for b in range(2):
                load_w2(b, expert_of(last * 2 + b), lambda s_: sp.wait_ge(ev("rows_filled_for_dve"), last))
            for n, (c0, w) in enumerate(LATE_A):
                need = None
                if n < 4:
                    need = [(ev("hidden_filled"), last * 4 + 2), (ev("hidden_filled"), last * 4 + 2),
                            (ev("rows_filled_for_dve"), pairs), (ev("hidden_filled"), pairs * 4)][n]
                ring2.load(sp, cols_of(w), k_rows(w_in2, slice(c0, c0 + w)), need)
            ring2.load(sp, cols_of(2048, 2), w_ukv.rearrange("(k p) n -> p k n", p=P))
            for c0, w in LATE_B:
                ring2.load(sp, cols_of(w), k_rows(w_in2, slice(c0, c0 + w)))
            for n in range(2):
                ring2.load(sp, cols_of(512), k_rows(w_o2, slice(n * 512, n * 512 + 512)))
            for n in range(8):
                ring2.load(sp, cols_of(512), k_rows(w_up, slice(n * 512, n * 512 + 512)))
            for n in range(8):
                ring2.load(sp, cols_of(D, 4), w_down[n * 512:n * 512 + 512, :].rearrange("(k p) n -> p k n", p=P))
            sp.wait_ge(ev("output_ready"), 4)
            sp.dma_start(out[0].rearrange("(t p) d -> p t d", p=P), x).then_inc(ev("output_written"), 16)
            sp.wait_ge(ev("output_written"), 16)


_INS = ["x", "c", "w_ada", "b_ada", "w_in", "w_pool", "pool_scale", "conv_w", "conv_b", "dt_bias", "a_log",
        "d_skip", "ssd_norm_w", "w_out", "w_group", "b_group", "w_router", "b_router", "w13", "w2",
        "final_norm_w", "mem_2", "positions_2", "g_mix_2", "w_in_2", "b_gate_2", "g_ckv_2", "w_ukv_2",
        "g_q_nope_2", "g_k_nope_2", "g_q_rope_2", "g_k_rope_2", "w_gla_gate_2", "b_gla_gate_2", "g_gla_out_2",
        "g_mem_2", "w_mem_kv_2", "g_q_mem_2", "g_k_mem_2", "w_o_2", "g_ffn_2", "w_up_2", "w_down_2"]


def program(nc, arrays):
    args = {}
    for name, v in arrays.items():
        args[name] = nc.dram_tensor(f"in_{name}_dram", v.shape, mybir.dt.from_np(v.dtype), kind="ExternalInput").ap()
    out = nc.dram_tensor("out_0_dram", (1, T, D), F32, kind="ExternalOutput").ap()
    build(nc, args, out)


def kernel(**inputs):
    import concourse.bacc as _bacc
    from concourse.bass_utils import run_bass_kernel_spmd as _run

    nc = _bacc.Bacc("TRN2", target_bir_lowering=False, num_devices=1)
    arrays = {name: np.ascontiguousarray(inputs[name]) for name in _INS}
    arrays["const"], arrays["pool_table"] = constants()
    program(nc, arrays)
    r = _run(nc, [{f"in_{k}_dram": v for k, v in arrays.items()}], core_ids=[0])
    return r.results[0]["out_0_dram"]
```

```python
from contextlib import ExitStack

import numpy as np

import concourse.bass as bass
from concourse import mybir

ALU = mybir.AluOpType
ACT = mybir.ActivationFunctionType
AX = mybir.AxisListType
F32 = mybir.dt.float32
F32R = mybir.dt.float32r
I32 = mybir.dt.int32

P = 128
D = 1024
T = 256
TT = T // P
KD = D // P
EPS = 1e-6

POOL_W, SSD_W, HEADS, HD, GROUPS, STATE, CONV = 256, 768, 12, 64, 4, 128, 4
RPG = HEADS // GROUPS
XBC = SSD_W + 2 * GROUPS * STATE
NXB = XBC // P
IN1 = POOL_W + SSD_W + XBC + HEADS
EG, EPG, FF = 4, 8, 512
NE = EG * EPG
SLOTS = 64
MAXB = NE + 2 * T // SLOTS
MH, NOPE, ROPE, VD, KVR = 8, 128, 64, 128, 256
GH, DK, DV, GRANK = 4, 128, 256, 16
EH, EQ, EV = 4, 64, 256
O_Q, O_CKV, O_KR = 0, 1536, 1792
O_GQ, O_GK, O_GV, O_GA, O_GR = 1856, 2368, 2880, 3904, 3920
O_MQ, O_GATE = 4944, 5200
LEVELS = 7
BIG = -1e30

ROWS = {}
_r = 0
for _n, _c in (("c", 8), ("conv_w", CONV * NXB), ("conv_b", NXB), ("ssd_norm_w", 6), ("pool_scale", 2),
               ("g_mix", 8), ("g_mem", 8), ("g_ffn", 8), ("g_ckv", 2),
               ("g_q_nope", 1), ("g_k_nope", 1)):
    ROWS[_n] = _r
    _r += _c
NROWS = _r
BADA = NROWS
assert NROWS <= P

CONST_COLS = {}
_r = 0
for _n, _c in (("ident", P), ("tri", P), ("strict", P), ("ones", P), ("seg_mask", P), ("causal", 3 * P),
               ("iota", P), ("level", LEVELS * P), ("inv", ROPE // 2), ("row_id", 1), ("row_before", 1), ("quarters", 1),
               ("rev4", EG), ("rev8", EPG)):
    CONST_COLS[_n] = (_r, _c)
    _r += _c
NCONST = _r


def constants():
    c = np.zeros((P, NCONST), np.float32)
    p, f = np.arange(P)[:, None], np.arange(P)[None, :]

    def put(name, value):
        a, n = CONST_COLS[name]
        c[:, a:a + n] = value
    put("ident", p == f)
    put("tri", p <= f)
    put("strict", p < f)
    put("ones", 1.0)
    put("seg_mask", np.where(p <= f, 0.0, BIG))
    causal = np.where(f <= p, 0.0, BIG)
    put("causal", np.concatenate([causal, np.zeros((P, P)), causal], 1))
    put("iota", np.broadcast_to(f, (P, P)))
    x = p ^ f
    put("level", np.concatenate([(x >= 2 ** l) & (x < 2 ** (l + 1)) & (p < f) for l in range(LEVELS)], 1))
    put("inv", (1.0 / (np.float32(10000.0) ** (np.arange(0, ROPE, 2, dtype=np.float32) / np.float32(ROPE))))[None, :])
    put("row_id", p)
    put("row_before", p - 1)
    put("quarters", p % 32 == 0)
    put("rev4", np.arange(EG, 0, -1)[None, :])
    put("rev8", np.arange(EPG, 0, -1)[None, :])
    pool = np.zeros((P, 2, T), np.float32)
    for g, w in enumerate((2, 4, 8, 16)):
        cnt = np.minimum(np.arange(1, T + 1, dtype=np.float32), np.float32(w))
        pool[64 * (g % 2):64 * (g % 2) + 64, g // 2] = np.float32(1.0) / cnt
    return c, pool.reshape(P, 2 * T)


class Signal:

    def __init__(self, sem):
        self.sem, self.n = sem, 0


class Chained:

    def __init__(self, eng, sem):
        self.eng, self.done = eng, Signal(sem)

    def __call__(self, ins, signal=None):
        s = signal or self.done
        s.n += 1
        ins.then_inc(s.sem, 1)
        self.eng.wait_ge(s.sem, s.n)


class LoopChained:

    def __init__(self, eng, sem, i, per):
        self.eng, self.sem, self.i, self.per, self.n = eng, sem, i, per, 0

    def __call__(self, ins):
        self.n += 1
        ins.then_inc(self.sem, 1)
        self.eng.wait_ge(self.sem, self.i * self.per + (self.n - self.per))

    def end(self):
        assert self.n == self.per, (self.n, self.per)


class PsumBanks:

    def __init__(self, banks, filled, drained):
        self.banks, self.filled, self.drained = banks, filled, drained
        self.order, self.by = [], {}
        self.count = {"dve": 0, "act": 0}
        self.seen = {"dve": 0, "act": 0}

    def fill(self, pe, name, reader):
        n = len(self.order)
        if n >= 8:
            r, k = self.order[n - 8]
            pe.wait_ge(self.drained[r], k + 1)
        assert name not in self.by, name
        self.by[name] = (n % 8, reader, self.count[reader])
        self.order.append((reader, self.count[reader]))
        self.count[reader] += 1
        return self.banks[n % 8]

    def full(self, name, ins):
        ins.then_inc(self.filled[self.by[name][1]], 1)

    def wait_drained(self, pe, name):
        _, r, k = self.by[name]
        pe.wait_ge(self.drained[r], k + 1)

    def wait_filled(self, eng, name):
        _, r, k = self.by[name]
        eng.wait_ge(self.filled[r], k + 1)

    def read(self, eng, name, reader):
        b, r, k = self.by[name]
        assert r == reader and k == self.seen[reader], (name, r, k, self.seen[reader])
        eng.wait_ge(self.filled[r], k + 1)
        return self.banks[b]

    def release(self, name, ins, eng):
        _, r, k = self.by[name]
        self.seen[r] += 1
        ins.then_inc(self.drained[r], 1)
        eng.wait_ge(self.drained[r], k + 1)


class WeightRing:

    def __init__(self, ps, slots, landed):
        self.ps, self.slots, self.landed = ps, slots, landed
        self.n, self.loads, self.taken, self.free_at = len(slots), 0, 0, {}

    def take(self, pe):
        k = self.taken
        self.taken += 1
        pe.wait_ge(self.landed[k % self.n], 16 * (k // self.n + 1))
        return self.slots[k % self.n]

    def last_use(self, bank_name, k=None):
        self.free_at[self.taken - 1 if k is None else k] = bank_name

    def wait_used(self, eng, k):
        at = self.free_at[k]
        if isinstance(at, tuple):
            eng.wait_ge(*at)
        else:
            self.ps.wait_filled(eng, at)

    def load(self, sp, view, src, need=None):
        k = self.loads
        self.loads += 1
        if k >= self.n:
            self.wait_used(sp, k - self.n)
        if need:
            sp.wait_ge(*need)
        s = k % self.n
        sp.dma_start(view(self.slots[s]), src).then_inc(self.landed[s], 16)


def build(nc, a, out):
    ctx = ExitStack()
    with ctx:
        def sb(name, cols, dt=F32, parts=P):
            return ctx.enter_context(nc.sbuf_tensor(name, [parts, cols], dt))

        def twin(name, cols):
            with nc.sbuf_tensor(f"{name}_parts", [P, cols], F32R) as parts:
                pass
            whole = sb(name, cols)
            return whole, parts

        def sem(name):
            return ctx.enter_context(nc.semaphore(name))

        def v3(ap, n):
            return ap.rearrange("p (a b) -> p a b", a=n)

        def over(ap, n, axis):
            x = ap.unsqueeze(axis)
            shape = list(x.shape)
            shape[axis] = n
            return x.to_broadcast(shape)

        ring_mem, ring_mem_r = twin("weight_ring", 6 * 4096)
        cst = sb("constants", NCONST)
        C = {n: cst[:, x:x + w] for n, (x, w) in CONST_COLS.items()}
        ident, ones = C["ident"], C["ones"]
        prm = sb("param_cols", NROWS + 48)
        x = v3(sb("x_tokens", TT * D)[:, :], TT)
        hT_sb, hT_r = twin("hT", KD * T)
        hT = v3(hT_sb[:, :], KD)
        g1b, g1b_r = twin("gate1_rows", D)
        g2b, g2b_r = twin("gate2_rows", D)
        fnw = sb("final_norm_rows", D)
        rows2 = sb("norm_gain_rows", 512)
        kmT = v3(sb("mem_keysT", 2 * T)[:, :], 2)
        vm_sb, vm_r = twin("mem_values", TT * D)
        vm = v3(vm_sb[:, :], TT)
        small = sb("small", 1100)
        small_at = [0]

        def tiny(n, dt=F32):
            v = small[:, small_at[0]:small_at[0] + n]
            small_at[0] += n
            assert small_at[0] <= 1100, small_at
            return v if dt == F32 else v.bitcast(dt)

        work, work_r = twin("work", 14840)
        extra = ring_mem[:, 4 * 4096:6 * 4096]

        def area(*bases):
            left = [[b, 0] for b in bases]

            def alloc(n):
                for e in left:
                    if e[1] + n <= e[0].shape[1]:
                        e[1] += n
                        return e[0][:, e[1] - n:e[1]]
                raise AssertionError((n, [(b.shape, u) for b, u in left]))
            return alloc

        banks = [ctx.enter_context(nc.psum_tensor(f"bank{i}", [P, 512], F32)) for i in range(8)]

        def flat(v):
            return v.rearrange("p a b -> p (a b)")

        m1 = area(work[:, :])
        xn_f = m1(TT * D)
        xn = v3(xn_f, TT)
        mixT = v3(hT_sb[:, :], KD)
        raw_f = m1(NXB * (T + 3))
        raw = v3(raw_f, NXB)
        xb_f = m1(NXB * T)
        xb = v3(xb_f, NXB)
        cv_f, ce_f = m1(4 * T), m1(4 * T)
        cv, ce = v3(cv_f, 4), v3(ce_f, 4)
        z = v3(m1(TT * SSD_W), TT)
        wpool = v3(m1(2 * P), 2)
        y_f = m1(TT * SSD_W)
        yv = v3(y_f, TT)
        prc = v3(y_f[:, 0:2 * T], 2)
        prm_rows = cv_f[:, 0:2 * P]
        u_mem = area(vm_sb[:, :])
        PAD = 16
        uT, sA, sB = (v3(u_mem(2 * (T + PAD)), 2) for _ in range(3))
        diff = kmT
        r_mem = area(raw_f)
        xtok = v3(r_mem(TT * 1280), TT)
        prevT = v3(r_mem(GROUPS * RPG * HD), GROUPS)
        xdt = v3(hT_sb[:, 0:TT * SSD_W], TT)
        seg2 = [v3(cv_f[:, n * RPG * P:(n + 1) * RPG * P], RPG) for n in range(2)]
        s_mem = area(ring_mem[:, 4 * 4096:5 * 4096])
        segs = [v3(s_mem(RPG * P), RPG) for _ in range(TT * GROUPS)]
        mrow = [s_mem(512) for _ in range(2)]
        t_mem = area(ring_mem[:, 5 * 4096:6 * 4096])
        mem_x = v3(t_mem(TT * D), TT)
        memT = v3(t_mem(KD * T), KD)
        zt = [mem_x[:, t, 0:SSD_W] for t in range(TT)]
        xcd = ce_f[:, 0:SSD_W]
        ybuf = ce_f[:, SSD_W:SSD_W + RPG * HD]
        m3 = area(work[:, TT * D:])
        xeT = v3(m3(KD * P), KD)
        hs = m3(D)
        ge, gt, sT = (m3(4 * P) for _ in range(3))
        osb = m3(D)
        mk, msq = flat(kmT), m3(TT * EH * EQ)
        pick = v3(m3(TT * P), TT)
        wr = v3(m3(KD * (EG + NE)), KD)
        acc_f = m3(TT * D)
        acc = v3(acc_f, TT)
        diag = v3(acc_f[:, D:2 * D], 8)
        slot_rows, gate_rows = m3(2 * T), m3(2 * T)
        share_f = m3(2 * T)
        slot_id = m3(P)
        m2 = area(work[:, :], extra)
        ysum, obr = v3(m2(TT * D), TT), v3(m2(TT * D), TT)
        pr_f, pT_f = m2(3 * TT * T), m2(2 * TT * T)
        pr, pT = ([f_[:, n * TT * T:(n + 1) * TT * T] for n in range(m)] for f_, m in ((pr_f, 3), (pT_f, 2)))
        QW = MH * (NOPE + ROPE)
        q = [vm_sb[:, 0:QW], m2(QW)]
        ckv = [v3(c_, 1) for c_ in (vm_sb[:, QW:QW + KVR + ROPE], flat(kmT)[:, 0:KVR + ROPE])]
        used2 = 2 * TT * D + 5 * TT * T + QW

        def branch_area():
            return area(work[:, used2:], extra)
        b1 = branch_area()
        gv, gr = v3(b1(TT * D), TT), v3(b1(TT * D), TT)
        gates1 = b1(2 * GH * T)
        gbT, lev = (v3(gates1[:, n * GH * T:(n + 1) * GH * T], GH) for n in range(2))
        gates1 = v3(gates1, TT)
        gqT, gkT = v3(b1(GH * T), GH), v3(b1(GH * T), GH)
        qk = v3(b1(GH * T), GH)
        att = [v3(b1(GH * P), GH) for _ in range(3)]
        la, lt = v3(b1(TT * GH * DK), TT), v3(b1(TT * GH * DK), TT)
        gaT = b1(T)
        wgate = b1(GH * DK)
        bgla = b1(GH * DK)
        ggla = b1(DV)
        b0 = area(flat(gv))
        qm = v3(b0(TT * EH * EQ), TT)
        qmT = v3(b0(2 * T), 2)
        qsq = v3(b0(TT * EH * EQ), TT)
        gates2 = gr
        b2 = branch_area()
        gates0 = v3(b2(TT * D), TT)
        kv = v3(b2(TT * MH * (NOPE + VD)), TT)
        qnT, qrT = v3(b2(MH * T), MH), v3(b2(4 * T), 4)
        knT, krT = v3(b2(MH * T), MH), b2(T)
        qsqs = [flat(qnT)[:, 0:QW], flat(knT)[:, 0:QW]]
        ksqs = [pr_f[:, 0:MH * NOPE], pT_f]
        ckT = v3(b2(2 * T), 2)
        ropeb = v3(b2(TT * MH * ROPE), TT)
        kr2 = v3(b2(TT * 2 * ROPE), TT)
        nsq = b2(MH * ROPE)
        csq = pr_f[:, 0:KVR]
        pieces_ = [work_r[:, n * 4 * T:(n + 1) * 4 * T] for n in range(14)] + [g1b_r[:, :], g2b_r[:, :]]
        aH, aL = ([v3(pieces_[2 * n + m], 4) for n in range(8)] for m in range(2))
        relu = [fnw[:, n * 2 * T:(n + 1) * 2 * T] for n in range(2)]
        hH, hL = (v3(v_, KD) for v_ in (vm_r[:, :], hT_r[:, :]))

        S = {}

        def ev(name):
            if name not in S:
                S[name] = sem(name)
            return S[name]
        ps = PsumBanks(banks, {r: ev(f"bank_filled_for_{r}") for r in ("dve", "act")},
                       {r: ev(f"bank_drained_by_{r}") for r in ("dve", "act")})
        ps2 = PsumBanks(banks, {r: ev(f"late_bank_filled_for_{r}") for r in ("dve", "act")},
                        {r: ev(f"late_bank_drained_by_{r}") for r in ("dve", "act")})
        slots = [ring_mem[:, i * 4096:(i + 1) * 4096] for i in range(6)]
        ring = WeightRing(ps, slots[:4], [ev(f"weights_landed_{i}") for i in range(4)])
        low_slots = [ring_mem_r[:, i * 4096:(i + 1) * 4096] for i in range(4)]
        high_slots = [ring_mem_r[:, i * 4096:(i + 1) * 4096] for i in (4, 5)]
        ring2 = WeightRing(ps2, slots[:4], [ev(f"late_weights_landed_{i}") for i in range(4)])
        xw_landed = [ev(f"expert_weights_landed_{i}") for i in range(6)]

        cs = tiny(KD)
        ctmp = tiny(KD)
        modc = tiny(48)
        ss, ss_w = tiny(TT), tiny(TT)
        rs = tiny(40)
        rt = [tiny(40) for _ in range(2)]
        dt_b, alog_b, dskip_b = tiny(HEADS), tiny(HEADS), tiny(HEADS)
        dtr, dta, dtv = (v3(tiny(TT * HEADS), TT) for _ in range(3))
        nega = tiny(HEADS)
        acs = v3(tiny(3 * HEADS), 3)
        eacs, dte = tiny(HEADS), tiny(HEADS)
        gss = tiny(TT * GROUPS)
        rb = tiny(EG + NE)
        lg = v3(tiny(TT * (EG + NE)), TT)
        gm, pg, gsm = tiny(TT), tiny(TT), tiny(TT)
        ohg = v3(tiny(TT * EG), TT)
        gtm = v3(tiny(TT * EG), TT)
        w8, oh1, oh2, t8 = (v3(tiny(TT * EPG), TT) for _ in range(4))
        v1, v2, e2, gate1, gate2 = (tiny(TT) for _ in range(5))
        route_area = area(acc_f[:, 0:D])
        wide = route_area(TT * NE)
        sel1, sel2, sel = (v3(route_area(TT * NE), TT) for _ in range(3))
        cnt, nblk = route_area(NE), route_area(NE)
        cumA, cumB = route_area(2 * NE), route_area(2 * NE)
        slot_of = v3(route_area(TT * NE), TT)
        dest = [tiny(TT) for _ in range(2)]
        be, slot_col = tiny(1), tiny(1)
        meta = tiny(P + 4, I32)
        in_last = tiny(1)
        npf, wrap = tiny(1), tiny(TT)
        pos_i, pos_f = tiny(TT, I32), tiny(TT)
        NI = ROPE // 2
        ang, rn, cosv, sinv = (v3(tiny(TT * NI), TT) for _ in range(4))
        mxs, sums, inverse = ([tiny(TT) for _ in range(m)] for m in (3, 3, 4))
        hss = tiny(40)

        def k_rows(w, cols):
            return w.rearrange("(k p) n -> p k n", p=P)[:, :, cols]

        w_ada, w_in, w_out = a["w_ada"][0], a["w_in"][0], a["w_out"][0]
        w13, w2 = a["w13"][0], a["w2"][0]
        w_in2, w_ukv, w_mkv = a["w_in_2"][0], a["w_ukv_2"][0], a["w_mem_kv_2"][0]
        w_o2, w_up, w_down = a["w_o_2"][0], a["w_up_2"][0], a["w_down_2"][0]

        def cols_of(n, k=KD):
            return lambda s: s[:, 0:k * n].rearrange("p (k n) -> p k n", k=k)

        block = ctx.enter_context(nc.Block())
        ADA1, ADA2 = range(0, 4), range(4, 12)
        IN_SLOTS = [(i * 512, min(512, IN1 - i * 512)) for i in range(6)]
        IN_ORDER = (2, 3, 4, 5, 0, 1)
        MEM_SLOTS = [(0, 512), (512, 512), (1024, 256)]
        BESIDE = [[("ada", 4), ("mk", 0), ("mk", 1), ("adaT", 4)], [("mv", 0, 0), ("mv", 0, 1), ("ada", 5), ("adaT", 5)],
                  [("ada", 6), ("mv", 1, 0), ("adaT", 6)], [("mv", 1, 1), ("ada", 7), ("adaT", 7)],
                  [("ada", 8), ("mv", 2, 0), ("adaT", 8)], [("mv", 2, 1), ("ada", 9), ("adaT", 9)],
                  [], [], [("ada", 10), ("adaT", 10), ("ada", 11), ("adaT", 11)]]
        LATE_A = [(O_MQ, 256), (O_GATE + 2048, 512), (O_GATE + 2560, 512), (O_GQ, 512), (O_GK, 512), (O_GA, 16),
                  (O_GV, 512), (O_GV + 512, 512), (O_GR, 512), (O_GR + 512, 512), (O_Q, 512), (O_Q + 512, 512),
                  (O_Q + 1024, 512), (O_CKV, 320), (O_GATE + 1024, 512), (O_GATE + 1536, 512), (O_GATE, 512)]
        LATE_B = [(O_GATE + 512, 512)]
        FFN_LOAD = len(LATE_A) + 1 + len(LATE_B) + 2
        FILL = [("gr", 0, 0), ("gr", 0, 1), ("gr", 1, 0), ("gr", 1, 1)] + [("q", n, t) for n in range(3) for t in range(2)] + [
            ("ckv", 0, 0), ("ckv", 0, 1)]
        SHARE = (1, 1, 2, 1, 1, 2, 1, 1, 2)
        FILLS = [FILL[sum(SHARE[:n]):sum(SHARE[:n + 1])] for n in range(LEVELS + 2)]
        @block.tensor
        def _(pe):
            mm = nc.tensor.matmul

            def transposes(ps, name, reader, pieces):
                bank = ps.fill(pe, name, reader)
                for src, col in pieces:
                    n, w = src.shape[0], src.shape[1]
                    last = nc.tensor.transpose(bank[0:w, col:col + n], src, ident[0:n, 0:n])
                ps.full(name, last)

            def all_channels(ps, name, src):
                for j in range(4):
                    transposes(ps, f"{name}{j}", ("dve", "act")[j % 2],
                               [(src[:, t, (2 * j + b) * P:(2 * j + b + 1) * P], b * T + t * P)
                                for b in range(2) for t in range(TT)])

            fresh = [None]

            def input_block(j):
                if fresh[0] and j % 2 == 0:
                    banks_, name, count = fresh[0]
                    banks_.wait_drained(pe, f"{name}{j // 2}")
                    if j == count - 2:
                        fresh[0] = None

            def tokens_out(ps, name, reader, lhs, w, width, col=0, k=KD):
                for t in range(TT):
                    bank = ps.fill(pe, f"{name}t{t}", reader)
                    for j in range(k):
                        input_block(j)
                        last = mm(bank[:, 0:width], lhs[:, j, t * P:t * P + P], w[:, j, col:col + width],
                                  start=(j == 0), stop=(j == k - 1))
                    ps.full(f"{name}t{t}", last)

            def channels_out(ps, name, reader, lhs, w, col):
                bank = ps.fill(pe, name, reader)
                for b in range(2):
                    for j in range(KD):
                        input_block(j)
                        last = mm(bank[:, b * T:b * T + T], w[:, j, col + b * P:col + b * P + P], lhs[:, j, :],
                                  start=(j == 0), stop=(j == KD - 1))
                ps.full(name, last)

            def by_tiles(ps, ring_, name, lhs, first=0):
                ws = [cols_of(512)(ring_.take(pe)) for _ in range(2)]
                for t in range(TT):
                    for n, w in enumerate(ws):
                        bank = ps.fill(pe, f"{name}{n}t{t}", "dve")
                        for j in range(KD):
                            input_block(j)
                            last = mm(bank[:, :], lhs[:, j, t * P:t * P + P], w[:, (j + first) % KD, :], start=(j == 0),
                                      stop=(j == KD - 1))
                        ps.full(f"{name}{n}t{t}", last)
                for n in range(2):
                    ring_.last_use(f"{name}{n}t{TT - 1}", ring_.taken - 2 + n)

            pe.wait_ge(ev("constants_loaded"), 16)
            pe.wait_ge(ev("param_rows_loaded"), 192)
            transposes(ps, "params", "dve", [(prm_rows[0:NROWS, 0:P], 0), (prm_rows[0:48, P:2 * P], NROWS)])

            def ada(n):
                w = cols_of(512)(ring.take(pe))
                if n == 0:
                    pe.wait_ge(ev("c_gated"), 1)
                bank = ps.fill(pe, f"ada{n}", "act")
                for k in range(KD):
                    g = k % 4
                    last = mm(bank[32 * g:32 * g + 32, :], cs[:, k:k + 1].to_broadcast([P, 32]), w[:, k, :],
                              start=(k < 4), stop=(k >= 4), tile_position=(0, 32 * g))
                ps.full(f"ada{n}", last)
                ring.last_use(f"ada{n}")

            def ada_spread(n):
                ps.wait_drained(pe, f"ada{n}")
                bank = ps.fill(pe, f"adaT{n}", "dve")
                if n // 2 in (2, 5):
                    last = mm(bank[:, :], C["quarters"].to_broadcast([P, P]), mrow[n % 2], start=True, stop=True)
                else:
                    for j in range(4):
                        last = mm(bank[:, j:j + 1], mrow[n % 2][:, j * P:j * P + P], C["quarters"],
                                  start=True, stop=True)
                ps.full(f"adaT{n}", last)

            for n in ADA1:
                ada(n)
                if n:
                    ada_spread(n - 1)
            ada_spread(ADA1[-1])

            pe.wait_ge(ev("x_normed"), 1)
            all_channels(ps, "h1", xn)
            fresh[0] = (ps, "h1", KD)
            for s_ in range(2, 6):
                wd = IN_SLOTS[s_][1]
                w = cols_of(wd)(ring.take(pe))
                channels_out(ps, f"xb{2 * (s_ - 2)}", "act", hT, w, 0)
                if s_ < 5:
                    channels_out(ps, f"xb{2 * (s_ - 2) + 1}", "act", hT, w, 256)
                    ring.last_use(f"xb{2 * (s_ - 2) + 1}")
                else:
                    bank = ps.fill(pe, "dt", "dve")
                    for t in range(TT):
                        for j in range(KD):
                            last = mm(bank[:, t * HEADS:(t + 1) * HEADS], hT[:, j, t * P:t * P + P],
                                      w[:, j, 256:256 + HEADS], start=(j == 0), stop=(j == KD - 1))
                    ps.full("dt", last)
                    ring.last_use("dt")
            pe.wait_ge(ev("mem_normed"), 1)
            all_channels(ps, "memT", mem_x)
            w = cols_of(512)(ring.take(pe))
            channels_out(ps, "u", "act", hT, w, 0)
            bank = ps.fill(pe, "z0", "act")
            for t in range(TT):
                for j in range(KD):
                    last = mm(bank[:, t * 256:t * 256 + 256], hT[:, j, t * P:t * P + P], w[:, j, 256:512],
                              start=(j == 0), stop=(j == KD - 1))
            ps.full("z0", last)
            ring.last_use("z0")
            pe.wait_ge(ev("decay_steps"), 1)
            bank = ps.fill(pe, "acs", "dve")
            for t in range(TT):
                mm(bank[:, t * HEADS:(t + 1) * HEADS], C["tri"], dta[:, t, :], start=True, stop=True)
            last = mm(bank[:, 2 * HEADS:3 * HEADS], ones, dta[:, 0, :], start=True, stop=True)
            ps.full("acs", last)

            def decay_rows(t):
                for g in range(GROUPS):
                    bank = ps.fill(pe, f"row{t}{g}", "dve")
                    for r in range(RPG):
                        h = RPG * g + r
                        last = mm(bank[:, r * P:r * P + P], dta[:, t, h:h + 1].to_broadcast([P, P]), C["tri"],
                                  start=True, stop=True)
                    ps.full(f"row{t}{g}", last)
            decay_rows(0)
            w = cols_of(512)(ring.take(pe))
            tokens_out(ps, "z1", "act", hT, w, 512)
            ring.last_use("z1t1")
            decay_rows(1)
            pe.wait_ge(ev("conv_gated"), 4)
            for t in range(TT):
                lots = ((0, 4), (4, 8), (8, 10)) if t == 0 else ((0, 4), (4, 6))
                for lo, hi in lots:
                    transposes(ps, f"xs{t}_{lo}", "act",
                               [(xb[:, k, t * P:t * P + P], (k - lo) * P) for k in range(lo, hi)])
            pe.wait_ge(ev("pool_weights_loaded"), 64)
            pe.wait_ge(ev("pooled"), 1)
            bank = ps.fill(pe, "pool", "act")
            for b in range(2):
                last = mm(bank[:, b * T:b * T + T], wpool[:, b, :], diff[:, b, :], start=True, stop=True)
            ps.full("pool", last)

            def beside(step):
                for what, n, *t in BESIDE[step]:
                    if what == "ada":
                        ada(n)
                    elif what == "adaT":
                        ada_spread(n)
                    else:
                        t, part, width, col = (n, 0, 256, 0) if what == "mk" else (
                            t[0], n, (256, 512, 256)[n], 256 if n == 0 else 0)
                        if t == 0 and (what == "mk" or n):
                            mem_w[part] = (cols_of(MEM_SLOTS[part][1])(ring.take(pe)), ring.taken - 1)
                        w, k = mem_w[part]
                        name = f"mk{t}" if what == "mk" else f"mv{n}{t}"
                        bank = ps.fill(pe, name, "dve" if what == "mk" else "act")
                        for j in range(KD):
                            last = mm(bank[:, 0:width], memT[:, j, t * P:t * P + P], w[:, j, col:col + width],
                                      start=(j == 0), stop=(j == KD - 1))
                        ps.full(name, last)
                        if t and what == "mv":
                            ring.last_use(name, k)
            mem_w = {}
            for j in range(4):
                ps.wait_drained(pe, f"memT{j}")
            beside(0)
            pe.wait_ge(ev("xcd_ready"), 1)
            for g in range(GROUPS):
                bank = ps.fill(pe, f"state{g}", "dve")
                last = mm(bank[:, 0:RPG * HD], xtok[:, 0, SSD_W + g * P:SSD_W + g * P + P],
                          xcd[:, g * RPG * HD:(g + 1) * RPG * HD], start=True, stop=True)
                ps.full(f"state{g}", last)

            def pair_products(n):
                t, g = divmod(n, GROUPS)
                bank = ps.fill(pe, f"cb{n}", "dve")
                last = mm(bank[:, 0:P], xb[:, 6 + g, t * P:t * P + P], xb[:, 10 + g, t * P:t * P + P],
                          start=True, stop=True)
                ps.full(f"cb{n}", last)
            pair_products(0)
            for n in range(TT * GROUPS):
                t, g = divmod(n, GROUPS)
                if n + 1 < TT * GROUPS:
                    pair_products(n + 1)
                if n:
                    beside(n)
                ps.wait_drained(pe, f"cb{n}")
                bank = ps.fill(pe, f"yd{n}", "dve")
                for r in range(RPG):
                    h = RPG * g + r
                    last = mm(bank[:, r * HD:r * HD + HD], seg2[n % 2][:, r, :], xdt[:, t, h * HD:h * HD + HD],
                              start=True, stop=True)
                ps.full(f"yd{n}", last)
                if t:
                    bank = ps.fill(pe, f"yo{g}", "dve")
                    last = mm(bank[:, 0:RPG * HD], xb[:, 10 + g, P:2 * P], prevT[:, g, :], start=True, stop=True)
                    ps.full(f"yo{g}", last)
            beside(TT * GROUPS)
            pe.wait_ge(ev("ssd_normed"), 1)
            for j in range(3):
                transposes(ps, f"yT{j}", "act", [(yv[:, t, (2 * j + b) * P:(2 * j + b + 1) * P], b * T + t * P)
                                                for b in range(2) for t in range(TT)])
            fresh[0] = (ps, "yT", 6)
            by_tiles(ps, ring, "mix", mixT, 2)
            pe.wait_ge(ev("x_normed"), 2)
            all_channels(ps, "h2", xn)
            fresh[0] = (ps, "h2", KD)
            pe.wait_ge(ev("router_loaded"), 32)
            tokens_out(ps, "router", "dve", hT, wr, EG + NE)
            pe.wait_ge(ev("chosen"), 1)
            bank = ps.fill(pe, "rank", "dve")
            mm(bank[:, 0:NE], C["strict"], sel[:, 0, :], start=True, stop=True)
            mm(bank[:, NE:2 * NE], ones, sel[:, 0, :], start=True, stop=False)
            mm(bank[:, NE:2 * NE], C["strict"], sel[:, 1, :], start=False, stop=True)
            mm(bank[:, 2 * NE:3 * NE], ones, sel[:, 0, :], start=True, stop=False)
            last = mm(bank[:, 2 * NE:3 * NE], ones, sel[:, 1, :], start=False, stop=True)
            ps.full("rank", last)
            pe.wait_ge(ev("block_experts"), 1)
            bank = ps.fill(pe, "experts", "dve")
            last = mm(bank[0:1, 0:P], be, ident, start=True, stop=True)
            ps.full("experts", last)

            pe.wait_ge(ev("routed"), 1)
            pairs = pe.value_load(meta[0:1, P:P + 1], min_val=4, max_val=MAXB // 2)
            last_pair = pe.value_load(meta[0:1, P + 1:P + 2], min_val=3, max_val=MAXB // 2 - 1)
            gA, gB, hA, hB, tA, tB, oA, oB = banks

            def gather(i):
                pe.wait_ge(ev("slots_picked"), i + 1)
                for k in range(KD):
                    dst = (gA, gB)[k // 4][:, (k % 4) * P:(k % 4) * P + P]
                    for t in range(TT):
                        last = mm(dst, xn[:, t, k * P:k * P + P], pick[:, t, :], start=(t == 0), stop=(t == TT - 1))
                    if k % 4 == 3:
                        last.then_inc(ev("gather_filled"), 1)

            def hidden(i):
                pe.wait_ge(ev("slots_in_by_act"), i + 1)
                pe.wait_ge(ev("slots_in_by_dve"), i + 1)
                pe.wait_ge(ev("hidden_out_by_act"), i)
                pe.wait_ge(ev("hidden_out_by_dve"), i)
                for part in range(2):
                    for b in range(2):
                        pe.wait_ge(xw_landed[3 * b + part], i * 16 + 16)
                    w = [slots[3 * b + part].rearrange("p (k n) -> p k n", k=4) for b in range(2)]
                    for k in range(4):
                        for n, dst in enumerate((hA, hB)):
                            for b in range(2):
                                last = mm(dst[SLOTS * b:SLOTS * b + SLOTS, :],
                                          xeT[:, 4 * part + k, b * SLOTS:b * SLOTS + SLOTS],
                                          w[b][:, k, n * 512:n * 512 + 512], start=(part == 0 and k == 0),
                                          stop=(part == 1 and k == 3))
                            if part and k == 3:
                                last.then_inc(ev("hidden_filled"), 1)
                    if part == 0:
                        last.then_inc(ev("first_halves_used"), 1)

            def hidden_transposes(i):
                pe.wait_ge(ev("hidden_out_by_act"), i + 1)
                pe.wait_ge(ev("hidden_out_by_dve"), i + 1)
                pe.wait_ge(ev("hidden_gated"), i)
                for f in range(8):
                    last = nc.tensor.transpose((tA, tB)[f // 4][:, (f % 4) * P:(f % 4) * P + P], hs[:, f * P:f * P + P],
                                               ident)
                    if f % 4 == 3:
                        last.then_inc(ev("hidden_transposed"), 1)

            def rows_out(m, at_end=False):
                pe.wait_ge(ev("hidden_gated"), m + 1)
                pe.wait_ge(ev("parts_added"), m * 4 + 1)
                at = [3 * b + (0 if at_end else 2) for b in range(2)]
                for s_ in at:
                    pe.wait_ge(xw_landed[s_], m * 16 + (32 if at_end else 16))
                w = [slots[s_].rearrange("p (k n) -> p k n", k=4) for s_ in at]
                for n_, dst in enumerate((oA, oB)):
                    for f in range(4):
                        for b in range(2):
                            last = mm(dst[SLOTS * b:SLOTS * b + SLOTS, :], sT[:, f * P + b * SLOTS:f * P + b * SLOTS + SLOTS],
                                      w[b][:, f, n_ * 512:n_ * 512 + 512], start=(f == 0), stop=(f == 3))
                    last.then_inc(ev(("rows_filled_for_act", "rows_filled_for_dve")[n_]), 1)

            def combine(m, t):
                if t == 0:
                    pe.wait_ge(ev("rows_out_by_act"), m + 1)
                    pe.wait_ge(ev("rows_out_by_dve"), m + 1)
                    pe.wait_ge(ev("shares_ready"), m + 1)
                else:
                    pe.wait_ge(ev("parts_added"), m * 4 + 3)
                for n_, dst in enumerate((oA, oB)):
                    mm(dst[:, :], share_f[:, t * P:t * P + P], osb[:, n_ * 512:n_ * 512 + 512], start=True,
                       stop=True).then_inc(ev("parts_filled"), 1)

            for r in ("dve", "act"):
                pe.wait_ge(ps.drained[r], ps.count[r])
            pe.sem_inc(ev("parts_filled"), 1)
            gather(0)
            hidden(0)
            hidden_transposes(0)
            gather(1)
            for n, dst in enumerate((oA, oB)):
                pe.wait_ge(ev("columns_spread"), 4 * n + 4)
                for m in range(4):
                    last = mm(dst[:, m * P:m * P + P], ones, diag[:, 4 * n + m, :], start=True, stop=True)
                last.then_inc(ev("lead_filled"), 1)
            with pe.Fori(1, pairs) as i:
                hidden(i)
                rows_out(i - 1)
                hidden_transposes(i)
                combine(i - 1, 0)
                gather(i + 1)
                combine(i - 1, 1)
            rows_out(last_pair, True)
            pe.wait_ge(ev("mem_keys_normed"), 1)
            pe.wait_ge(ev("hidden_gated"), pairs)
            for b in range(2):
                for t in range(TT):
                    last = nc.tensor.transpose(tA[:, b * T + t * P:b * T + t * P + P],
                                               mk[:, t * EH * EQ + b * P:t * EH * EQ + b * P + P], ident)
            last.then_inc(ev("mem_keys_transposed"), 1)
            combine(last_pair, 0)
            combine(last_pair, 1)

            def softmax_products(name, qs, ks, causal):
                bank = ps2.fill(pe, f"s_{name}", "dve")
                for t in range(TT):
                    at, w = ((0, P), (P, T))[t] if causal else (t * T, T)
                    n = len(qs)
                    for m, (qa, ka) in enumerate(zip(qs, ks)):
                        last = mm(bank[:, at:at + w], qa[:, t * P:t * P + P], ka[:, 0:w], start=(m == 0), stop=(m == n - 1))
                ps2.full(f"s_{name}", last)

            def pieces(causal):
                return ((0, 0), (1, 0), (1, 1)) if causal else ((0, 0), (0, 1), (1, 0), (1, 1))

            def softmax_transposes(name, idx, causal):
                pe.wait_ge(ev("probs_ready"), idx + 1)
                transposes(ps2, f"pT_{name}", "act", [(pr[idx % 3][:, n * P:n * P + P], n * P)
                                                     for n in range(len(pieces(causal)))])

            def softmax_values(name, idx, value, width, causal):
                ps2.wait_drained(pe, f"pT_{name}")
                bank = ps2.fill(pe, f"o_{name}", "act")
                for n, (t, k) in enumerate(pieces(causal)):
                    last = mm(bank[:, t * width:t * width + width], pT[idx % 2][:, n * P:n * P + P], value(k),
                              start=(k == 0), stop=(k == 1 or (causal and t == 0)))
                ps2.full(f"o_{name}", last)

            def attention(heads, args, first, value, width, causal, fill=()):
                for h in range(heads + 3):
                    if h < heads:
                        softmax_products(f"{first + h}", *args(h), causal)
                    if h < len(fill):
                        fill[h]()
                    if 2 <= h < heads + 2:
                        softmax_transposes(f"{first + h - 2}", first + h - 2, causal)
                    if h >= 3:
                        softmax_values(f"{first + h - 3}", first + h - 3, value(h - 3), width, causal)

            def gate(br, n):
                w = cols_of(512)(ring2.take(pe))
                tokens_out(ps2, f"gate{br}{n}", "dve", hT, w, 512)
                ring2.last_use(f"gate{br}{n}t1")

            pe.wait_ge(ev("mem_keys_out"), 1)
            pe.wait_ge(ev("parts_added"), pairs * 4 + 1)
            pe.wait_ge(ev("x_normed"), 3)
            all_channels(ps2, "h3", xn)
            fresh[0] = (ps2, "h3", KD)
            w = cols_of(256)(ring2.take(pe))
            tokens_out(ps2, "mq", "dve", hT, w, 256)
            ring2.last_use("mqt1")
            for n in range(2):
                gate(2, n)
            pe.wait_ge(ev("mem_q_normed"), 1)
            transposes(ps2, "mqT", "act", [(qm[:, t, b * P:b * P + P], b * T + t * P)
                                           for b in range(2) for t in range(TT)])
            ps2.wait_drained(pe, "mqT")

            def gla_channels(nm, b):
                if b == 0:
                    taken[0] = cols_of(512)(ring2.take(pe))
                channels_out(ps2, f"{nm}{b}", "act", hT, taken[0], b * 256)
                if b:
                    ring2.last_use(f"{nm}1")
            taken = [None]
            attention(EH, lambda h: ([qmT[64 * (h % 2):64 * (h % 2) + 64, h // 2, :]],
                                     [kmT[64 * (h % 2):64 * (h % 2) + 64, h // 2, :]]), 0,
                      lambda h: lambda k: vm[:, k, h * EV:h * EV + EV], EV, False,
                      [lambda nm=nm, b=b: gla_channels(nm, b) for nm in ("gq", "gk") for b in range(2)])
            w = cols_of(GRANK)(ring2.take(pe))
            bank = ps2.fill(pe, "ga", "act")
            for j in range(KD):
                last = mm(bank[0:GRANK, 0:T], w[:, j, :], hT[:, j, :], start=(j == 0), stop=(j == KD - 1))
            ps2.full("ga", last)
            ring2.last_use("ga")
            for n in range(2):
                w = cols_of(512)(ring2.take(pe))
                tokens_out(ps2, f"gv{n}", "act", hT, w, 512)
                ring2.last_use(f"gv{n}t1")
                if n == 0:
                    ps2.wait_drained(pe, "ga")
                    pe.wait_ge(ev("gla_rows_loaded"), 48)
                    for t in range(TT):
                        bank = ps2.fill(pe, f"lg{t}", "dve")
                        last = mm(bank[:, :], gaT[0:GRANK, t * P:t * P + P], wgate[0:GRANK, :], start=True, stop=True)
                        ps2.full(f"lg{t}", last)
            def fill(lvl):
                for nm, n, t in FILLS[lvl]:
                    width = 320 if nm == "ckv" else 512
                    if t == 0:
                        taken[0] = cols_of(width)(ring2.take(pe))
                    bank = ps2.fill(pe, f"{nm}{n}t{t}", "act")
                    for j in range(KD):
                        last = mm(bank[:, 0:width], hT[:, j, t * P:t * P + P], taken[0][:, j, :], start=(j == 0),
                                  stop=(j == KD - 1))
                    ps2.full(f"{nm}{n}t{t}", last)
                    if t:
                        ring2.last_use(f"{nm}{n}t1")
            fill(0)
            pe.wait_ge(ev("log_decays"), 1)
            for j in range(2):
                bank = ps2.fill(pe, f"cum{j}", "act")
                for b in range(2):
                    for t in range(TT):
                        h = 2 * j + b
                        last = mm(bank[:, b * T + t * P:b * T + t * P + P], la[:, t, h * DK:h * DK + DK], C["tri"],
                                  start=True, stop=True)
                ps2.full(f"cum{j}", last)
            for lvl in range(LEVELS + 1):
                if lvl == 0:
                    ps2.wait_drained(pe, "gk1")
                else:
                    fill(lvl)
                    pe.wait_ge(ev("level_ready"), lvl)
                for t in range(TT):
                    bank = ps2.fill(pe, f"lvl{lvl}{t}", "dve")
                    for h in range(GH):
                        k_ = (gkT if lvl == 0 else qk)[:, h, t * P:t * P + P]
                        q_ = (gqT if lvl == 0 else qk)[:, h, t * P:t * P + P]
                        last = mm(bank[:, h * P:h * P + P], k_, q_, start=True, stop=True)
                    ps2.full(f"lvl{lvl}{t}", last)
            fill(LEVELS + 1)
            pe.wait_ge(ev("level_ready"), LEVELS + 1)
            bank = ps2.fill(pe, "cross", "act")
            for h in range(GH):
                last = mm(bank[:, h * P:h * P + P], qk[:, h, 0:P], qk[:, h, P:2 * P], start=True, stop=True)
            ps2.full("cross", last)
            ps2.wait_drained(pe, f"lvl{LEVELS}1")
            ps2.wait_drained(pe, "cross")
            for h in range(GH):
                bank = ps2.fill(pe, f"go{h}", "dve")
                mm(bank[:, 0:DV], att[0][:, h, :], gv[:, 0, h * DV:h * DV + DV], start=True, stop=True)
                mm(bank[:, DV:2 * DV], att[2][:, h, :], gv[:, 0, h * DV:h * DV + DV], start=True, stop=False)
                last = mm(bank[:, DV:2 * DV], att[1][:, h, :], gv[:, 1, h * DV:h * DV + DV], start=False, stop=True)
                ps2.full(f"go{h}", last)
            gate(1, 0)
            gate(1, 1)
            gate(0, 0)
            pe.wait_ge(ev("ckv_normed"), 1)
            transposes(ps2, "ckT", "act", [(ckv[t][:, 0, b * P:b * P + P], b * T + t * P)
                                           for b in range(2) for t in range(TT)])
            ps2.wait_drained(pe, "ckT")
            w = cols_of(2048, 2)(ring2.take(pe))
            for n in range(4):
                tokens_out(ps2, f"kv{n}", "act", ckT, w, 512, col=n * 512, k=2)
            ring2.last_use("kv3t1")
            gate(0, 1)
            pe.wait_ge(ev("rope_k_ready"), 1)
            transposes(ps2, "krT", "act", [(kr2[:, t, :], t * P) for t in range(TT)])
            pe.wait_ge(ev("mla_q_ready"), 1)
            for j in range(4):
                transposes(ps2, f"qnT{j}", "act", [(q[t][:, (2 * j + b) * 192:(2 * j + b) * 192 + P], b * T + t * P)
                                                  for b in range(2) for t in range(TT)])
            for j in range(2):
                transposes(ps2, f"qrT{j}", "act", [(ropeb[:, t, (2 * j + b) * P:(2 * j + b + 1) * P], b * T + t * P)
                                                  for b in range(2) for t in range(TT)])
            pe.wait_ge(ev("mla_k_ready"), 1)
            for j in range(4):
                transposes(ps2, f"knT{j}", "act",
                           [(kv[:, t, (2 * j + b) * 256:(2 * j + b) * 256 + P], b * T + t * P)
                            for b in range(2) for t in range(TT)])
            for j in range(4):
                ps2.wait_drained(pe, f"knT{j}")

            def mla_args(h):
                lo = 64 * (h % 2)
                return ([qnT[:, h, :], qrT[lo:lo + 64, h // 2, :]], [knT[:, h, :], krT[lo:lo + 64, :]])
            attention(MH, mla_args, EH, lambda h: lambda k: kv[:, k, h * 256 + P:h * 256 + 256], VD, True)
            pe.wait_ge(ev("branches_summed"), 1)
            all_channels(ps2, "ysT", ysum)
            fresh[0] = (ps2, "ysT", KD)
            by_tiles(ps2, ring2, "wo", hT)
            pe.wait_ge(ev("x_normed"), 4)
            for j in range(4):
                transposes(ps2, f"h4{j}", "dve", [(xn[:, t, (2 * j + b) * P:(2 * j + b + 1) * P], b * T + t * P)
                                                 for b in range(2) for t in range(TT)])
            fresh[0] = (ps2, "h4", KD)

            def parts(n, k, width):
                ring2.take(pe)
                low = low_slots[(FFN_LOAD + n) % 4]
                pe.wait_ge(ev("low_parts"), n + 1)
                return cols_of(width, k)(high_slots[n % 2]), cols_of(width, k)(low)

            for n in range(8):
                wH, wL = parts(n, KD, 512)
                for b in range(2):
                    bank = ps2.fill(pe, f"up{n}{b}", "act")
                    for c in range(2):
                        for j in range(KD):
                            input_block(j)
                            at = (2 * b + c) * P
                            for m, (w_, h_) in enumerate(((wH, hH), (wH, hL), (wL, hH))):
                                last = mm(bank[:, c * T:c * T + T], w_[:, j, at:at + P], h_[:, j, :],
                                          start=(j == 0 and m == 0), stop=(j == KD - 1 and m == 2))
                    ps2.full(f"up{n}{b}", last)
                ring2.last_use(f"up{n}1")
            accs = [ps2.fill(pe, f"down{t}{n}", "dve") for t in range(TT) for n in range(2)]
            for g in range(8):
                wH, wL = parts(8 + g, 4, D)
                pe.wait_ge(ev("ffn_squared"), 2 * g + 2)
                for m, acc_ in enumerate(accs):
                    t, n = m // 2, m % 2
                    for j in range(4):
                        for i_, (a_, w_) in enumerate(((aH, wH), (aH, wL), (aL, wH))):
                            last = mm(acc_[:, :], a_[g][:, j, t * P:t * P + P], w_[:, j, n * 512:n * 512 + 512],
                                      start=(g == 0 and j == 0 and i_ == 0), stop=(g == 7 and j == 3 and i_ == 2))
                    if g == 7:
                        ps2.full(f"down{t}{n}", last)
                    elif m == 3:
                        last.then_inc(ev("down_weights_used"), 1)
                ring2.last_use((ev("down_weights_used"), g + 1))
        @block.scalar
        def _(act):
            do = Chained(act, ev("act_step"))
            A = nc.scalar.activation

            def raise_(name):
                act.sem_inc(ev(name), 1)

            def drain(ps, name, pairs, scale=None, shift=None):
                bank = ps.read(act, name, "act")
                for n, (dst, src) in enumerate(pairs(bank)):
                    sc, sh = (scale[n] if scale else 1.0), (shift[n] if shift else 0.0)
                    ins = A(dst, src, ACT.Identity, bias=sh, scale=sc)
                    if n == len(pairs(bank)) - 1:
                        ps.release(name, ins, act)
                    else:
                        do(ins)

            def to_channels(ps, name, dst, scale, shift):
                for j in (1, 3):
                    drain(ps, f"{name}{j}", lambda bank: [(dst[:, 2 * j + b, :], bank[:, b * T:b * T + T]) for b in range(2)],
                          [scale if isinstance(scale, float) else scale[:, 2 * j + b:2 * j + b + 1] for b in range(2)],
                          [shift[:, 2 * j + b:2 * j + b + 1] for b in range(2)] if shift is not None else None)

            ps.wait_drained(act, "params")
            do(A(ctmp, prm[:, 0:8], ACT.Tanh, scale=0.5))
            raise_("c_tanh")
            act.wait_ge(ev("x_loaded"), 16)
            for t in range(TT):
                do(A(hT_sb[:, 0:D], x[:, t, :], ACT.Square, accum_out=ss[:, t:t + 1]))
                raise_("squares")
            def ada_row(n):
                drain(ps, f"ada{n}", lambda bank: [(mrow[n % 2], bank[:, :])])
            for n in ADA1:
                ada_row(n)
            ps.wait_drained(act, "adaT3")
            to_channels(ps, "h1", hT, modc[:, 8:16], modc[:, 0:8])
            act.wait_ge(ev("memory_loaded"), 16)
            act.wait_ge(ev("x_normed"), 1)
            for t in range(TT):
                do(A(ring_mem[:, 4 * 4096:4 * 4096 + D], mem_x[:, t, :], ACT.Square, accum_out=ss[:, t:t + 1]))
                raise_("squares")
            act.wait_ge(ev("pads_zeroed"), 1)
            for n in range(4):
                for j in (2 * n, 2 * n + 1):
                    if j < 7:
                        drain(ps, f"xb{j}", lambda bank: [(raw[:, 2 * j:2 * j + 2, 3:3 + T], v3(bank[:, :], 2))])
                act.wait_ge(ev("conv_batch"), n + 1)
                w = 4 if n < 3 else 2
                do(A(ce[:, 0:w, :], cv[:, 0:w, :], ACT.Tanh))
                raise_("conv_tanh")
            act.wait_ge(ev("dt_abs"), 1)
            do(A(flat(dta), flat(dta), ACT.Exp, scale=-1.0))
            do(A(flat(dta), flat(dta), ACT.Ln, bias=1.0))
            do(A(nega, alog_b, ACT.Exp))
            raise_("dt_log")
            to_channels(ps, "memT", memT, prm[:, ROWS["g_mem"]:ROWS["g_mem"] + 8], None)
            drain(ps, "u", lambda bank: [(uT[:, :, PAD:PAD + T], v3(bank[:, :], 2))])
            drain(ps, "z0", lambda bank: [(z[:, :, 0:256], v3(bank[:, :], 2))], [0.5])
            act.wait_ge(ev("decay_sums"), 1)
            do(A(dte, dte, ACT.Exp))
            do(A(eacs, acs[:, 1, :], ACT.Exp))
            raise_("decay_exps")

            def segment_exps(t):
                for g in range(GROUPS):
                    n = t * GROUPS + g
                    act.wait_ge(ev("segment_sums"), n + 1)
                    do(A(segs[n], segs[n], ACT.Exp))
                    raise_("segment_exps")
            segment_exps(0)
            for t in range(TT):
                drain(ps, f"z1t{t}", lambda bank: [(z[:, t, 256:768], bank[:, :])], [0.5])
            act.wait_ge(ev("conv_gated"), 4)
            for t in range(TT):
                if t:
                    segment_exps(1)
                for lo, hi in (((0, 4), (4, 8), (8, 10)) if t == 0 else ((0, 4), (4, 6))):
                    drain(ps, f"xs{t}_{lo}", lambda bank: [(xtok[:, t, lo * P:hi * P], bank[:, 0:(hi - lo) * P])])
            for t in range(TT):
                do(A(zt[t], z[:, t, :], ACT.Tanh))
            raise_("z_tanh")
            drain(ps, "pool", lambda bank: [(mixT[:, 6 + b, :], bank[:, b * T:b * T + T]) for b in range(2)],
                  [prm[:, ROWS["pool_scale"] + b:ROWS["pool_scale"] + b + 1] for b in range(2)])
            for step in BESIDE:
                for what, n, *t in step:
                    if what == "ada":
                        ada_row(n)
                    elif what == "mv":
                        lo, w = ((0, 256), (256, 512), (768, 256))[n]
                        drain(ps, f"mv{n}{t[0]}", lambda bank: [(vm[:, t[0], lo:lo + w], bank[:, 0:w])])
            for j in range(3):
                drain(ps, f"yT{j}", lambda bank: [(mixT[:, 2 * j + b, :], bank[:, b * T:b * T + T]) for b in range(2)],
                      [prm[:, ROWS["ssd_norm_w"] + 2 * j + b:ROWS["ssd_norm_w"] + 2 * j + b + 1] for b in range(2)])
            for t in range(TT):
                act.wait_ge(ev("x_updated"), t + 1)
                do(A(raw_f[:, 0:D], x[:, t, :], ACT.Square, accum_out=ss[:, t:t + 1]))
                raise_("squares")
            to_channels(ps, "h2", hT, modc[:, 32:40], modc[:, 24:32])
            act.wait_ge(ev("group_shifted"), 1)
            do(A(flat(gtm), flat(gtm), ACT.Exp))
            raise_("group_exps")
            act.wait_ge(ev("top_gap"), 1)
            do(A(e2, v2, ACT.Exp))
            raise_("top_exp")

            act.wait_ge(ev("routed"), 1)
            pairs = act.value_load(meta[0:1, P:P + 1], min_val=4, max_val=MAXB // 2)
            last_pair = act.value_load(meta[0:1, P + 1:P + 2], min_val=3, max_val=MAXB // 2 - 1)
            gA, gB, hA, hB, tA, tB, oA, oB = banks

            def slots_in(i, lc):
                act.wait_ge(ev("gather_filled"), i * 2 + 1)
                for k in range(4):
                    ins = A(xeT[:, k, :], gA[:, k * P:k * P + P], ACT.Identity, scale=modc[:, 32 + k:33 + k],
                            bias=modc[:, 24 + k:25 + k])
                    if k < 3:
                        lc(ins)
                ins.then_inc(ev("slots_in_by_act"), 1)

            def hidden_out(i):
                act.wait_ge(ev("hidden_filled"), i * 2 + 1)
                A(hs[:, 0:512], hA[:, :], ACT.Identity).then_inc(ev("hidden_out_by_act"), 1)

            def gate_tanh(i):
                act.wait_ge(ev("hidden_transposed"), i * 2 + 1)
                A(ge, tA[:, :], ACT.Tanh, scale=0.5).then_inc(ev("gate_tanhs"), 1)

            def rows_out(m):
                act.wait_ge(ev("rows_filled_for_act"), m + 1)
                act.wait_ge(ev("parts_filled"), m * 4 + 1)
                A(osb[:, 0:512], oA[:, :], ACT.Identity).then_inc(ev("rows_out_by_act"), 1)

            def turn(i, lc, first):
                hidden_out(i)
                if not first:
                    rows_out(i - 1)
                gate_tanh(i)
                slots_in(i + 1, lc)
                if first:
                    act.wait_ge(ev("lead_filled"), 2)
                    lc(A(gate_rows, oB[:, :], ACT.Identity))
                    act.sem_inc(ev("lead_out"), 1)

            lead = Chained(act, ev("act_lead_step"))
            slots_in(0, lead)
            turn(0, lead, True)
            with act.Fori(1, pairs) as i:
                lc = LoopChained(act, ev("act_expert_step"), i, 3)
                turn(i, lc, False)
                lc.end()
            rows_out(last_pair)
            act.wait_ge(ev("mem_keys_transposed"), 1)
            A(flat(kmT), tA[:, :], ACT.Identity).then_inc(ev("mem_keys_out"), 1)

            for t in range(TT):
                act.wait_ge(ev("x_updated"), TT + t + 1)
                do(A(hT_sb[:, 0:D], x[:, t, :], ACT.Square, accum_out=ss[:, t:t + 1]))
                raise_("squares")
            for t in range(TT):
                act.wait_ge(ev("x_updated"), 2 * TT + t + 1)
                do(A(hT_sb[:, 0:D], acc[:, t, :], ACT.Square, accum_out=ss_w[:, t:t + 1]))
                raise_("squares")
            to_channels(ps2, "h3", hT, prm[:, ROWS["g_mix"]:ROWS["g_mix"] + 8], None)
            act.wait_ge(ev("angles_ready"), 1)
            do(A(flat(sinv), flat(ang), ACT.Sin))
            do(A(flat(cosv), flat(rn), ACT.Sin))
            raise_("rope_tables")
            def gate_tanhs(name, buf, cols=None):
                act.wait_ge(ev(f"gate_logits_{name}"), 1)
                for t in range(TT):
                    v_ = buf[:, t, :] if cols is None else buf[:, t, cols]
                    do(A(v_, v_, ACT.Tanh, scale=0.5))
                raise_(f"gate_tanhs_{name}")
            gate_tanhs("2", gates2)
            drain(ps2, "mqT", lambda bank: [(flat(qmT), bank[:, :])])

            def attention(heads, first, scale, causal, width, fill=()):
                for h in range(heads + 3):
                    if h < len(fill):
                        fill[h]()
                    if 2 <= h < heads + 2:
                        w = 3 * P if causal else 4 * P
                        drain(ps2, f"pT_{first + h - 2}", lambda bank: [(pT[(first + h - 2) % 2][:, 0:w], bank[:, 0:w])])
                    if h < heads:
                        n = first + h
                        act.wait_ge(ev("scores_maxed"), n + 1)
                        for t in range(TT):
                            at, w = ((0, P), (P, T))[t] if causal else (t * T, T)
                            v_ = pr[n % 3][:, at:at + w]
                            do(A(v_, v_, ACT.Exp, bias=mxs[n % 3][:, t:t + 1], scale=scale,
                                 accum_out=sums[n % 3][:, t:t + 1]))
                        raise_("probs_ready")
                    if h >= 3:
                        n = first + h - 3
                        act.wait_ge(ev("sums_inverted"), n + 1)
                        drain(ps2, f"o_{n}", lambda bank: [(obr[:, t, (h - 3) * width:(h - 2) * width],
                                                            bank[:, t * width:(t + 1) * width]) for t in range(TT)],
                              [inverse[n % 4][:, t:t + 1] for t in range(TT)])

            def gla_channels(nm, dst, b, scale):
                drain(ps2, f"{nm}{b}", lambda bank: [(flat(dst)[:, b * 512:b * 512 + 512], bank[:, :])], [scale])
            attention(EH, 0, EQ ** -0.5, False, EV,
                      [lambda nm=nm, dst=dst, b=b, s_=s_: gla_channels(nm, dst, b, s_)
                       for nm, dst, s_ in (("gq", gqT, DK ** -0.5), ("gk", gkT, 1.0)) for b in range(2)])
            drain(ps2, "ga", lambda bank: [(gaT[0:GRANK, :], bank[0:GRANK, 0:T])])
            for n in range(2):
                for t in range(TT):
                    drain(ps2, f"gv{n}t{t}", lambda bank: [(gv[:, t, n * 512:n * 512 + 512], bank[:, :])])
            act.wait_ge(ev("log_arg"), 1)
            do(A(flat(lt), flat(lt), ACT.Exp, scale=-1.0))
            do(A(flat(lt), flat(lt), ACT.Ln, bias=1.0))
            raise_("log_done")
            def fill_drains(lvl):
                for nm, n, t in FILLS[lvl]:
                    if nm == "gr":
                        drain(ps2, f"gr{n}t{t}", lambda bank: [(gr[:, t, n * 512:n * 512 + 512], bank[:, :])], [0.5])
                    elif nm == "q":
                        drain(ps2, f"q{n}t{t}", lambda bank: [(q[t][:, n * 512:n * 512 + 512], bank[:, :])])
                    else:
                        drain(ps2, f"ckv0t{t}", lambda bank: [(ckv[t][:, 0, :], bank[:, 0:KVR + ROPE])])
            act.wait_ge(ev("gate_2_added"), 1)
            fill_drains(0)
            for j in range(2):
                drain(ps2, f"cum{j}", lambda bank: [(flat(gbT)[:, j * 512:j * 512 + 512], bank[:, :])])
            for lvl in range(1, LEVELS + 2):
                act.wait_ge(ev("level_differences"), lvl)
                do(A(flat(lev), flat(lev), ACT.Exp))
                raise_("level_exps")
                fill_drains(lvl)
            raise_("latents_out")
            for t, e_ in enumerate((flat(la), flat(lt))):
                do(A(e_, gr[:, t, :], ACT.Tanh))
            raise_("r_tanh")
            drain(ps2, "cross", lambda bank: [(flat(att[2]), bank[:, :])])
            act.wait_ge(ev("gla_summed"), 1)
            for t, sq_ in enumerate((gqT, gkT)):
                do(A(flat(sq_), obr[:, t, :], ACT.Square))
            raise_("gla_squares")
            gate_tanhs("1", gates1)
            act.wait_ge(ev("gla_done"), 1)
            for t in range(TT):
                do(A(qsqs[t], q[t], ACT.Square))
            raise_("q_squares")
            drain(ps2, "ckT", lambda bank: [(ckT[:, b, :], bank[:, b * T:b * T + T]) for b in range(2)],
                  [prm[:, ROWS["g_ckv"] + b:ROWS["g_ckv"] + b + 1] for b in range(2)])
            for n in range(4):
                for t in range(TT):
                    drain(ps2, f"kv{n}t{t}", lambda bank: [(kv[:, t, n * 512:n * 512 + 512], bank[:, :])])
            for t in range(TT):
                do(A(v3(ksqs[t], MH), v3(kv[:, t, :], MH)[:, :, 0:NOPE], ACT.Square))
            raise_("k_squares")
            gate_tanhs("0a", gates0, slice(0, 512))
            drain(ps2, "krT", lambda bank: [(krT, bank[:, 0:T])])
            for j in range(4):
                drain(ps2, f"qnT{j}", lambda bank: [(flat(qnT)[:, j * 512:j * 512 + 512], bank[:, :])],
                      [prm[:, ROWS["g_q_nope"]:ROWS["g_q_nope"] + 1]])
            for j in range(2):
                drain(ps2, f"qrT{j}", lambda bank: [(flat(qrT)[:, j * 512:j * 512 + 512], bank[:, :])])
            for j in range(4):
                drain(ps2, f"knT{j}", lambda bank: [(flat(knT)[:, j * 512:j * 512 + 512], bank[:, :])],
                      [prm[:, ROWS["g_k_nope"]:ROWS["g_k_nope"] + 1]])
            gate_tanhs("0b", gates0, slice(512, 1024))
            attention(MH, EH, (NOPE + ROPE) ** -0.5, True, VD)
            to_channels(ps2, "ysT", hT, 0.5, None)
            def high_part(n):
                k = FFN_LOAD + n
                act.wait_ge(ring2.landed[k % 4], 16 * (k // 4 + 1))
                if n >= 2:
                    ring2.wait_used(act, k - 2)
                do(A(high_slots[n % 2], slots[k % 4], ACT.Identity))
                raise_("high_parts")
            high_part(0)
            high_part(1)
            for t in range(TT):
                act.wait_ge(ev("x_updated"), 3 * TT + t + 1)
                do(A(fnw[:, :], x[:, t, :], ACT.Square, accum_out=ss[:, t:t + 1]))
                raise_("squares")
            for j in range(4):
                ps2.wait_filled(act, f"h4{j}")
                bank = ps2.banks[ps2.by[f"h4{j}"][0]]
                for b in range(2):
                    c = 2 * j + b
                    do(A(hH[:, c, :], bank[:, b * T:b * T + T], ACT.Identity,
                         scale=prm[:, ROWS["g_ffn"] + c:ROWS["g_ffn"] + c + 1]))
                raise_("ffn_input_high")
            for n in range(8):
                for b in range(2):
                    m = 2 * n + b
                    if m >= 2:
                        act.wait_ge(ev("ffn_squared"), m - 1)
                    bank = ps2.read(act, f"up{n}{b}", "act")
                    ps2.release(f"up{n}{b}", A(relu[b], bank[:, :], ACT.Relu), act)
                    do(A(flat(aH[n])[:, b * 512:b * 512 + 512], relu[b], ACT.Square))
                    raise_("ffn_high")
                high_part(n + 2)
            for n in range(10, 16):
                high_part(n)
        @block.vector
        def _(dve):
            do = Chained(dve, ev("dve_step"))
            spread = Signal(ev("columns_spread"))
            V = nc.vector

            def raise_(name):
                dve.sem_inc(ev(name), 1)

            def ts(out_, in_, s1, op0, s2=None, op1=ALU.bypass):
                return V.tensor_scalar(out_, in_, s1, s2, op0, op1)

            def tt(out_, x_, y_, op):
                return V.tensor_tensor(out_, x_, y_, op)

            def stt(out_, x_, s_, y_, op0, op1):
                return V.scalar_tensor_tensor(out_, x_, s_, y_, op0, op1)

            def rsqrt(dst, n, sums_, width):
                v, w = rt[0][:, 0:n], rt[1][:, 0:n]
                at = 0
                for m, wd in (width if isinstance(width, list) else [(n, width)]):
                    do(ts(v[:, at:at + m], sums_[:, at:at + m], 1.0 / wd, ALU.mult, EPS, ALU.add))
                    at += m
                do(ts(w.bitcast(I32), v.bitcast(I32), 1, ALU.logical_shift_right))
                do(ts(dst.bitcast(I32), w.bitcast(I32), -1.0, ALU.mult, 1597463007.0, ALU.add))
                for _ in range(3):
                    do(tt(w, dst, dst, ALU.mult))
                    do(stt(w, w, -0.5, v, ALU.mult, ALU.mult))
                    do(stt(dst, w, 1.5, dst, ALU.add, ALU.mult))

            def times_sigmoid(dst, tanh_half, y_):
                do(stt(dst, tanh_half, 1.0, y_, ALU.add, ALU.mult))

            def to_channels(ps, name, dst, scale, shift):
                for j in (0, 2):
                    bank = ps.read(dve, f"{name}{j}", "dve")
                    for b in range(2):
                        c = 2 * j + b
                        o_, i_ = dst[:, c, :], bank[:, b * T:b * T + T]
                        if shift is not None:
                            ins = ts(o_, i_, scale[:, c:c + 1], ALU.mult, shift[:, c:c + 1], ALU.add)
                        elif scale is not None:
                            ins = ts(o_, i_, scale if isinstance(scale, float) else scale[:, c:c + 1], ALU.mult)
                        else:
                            ins = V.tensor_copy(o_, i_)
                        if b:
                            ps.release(f"{name}{j}", ins, dve)
                        else:
                            do(ins)

            norm_no = [0]

            def normalize(dst, src, tiles=range(TT)):
                norm_no[0] += len(tiles)
                dve.wait_ge(ev("squares"), norm_no[0])
                cols = slice(tiles[0], tiles[-1] + 1)
                rsqrt(rs[:, cols], len(tiles), ss[:, cols], D)
                for t in tiles:
                    do(ts(dst[:, t, :], src[:, t, :], rs[:, t:t + 1], ALU.mult))

            bank = ps.read(dve, "params", "dve")
            ps.release("params", V.tensor_copy(prm[:, :], bank[:, 0:NROWS + 48]), dve)
            do(ts(cs, prm[:, 0:8], 0.5, ALU.mult))
            dve.wait_ge(ev("c_tanh"), 1)
            times_sigmoid(cs, ctmp, cs)
            raise_("c_gated")
            halved = prm[:, ROWS["conv_w"]:ROWS["conv_b"] + NXB]
            do(ts(halved, halved, 0.5, ALU.mult))
            normalize(xn, x)
            raise_("x_normed")

            def ada_place(n):
                bank = ps.read(dve, f"adaT{n}", "dve")
                part, half = n // 2, n % 2
                if part in (2, 5):
                    rows = (g1b if part == 2 else g2b)[:, half * 512:half * 512 + 512]
                    if n == 4:
                        dve.wait_ge(ev("gate_rows_loaded"), 32)
                    ins = tt(rows, bank[:, :], rows, ALU.add)
                else:
                    ins = stt(modc[:, 4 * n:4 * n + 4], bank[:, 0:4], 1.0 if part in (1, 4) else 0.0,
                              prm[:, BADA + 4 * n:BADA + 4 * n + 4], ALU.add, ALU.add)
                ps.release(f"adaT{n}", ins, dve)
            for n in ADA1:
                ada_place(n)
            to_channels(ps, "h1", hT, modc[:, 8:16], modc[:, 0:8])
            normalize(mem_x, mem_x)
            raise_("mem_normed")
            for n in range(4):
                blocks = range(4 * n, min(4 * n + 4, NXB))
                for k in blocks:
                    if k % 2 == 0:
                        ps.wait_drained(dve, f"xb{k // 2}")
                    dst = cv[:, k - 4 * n, :]
                    w = [prm[:, ROWS["conv_w"] + j * NXB + k:ROWS["conv_w"] + j * NXB + k + 1] for j in range(CONV)]
                    bias = prm[:, ROWS["conv_b"] + k:ROWS["conv_b"] + k + 1]
                    do(ts(dst, raw[:, k, 3:3 + T], w[3], ALU.mult, bias, ALU.add))
                    for j in range(3):
                        do(stt(dst, raw[:, k, j:j + T], w[j], dst, ALU.mult, ALU.add))
                raise_("conv_batch")
                dve.wait_ge(ev("conv_tanh"), n + 1)
                m = len(blocks)
                times_sigmoid(xb[:, 4 * n:4 * n + m, :], ce[:, 0:m, :], cv[:, 0:m, :])
                raise_("conv_gated")
            bank = ps.read(dve, "dt", "dve")
            dve.wait_ge(ev("head_rows_loaded"), 48)
            ps.release("dt", tt(dtr, v3(bank[:, 0:TT * HEADS], TT), over(dt_b, TT, 1), ALU.add), dve)
            do(stt(flat(dta), flat(dtr), -1.0, flat(dtr), ALU.mult, ALU.max))
            raise_("dt_abs")
            dve.wait_ge(ev("dt_log"), 1)
            do(ts(dtv, dtr, 0.0, ALU.max))
            do(tt(dtv, dtv, dta, ALU.add))
            do(ts(nega, nega, -1.0, ALU.mult))
            do(tt(dta, dtv, over(nega, TT, 1), ALU.mult))
            raise_("decay_steps")
            to_channels(ps, "memT", memT, prm[:, ROWS["g_mem"]:ROWS["g_mem"] + 8], None)
            bank = ps.read(dve, "acs", "dve")
            ps.release("acs", V.tensor_copy(flat(acs), bank[:, 0:3 * HEADS]), dve)
            do(tt(dte, acs[:, 2, :], acs[:, 0, :], ALU.subtract))
            raise_("decay_sums")

            def segment_sums(t):
                for g in range(GROUPS):
                    bank = ps.read(dve, f"row{t}{g}", "dve")
                    for r in range(RPG):
                        h = RPG * g + r
                        ins = stt(segs[t * GROUPS + g][:, r, :], bank[:, r * P:r * P + P], acs[:, t, h:h + 1],
                                  C["seg_mask"], ALU.subtract, ALU.add)
                        if r < RPG - 1:
                            do(ins)
                    ps.release(f"row{t}{g}", ins, dve)
                    raise_("segment_sums")
            segment_sums(0)
            ps.wait_drained(dve, "u")
            dve.wait_ge(ev("pool_table_loaded"), 16)

            def widen(dst, src, by, blocks):
                do(tt(dst[:, blocks, PAD:PAD + T], src[:, blocks, PAD:PAD + T], src[:, blocks, PAD - by:PAD - by + T],
                      ALU.add))

            def group_mean(g, src):
                p0, b = 64 * (g % 2), g // 2
                do(tt(diff[p0:p0 + 64, b, :], src[p0:p0 + 64, b, PAD:PAD + T], prc[p0:p0 + 64, b, :], ALU.mult))
            both, last_ = slice(0, 2), slice(1, 2)
            widen(sA, uT, 1, both)
            group_mean(0, sA)
            widen(sB, sA, 2, both)
            group_mean(1, sB)
            widen(sA, sB, 4, last_)
            group_mean(2, sA)
            widen(sB, sA, 8, last_)
            group_mean(3, sB)
            do(tt(diff, diff, uT[:, :, PAD:PAD + T], ALU.subtract))
            raise_("pooled")
            segment_sums(1)
            ps.wait_drained(dve, "xs1_4")
            dve.wait_ge(ev("decay_exps"), 1)

            def heads(v, n=HD):
                return v.rearrange("p (h c) -> p h c", c=n)
            for t in range(TT):
                do(tt(heads(xdt[:, t, :]), heads(xtok[:, t, 0:SSD_W]), over(dtv[:, t, :], HD, 2), ALU.mult))
            do(tt(heads(xcd), heads(xdt[:, 0, :]), over(dte, HD, 2), ALU.mult))
            raise_("xcd_ready")
            for t in range(TT):
                do(tt(heads(yv[:, t, :]), heads(xtok[:, t, 0:SSD_W]), over(dskip_b, HD, 2), ALU.mult))
            GW = RPG * HD

            def decayed_products(n):
                dve.wait_ge(ev("segment_exps"), n + 1)
                bank = ps.read(dve, f"cb{n}", "dve")
                ps.release(f"cb{n}", tt(seg2[n % 2], segs[n], over(bank[:, 0:P], RPG, 1), ALU.mult), dve)

            def beside(step):
                for what, n, *t in BESIDE[step]:
                    if what == "adaT":
                        ada_place(n)
                    elif what == "mk":
                        bank = ps.read(dve, f"mk{n}", "dve")
                        ps.release(f"mk{n}", V.tensor_copy(mk[:, n * EH * EQ:(n + 1) * EH * EQ], bank[:, 0:256]), dve)
            sq = ce_f[:, 0:SSD_W]

            def gate_tile(t):
                do(tt(yv[:, t, :], yv[:, t, :], z[:, t, :], ALU.mult))
                do(tt(sq, yv[:, t, :], yv[:, t, :], ALU.mult))
                do(V.tensor_reduce(gss[:, t * GROUPS:(t + 1) * GROUPS], v3(sq, GROUPS), AX.X, ALU.add))
            beside(0)
            for g in range(GROUPS):
                bank = ps.read(dve, f"state{g}", "dve")
                ps.release(f"state{g}", V.tensor_copy(prevT[:, g, :], bank[:, 0:GW]), dve)
            decayed_products(0)
            for n in range(TT * GROUPS):
                t, g = divmod(n, GROUPS)
                if n + 1 < TT * GROUPS:
                    decayed_products(n + 1)
                if n:
                    beside(n)
                dst = yv[:, t, g * GW:g * GW + GW]
                bank = ps.read(dve, f"yd{n}", "dve")
                ps.release(f"yd{n}", tt(dst, bank[:, 0:GW], dst, ALU.add), dve)
                if n == 1:
                    dve.wait_ge(ev("z_tanh"), 1)
                    for t_ in range(TT):
                        times_sigmoid(z[:, t_, :], zt[t_], z[:, t_, :])
                if n == GROUPS:
                    gate_tile(0)
                if t:
                    bank = ps.read(dve, f"yo{g}", "dve")
                    ps.release(f"yo{g}", tt(heads(ybuf), heads(bank[:, 0:GW]),
                                            over(eacs[:, RPG * g:RPG * g + RPG], HD, 2), ALU.mult), dve)
                    do(tt(dst, dst, ybuf, ALU.add))
            gate_tile(1)
            rsqrt(rs[:, 0:TT * GROUPS], TT * GROUPS, gss, GW)
            for t in range(TT):
                yh = heads(yv[:, t, :], GW)
                do(tt(yh, yh, over(rs[:, t * GROUPS:(t + 1) * GROUPS], GW, 2), ALU.mult))
            raise_("ssd_normed")
            beside(TT * GROUPS)

            for t in range(TT):
                for n in range(2):
                    if t and n:
                        normalize(xn, x, [0])
                    bank = ps.read(dve, f"mix{n}t{t}", "dve")
                    cols = slice(n * 512, n * 512 + 512)
                    ps.release(f"mix{n}t{t}", tt(cv_f[:, 0:512], bank[:, :], g1b[:, cols], ALU.mult), dve)
                    do(tt(x[:, t, cols], x[:, t, cols], cv_f[:, 0:512], ALU.add))
                raise_("x_updated")
            normalize(xn, x, [1])
            raise_("x_normed")

            def head_norm(src, n, width, gain, sq_, t=None):
                do(tt(sq_, src, src, ALU.mult))
                do(V.tensor_reduce(hss[:, 0:n], sq_, AX.X, ALU.add))
                rsqrt(rs[:, 0:n], n, hss[:, 0:n], width)
                do(tt(src, src, over(rs[:, 0:n], width, 2), ALU.mult))
                if gain is not None:
                    do(tt(src, src, over(gain, n, 1), ALU.mult))
            to_channels(ps, "h2", hT, modc[:, 32:40], modc[:, 24:32])
            dve.wait_ge(ev("router_loaded"), 32)
            dve.wait_ge(ev("router_rows_loaded"), 32)
            for t in range(TT):
                bank = ps.read(dve, f"routert{t}", "dve")
                ps.release(f"routert{t}", tt(lg[:, t, :], bank[:, 0:EG + NE], rb, ALU.add), dve)

            def first_max(one_hot, values, top, rev, tmp):
                n = values.shape[2]
                do(V.tensor_reduce(top, values, AX.X, ALU.max))
                do(tt(tmp, values, over(top, n, 2), ALU.is_equal))
                do(tt(tmp, tmp, over(rev, TT, 1), ALU.mult))
                do(V.tensor_reduce(gsm, tmp, AX.X, ALU.max))
                do(tt(one_hot, over(gsm, n, 2), over(rev, TT, 1), ALU.is_equal))
            glog = lg[:, :, 0:EG]
            first_max(ohg, glog, gm, C["rev4"], gtm)
            do(tt(gtm, glog, over(gm, EG, 2), ALU.subtract))
            raise_("group_shifted")
            dve.wait_ge(ev("group_exps"), 1)
            do(V.tensor_reduce(gsm, gtm, AX.X, ALU.add))
            do(V.reciprocal(pg, gsm))
            w4 = wide.rearrange("p (t g e) -> p t g e", t=TT, g=EG)
            for t in range(TT):
                do(tt(w4[:, t], lg[:, t, EG:].rearrange("p (g e) -> p g e", g=EG), over(ohg[:, t, :], EPG, 2), ALU.mult))
                do(V.tensor_reduce(w8[:, t, :], w4[:, t].rearrange("p g e -> p e g"), AX.X, ALU.add))
            first_max(oh1, w8, v1, C["rev8"], t8)
            do(stt(w8, oh1, BIG, w8, ALU.mult, ALU.add))
            first_max(oh2, w8, v2, C["rev8"], t8)
            do(tt(v2, v2, v1, ALU.subtract))
            raise_("top_gap")
            dve.wait_ge(ev("top_exp"), 1)
            do(ts(v1, e2, 1.0, ALU.add))
            do(V.reciprocal(v1, v1))
            do(tt(gate1, pg, v1, ALU.mult))
            do(tt(gate2, gate1, e2, ALU.mult))
            for s_, oh in ((sel1, oh1), (sel2, oh2)):
                for t in range(TT):
                    do(tt(s_[:, t, :].rearrange("p (g e) -> p g e", g=EG), over(ohg[:, t, :], EPG, 2),
                          over(oh[:, t, :], EG, 1), ALU.mult))
            do(tt(sel, sel1, sel2, ALU.add))
            do(V.memset(cumA, 0.0))
            do(V.memset(cumB, 0.0))
            raise_("chosen")
            bank = ps.read(dve, "rank", "dve")
            do(V.tensor_copy(flat(slot_of), bank[:, 0:2 * NE]))
            ps.release("rank", V.tensor_copy(cnt, bank[:, 2 * NE:3 * NE]), dve)
            do(ts(nblk, cnt, 0.0, ALU.is_gt))
            for m in range(1, T // SLOTS):
                do(stt(nblk, cnt, float(m * SLOTS), nblk, ALU.is_gt, ALU.add))
            for e in (0, NE - 1):
                do(ts(nblk[:, e:e + 1], nblk[:, e:e + 1], 1.0, ALU.max))
            do(V.tensor_copy(cumA[:, NE:], nblk))
            cum = [cumA, cumB]
            for m in range(5):
                s_, d_ = cum[m % 2], cum[(m + 1) % 2]
                do(tt(d_[:, NE:], s_[:, NE:], s_[:, NE - 2 ** m:2 * NE - 2 ** m], ALU.add))
            ends = cumB[:, NE:]
            do(ts(wide[:, 0:NE], ends, C["row_before"], ALU.is_le))
            do(V.tensor_reduce(be, wide[:, 0:NE], AX.X, ALU.add))
            do(ts(be, be, float(NE - 1), ALU.min))
            raise_("block_experts")
            do(ts(npf, ends[:, NE - 1:NE], 1.0, ALU.add))
            do(V.tensor_copy(meta[0:1, P + 3:P + 4], npf[0:1, :]))
            do(ts(meta[0:1, P:P + 1], meta[0:1, P + 3:P + 4], 1, ALU.logical_shift_right))
            do(V.tensor_copy(in_last[0:1, :], meta[0:1, P:P + 1]))
            do(ts(in_last[0:1, :], in_last[0:1, :], -1.0, ALU.add))
            do(V.tensor_copy(meta[0:1, P + 1:P + 2], in_last[0:1, :]))
            do(stt(meta[0:1, P + 2:P + 3], in_last[0:1, :], -2.0, ends[0:1, NE - 1:NE], ALU.mult, ALU.add))
            bank = ps.read(dve, "experts", "dve")
            ps.release("experts", V.tensor_copy(meta[0:1, 0:P], bank[0:1, 0:P]), dve)
            raise_("routed")
            do(tt(cnt, ends, nblk, ALU.subtract))
            do(ts(cnt, cnt, 1.0, ALU.add, float(SLOTS), ALU.mult))
            do(tt(slot_of, slot_of, over(cnt, TT, 1), ALU.add))
            all_slots = npf
            do(ts(npf, ends[:, NE - 1:NE], float(SLOTS), ALU.mult))
            for s_, dst in ((sel1, dest[0]), (sel2, dest[1])):
                do(tt(v3(wide, TT), s_, slot_of, ALU.mult))
                do(V.tensor_reduce(dst, v3(wide, TT), AX.X, ALU.add))
                do(ts(wrap, dst, all_slots, ALU.is_ge, -1.0, ALU.mult))
                do(stt(dst, wrap, all_slots, dst, ALU.mult, ALU.add))
            do(V.tensor_copy(slot_id, C["iota"]))

            pairs = dve.value_load(meta[0:1, P:P + 1], min_val=4, max_val=MAXB // 2)
            last_pair = dve.value_load(meta[0:1, P + 1:P + 2], min_val=3, max_val=MAXB // 2 - 1)
            gA, gB, hA, hB, tA, tB, oA, oB = banks

            def choose_slots(i, lc):
                if i is not None:
                    dve.wait_ge(ev("gather_filled"), i * 2)
                for t in range(TT):
                    lc(ts(pick[:, t, :], slot_id, dest[0][:, t:t + 1], ALU.is_equal))
                    ins = stt(pick[:, t, :], slot_id, dest[1][:, t:t + 1], pick[:, t, :], ALU.is_equal, ALU.add)
                    lc(ins)
                lc(ts(slot_id, slot_id, float(P), ALU.add))
                dve.sem_inc(ev("slots_picked"), 1)

            def slots_in(i, lc):
                dve.wait_ge(ev("gather_filled"), i * 2 + 2)
                for k in range(4, 8):
                    ins = ts(xeT[:, k, :], gB[:, (k - 4) * P:(k - 4) * P + P], modc[:, 32 + k:33 + k], ALU.mult,
                             modc[:, 24 + k:25 + k], ALU.add)
                    if k < 7:
                        lc(ins)
                ins.then_inc(ev("slots_in_by_dve"), 1)

            def hidden_out(i):
                dve.wait_ge(ev("hidden_filled"), i * 2 + 2)
                V.tensor_copy(hs[:, 512:1024], hB[:, :]).then_inc(ev("hidden_out_by_dve"), 1)

            def gate(i, lc):
                dve.wait_ge(ev("gate_tanhs"), i + 1)
                lc(stt(gt, ge, 1.0, tA[:, :], ALU.add, ALU.mult))
                dve.wait_ge(ev("hidden_transposed"), i * 2 + 2)
                stt(sT, gt, 0.5, tB[:, :], ALU.mult, ALU.mult).then_inc(ev("hidden_gated"), 1)

            def rows_out(m):
                dve.wait_ge(ev("rows_filled_for_dve"), m + 1)
                dve.wait_ge(ev("parts_filled"), m * 4 + 1)
                V.tensor_copy(osb[:, 512:1024], oB[:, :]).then_inc(ev("rows_out_by_dve"), 1)

            def shares(m, lc):
                dve.wait_ge(ev("parts_filled"), m * 4 + 1)
                lc(stt(share_f, slot_rows, slot_col, gate_rows, ALU.is_equal, ALU.mult))
                lc(ts(slot_col, slot_col, float(P), ALU.add))
                tt(share_f[:, 0:T], share_f[:, 0:T], share_f[:, T:2 * T], ALU.add).then_inc(ev("shares_ready"), 1)

            def add_parts(m, t):
                if t == 0:
                    dve.wait_ge(ev("parts_added"), m * 4 + 1)
                for n_, src in enumerate((oA, oB)):
                    dve.wait_ge(ev("parts_filled"), m * 4 + (2 * t + n_ + 2))
                    dst = acc[:, t, n_ * 512:n_ * 512 + 512]
                    tt(dst, src[:, :], dst, ALU.add).then_inc(ev("parts_added"), 1)

            def spread_columns():
                for n, col in enumerate([c_[:, t:t + 1] for c_ in (dest[0], dest[1], gate1, gate2) for t in range(TT)]):
                    do(ts(diag[:, n, :], ident, col, ALU.mult), spread)
                do(V.tensor_copy(slot_col, C["row_id"]))
                dve.wait_ge(ev("lead_filled"), 1)
                do(V.tensor_copy(slot_rows, oA[:, :]))
                dve.wait_ge(ev("lead_filled"), 2)
                do(V.memset(acc_f, 0.0))

            def norm_memory_keys():
                dve.wait_ge(ev("norm_rows_loaded"), 96)
                head_norm(heads(mk, EQ), TT * EH, EQ, G_KM, heads(msq, EQ))
                raise_("mem_keys_normed")
            G_QR, G_KR, G_QM, G_KM = (rows2[:, 256 + 64 * n:320 + 64 * n] for n in range(4))

            def turn(i, lc, first):
                if not first:
                    shares(i - 1, lc)
                choose_slots(i + 1, lc)
                hidden_out(i)
                if not first:
                    rows_out(i - 1)
                gate(i, lc)
                if not first:
                    add_parts(i - 1, 0)
                slots_in(i + 1, lc)
                if first:
                    spread_columns()
                    dve.wait_ge(ev("lead_out"), 1)
                    dve.sem_inc(ev("parts_added"), 1)
                    norm_memory_keys()
                else:
                    add_parts(i - 1, 1)
            lead = Chained(dve, ev("dve_lead_step"))
            choose_slots(None, lead)
            slots_in(0, lead)
            turn(0, lead, True)
            with dve.Fori(1, pairs) as i:
                lc = LoopChained(dve, ev("dve_expert_step"), i, 2 + 5 + 1 + 3)
                turn(i, lc, False)
                lc.end()
            shares(last_pair, lead)
            rows_out(last_pair)
            add_parts(last_pair, 0)
            add_parts(last_pair, 1)

            dve.wait_ge(ev("parts_added"), pairs * 4 + 1)
            for t in range(TT):
                do(tt(acc[:, t, :], acc[:, t, :], g2b[:, :], ALU.mult))
                do(tt(x[:, t, :], x[:, t, :], acc[:, t, :], ALU.add))
                raise_("x_updated")
            dve.wait_ge(ev("final_rows_loaded"), 16)
            for t in range(TT):
                do(tt(acc[:, t, :], x[:, t, :], fnw[:, :], ALU.mult))
                raise_("x_updated")
            norm_no[0] += 2 * TT
            dve.wait_ge(ev("squares"), norm_no[0])
            rs1, rs2 = rs[:, 0:TT], rs[:, TT:2 * TT]
            rsqrt(rs1, TT, ss, D)
            do(tt(rs2, rs1, rs1, ALU.mult))
            do(tt(ss_w, ss_w, rs2, ALU.mult))
            rsqrt(rs2, TT, ss_w, D)
            do(tt(rs2, rs2, rs1, ALU.mult))
            for t in range(TT):
                do(ts(xn[:, t, :], acc[:, t, :], rs2[:, t:t + 1], ALU.mult))
            raise_("x_normed")
            to_channels(ps2, "h3", hT, prm[:, ROWS["g_mix"]:ROWS["g_mix"] + 8], None)
            for t in range(TT):
                do(ts(x[:, t, :], acc[:, t, :], rs1[:, t:t + 1], ALU.mult))
            dve.wait_ge(ev("positions_loaded"), 16)
            do(V.tensor_copy(pos_f, pos_i))
            do(tt(ang, over(C["inv"], TT, 1), over(pos_f, NI, 2), ALU.mult))
            ROUND = float(1.5 * 2 ** 23)
            do(ts(rn, ang, float(1.0 / (2 * np.pi)), ALU.mult, ROUND, ALU.add))
            do(ts(rn, rn, -ROUND, ALU.add))
            c1 = 6.28125
            c2 = float(np.float32(np.floor((2 * np.pi - c1) * 2 ** 22) / 2 ** 22))
            c3 = float(2 * np.pi - c1 - c2)
            for c_ in (c1, c2, c3):
                do(stt(ang, rn, -c_, ang, ALU.mult, ALU.add))
            PI_ = 3.1415925
            do(ts(rn, ang, float(np.pi / 2), ALU.add))
            do(ts(sinv, rn, float(np.pi), ALU.is_gt))
            do(stt(rn, sinv, -float(2 * np.pi), rn, ALU.mult, ALU.add))
            do(ts(rn, rn, -PI_, ALU.max, PI_, ALU.min))
            do(ts(ang, ang, -PI_, ALU.max, PI_, ALU.min))
            raise_("angles_ready")
            dve.wait_ge(ev("rope_tables"), 1)

            for t in range(TT):
                bank = ps2.read(dve, f"mqt{t}", "dve")
                ps2.release(f"mqt{t}", V.tensor_copy(qm[:, t, :], bank[:, 0:256]), dve)
            head_norm(heads(flat(qm), EQ), TT * EH, EQ, G_QM, heads(flat(qsq), EQ))
            raise_("mem_q_normed")

            def gate_logits(br, name, buf, rows, halves=(0, 1)):
                dve.wait_ge(ev(f"gate_bias_loaded_{br}"), 16)
                for n in halves:
                    for t in range(TT):
                        cols = slice(n * 512, n * 512 + 512)
                        bank = ps2.read(dve, f"gate{br}{n}t{t}", "dve")
                        ps2.release(f"gate{br}{n}t{t}", tt(buf[:, t, cols], bank[:, :], rows[:, cols], ALU.add), dve)
                raise_(f"gate_logits_{name}")

            def add_gated_branch(buf, first=False, cols=slice(0, D)):
                for t in range(TT):
                    if first:
                        times_sigmoid(ysum[:, t, cols], buf[:, t, cols], obr[:, t, cols])
                    else:
                        times_sigmoid(buf[:, t, cols], buf[:, t, cols], obr[:, t, cols])
                        do(tt(ysum[:, t, cols], ysum[:, t, cols], buf[:, t, cols], ALU.add))
            gate_logits(2, "2", gates2, g1b)

            def attention(n_heads, first, scale, causal, then=None):
                for h in range(n_heads + 1):
                    if h < n_heads:
                        n = first + h
                        bank = ps2.read(dve, f"s_{n}", "dve")
                        if n >= 3:
                            ps2.wait_filled(dve, f"pT_{n - 3}")
                        if causal:
                            ps2.release(f"s_{n}", tt(pr[n % 3][:, 0:3 * P], bank[:, 0:3 * P], C["causal"], ALU.add), dve)
                            do(V.tensor_reduce(mxs[n % 3][:, 0:1], pr[n % 3][:, 0:P], AX.X, ALU.max))
                            do(V.tensor_reduce(mxs[n % 3][:, 1:2], pr[n % 3][:, P:3 * P], AX.X, ALU.max))
                        else:
                            ps2.release(f"s_{n}", V.tensor_copy(pr[n % 3], bank[:, :]), dve)
                            do(V.tensor_reduce(mxs[n % 3], v3(pr[n % 3], TT), AX.X, ALU.max))
                        do(ts(mxs[n % 3], mxs[n % 3], -scale, ALU.mult))
                        raise_("scores_maxed")
                    if 1 <= h <= n_heads:
                        n = first + h - 1
                        dve.wait_ge(ev("probs_ready"), n + 1)
                        do(V.reciprocal(inverse[n % 4], sums[n % 3]))
                        raise_("sums_inverted")
                    if then and h == n_heads - 1:
                        then()
            attention(EH, 0, EQ ** -0.5, False)
            ps2.wait_drained(dve, f"o_{EH - 1}")
            dve.wait_ge(ev("gate_tanhs_2"), 1)
            add_gated_branch(gates2, True)
            raise_("gate_2_added")
            dve.wait_ge(ev("gla_rows_loaded"), 48)
            for t in range(TT):
                bank = ps2.read(dve, f"lg{t}", "dve")
                ps2.release(f"lg{t}", tt(la[:, t, :], bank[:, :], bgla, ALU.add), dve)
            do(stt(flat(lt), flat(la), -1.0, flat(la), ALU.mult, ALU.max))
            raise_("log_arg")
            do(ts(flat(la), flat(la), 0.0, ALU.min))
            dve.wait_ge(ev("log_done"), 1)
            do(tt(flat(la), flat(la), flat(lt), ALU.subtract))
            do(ts(flat(la), flat(la), 1.0 / 16.0, ALU.mult))
            raise_("log_decays")
            for t in range(TT):
                bank = ps2.read(dve, f"lvl0{t}", "dve")
                ps2.release(f"lvl0{t}", tt(att[t], v3(bank[:, :], GH), over(ident, GH, 1), ALU.mult), dve)
            ps2.wait_drained(dve, "cum1")
            def sides(v, side, half):
                w = v.rearrange("p h (b s c) -> p (h b) s c", s=2, c=half)
                return w[:, :, side, :]

            def level_differences(lvl):
                if lvl <= LEVELS:
                    half = 2 ** (lvl - 1)
                    mid = gbT.rearrange("p h (b s c) -> p (h b) s c", s=2, c=half)[:, :, 0, half - 1:half]
                    mid = mid.to_broadcast(list(sides(gbT, 0, half).shape))
                    do(tt(sides(lev, 0, half), mid, sides(gbT, 0, half), ALU.subtract))
                    do(tt(sides(lev, 1, half), sides(gbT, 1, half), mid, ALU.subtract))
                else:
                    mid = gbT[:, :, P - 1:P].to_broadcast([P, GH, P])
                    do(tt(lev[:, :, 0:P], mid, gbT[:, :, 0:P], ALU.subtract))
                    do(V.tensor_copy(lev[:, :, P:T], gbT[:, :, P:T]))
                raise_("level_differences")
            level_differences(1)
            for lvl in range(1, LEVELS + 2):
                half = 2 ** (lvl - 1)
                dve.wait_ge(ev("level_exps"), lvl)
                if lvl > 1:
                    ps2.wait_filled(dve, f"lvl{lvl - 1}1")
                do(tt(sides(qk, 0, half), sides(lev, 0, half), sides(gkT, 0, half), ALU.mult))
                do(tt(sides(qk, 1, half), sides(lev, 1, half), sides(gqT, 1, half), ALU.mult))
                raise_("level_ready")
                if lvl <= LEVELS:
                    level_differences(lvl + 1)
                    mask = C["level"][:, (lvl - 1) * P:lvl * P]
                    for t in range(TT):
                        bank = ps2.read(dve, f"lvl{lvl}{t}", "dve")
                        ps2.release(f"lvl{lvl}{t}", V.copy_predicated(att[t], over(mask, GH, 1).bitcast(I32),
                                                                      v3(bank[:, :], GH)), dve)
            dve.wait_ge(ev("latents_out"), 1)
            for t in range(TT):
                head_norm(ckv[t][:, :, 0:KVR], 1, KVR, None, csq.unsqueeze(1))
            raise_("ckv_normed")
            dve.wait_ge(ev("r_tanh"), 1)
            for t, e_ in enumerate((flat(la), flat(lt))):
                times_sigmoid(gr[:, t, :], e_, gr[:, t, :])
                do(tt(heads(gr[:, t, :], DV), heads(gr[:, t, :], DV), over(ggla, GH, 1), ALU.mult))
            for h in range(GH):
                bank = ps2.read(dve, f"go{h}", "dve")
                ps2.release(f"go{h}", V.tensor_copy(obr[:, :, h * DV:h * DV + DV], v3(bank[:, :], TT)), dve)
            raise_("gla_summed")
            dve.wait_ge(ev("gla_squares"), 1)
            for t, sq_ in enumerate((gqT, gkT)):
                do(V.tensor_reduce(hss[:, t * GH:(t + 1) * GH], heads(flat(sq_), DV), AX.X, ALU.add))
            rsqrt(rs[:, 0:TT * GH], TT * GH, hss[:, 0:TT * GH], DV)
            for t in range(TT):
                oh = heads(obr[:, t, :], DV)
                do(tt(oh, oh, over(rs[:, t * GH:(t + 1) * GH], DV, 2), ALU.mult))
                do(tt(obr[:, t, :], obr[:, t, :], gr[:, t, :], ALU.mult))
            gate_logits(1, "1", gates1, g2b)
            dve.wait_ge(ev("gate_tanhs_1"), 1)
            add_gated_branch(gates1)
            raise_("gla_done")

            def rotate(dst, src, t, n):
                c_, s_ = over(cosv[:, t, :], n, 1), over(sinv[:, t, :], n, 1)
                tmp = nsq[:, 0:n * NI].rearrange("p (n c) -> p n c", n=n)
                a_, b_ = src[:, :, 0:NI], src[:, :, NI:ROPE]
                do(tt(dst[:, :, 0:NI], a_, c_, ALU.mult))
                do(tt(tmp, b_, s_, ALU.mult))
                do(tt(dst[:, :, 0:NI], dst[:, :, 0:NI], tmp, ALU.subtract))
                do(tt(dst[:, :, NI:ROPE], a_, s_, ALU.mult))
                do(tt(tmp, b_, c_, ALU.mult))
                do(tt(dst[:, :, NI:ROPE], dst[:, :, NI:ROPE], tmp, ALU.add))
            for t in range(TT):
                head_norm(ckv[t][:, :, KVR:KVR + ROPE], 1, ROPE, G_KR, nsq[:, 0:ROPE].unsqueeze(1))
                rotate(kr2[:, t:t + 1, 0:ROPE], ckv[t][:, :, KVR:KVR + ROPE], t, 1)
                do(V.tensor_copy(kr2[:, t, ROPE:2 * ROPE], kr2[:, t, 0:ROPE]))
            raise_("rope_k_ready")
            gate_logits(0, "0a", gates0, fnw, (0,))
            dve.wait_ge(ev("q_squares"), 1)
            for part, (lo, w) in enumerate(((0, NOPE), (NOPE, ROPE))):
                for t in range(TT):
                    at = (part * TT + t) * MH
                    do(V.tensor_reduce(hss[:, at:at + MH], v3(qsqs[t], MH)[:, :, lo:lo + w], AX.X, ALU.add))
            rsqrt(rs[:, 0:2 * TT * MH], 2 * TT * MH, hss, [(TT * MH, NOPE), (TT * MH, ROPE)])
            for t in range(TT):
                qh = v3(q[t], MH)
                do(tt(qh[:, :, 0:NOPE], qh[:, :, 0:NOPE], over(rs[:, t * MH:(t + 1) * MH], NOPE, 2), ALU.mult))
                do(tt(qh[:, :, NOPE:], qh[:, :, NOPE:], over(rs[:, (TT + t) * MH:(TT + t + 1) * MH], ROPE, 2), ALU.mult))
                do(tt(qh[:, :, NOPE:], qh[:, :, NOPE:], over(G_QR, MH, 1), ALU.mult))
                rotate(heads(ropeb[:, t, :], ROPE), qh[:, :, NOPE:], t, MH)
            raise_("mla_q_ready")
            dve.wait_ge(ev("k_squares"), 1)
            for t in range(TT):
                do(V.tensor_reduce(hss[:, t * MH:(t + 1) * MH], v3(ksqs[t], MH), AX.X, ALU.add))
            rsqrt(rs[:, 0:TT * MH], TT * MH, hss, NOPE)
            for t in range(TT):
                kh = v3(kv[:, t, :], MH)[:, :, 0:NOPE]
                do(tt(kh, kh, over(rs[:, t * MH:(t + 1) * MH], NOPE, 2), ALU.mult))
            raise_("mla_k_ready")
            gate_logits(0, "0b", gates0, fnw, (1,))

            def first_heads_done():
                ps2.wait_drained(dve, f"o_{EH + MH // 2 - 1}")
                dve.wait_ge(ev("gate_tanhs_0a"), 1)
                add_gated_branch(gates0, cols=slice(0, D // 2))
            attention(MH, EH, (NOPE + ROPE) ** -0.5, True, first_heads_done)
            ps2.wait_drained(dve, f"o_{EH + MH - 1}")
            dve.wait_ge(ev("gate_tanhs_0b"), 1)
            add_gated_branch(gates0, cols=slice(D // 2, D))
            raise_("branches_summed")
            to_channels(ps2, "ysT", hT, 0.5, None)

            def low_part(n):
                dve.wait_ge(ev("high_parts"), n + 1)
                at = (FFN_LOAD + n) % 4
                do(tt(low_slots[at], slots[at], high_slots[n % 2].bitcast(F32), ALU.subtract))
                raise_("low_parts")
            low_part(0)
            low_part(1)
            for t in range(TT):
                for n in range(2):
                    if t and n:
                        normalize(xn, x, [0])
                    bank = ps2.read(dve, f"wo{n}t{t}", "dve")
                    dst = x[:, t, n * 512:n * 512 + 512]
                    ps2.release(f"wo{n}t{t}", tt(dst, bank[:, :], dst, ALU.add), dve)
                raise_("x_updated")
            normalize(xn, x, [1])
            raise_("x_normed")
            for j in range(4):
                bank = ps2.read(dve, f"h4{j}", "dve")
                dve.wait_ge(ev("ffn_input_high"), j + 1)
                for b in range(2):
                    c = 2 * j + b
                    ins = stt(hL[:, c, :], bank[:, b * T:b * T + T], prm[:, ROWS["g_ffn"] + c:ROWS["g_ffn"] + c + 1],
                              hH[:, c, :].bitcast(F32), ALU.mult, ALU.subtract)
                    if b:
                        ps2.release(f"h4{j}", ins, dve)
                    else:
                        do(ins)
            for n in range(8):
                for b in range(2):
                    dve.wait_ge(ev("ffn_high"), 2 * n + b + 1)
                    do(tt(relu[b], relu[b], relu[b], ALU.mult))
                    high = flat(aH[n])[:, b * 512:b * 512 + 512].bitcast(F32)
                    do(tt(flat(aL[n])[:, b * 512:b * 512 + 512], relu[b], high, ALU.subtract))
                    raise_("ffn_squared")
                low_part(n + 2)
            for n in range(10, 16):
                low_part(n)
            for t in range(TT):
                for n in range(2):
                    bank = ps2.read(dve, f"down{t}{n}", "dve")
                    dst = x[:, t, n * 512:n * 512 + 512]
                    ps2.release(f"down{t}{n}", tt(dst, bank[:, :], dst, ALU.add), dve)
                    raise_("output_ready")
        @block.gpsimd
        def _(pool):
            def rows_of(dst, src, name):
                pool.dma_start(dst, src.partition_broadcast(P)).then_inc(ev(name), 16)
            pool.memset(raw[:, :, 0:3], 0.0).then_inc(ev("pool_step"), 1)
            for v in (uT, sA, sB):
                pool.memset(v[:, :, 0:PAD], 0.0).then_inc(ev("pool_step"), 1)
            pool.memset(wpool, 0.0).then_inc(ev("pool_step"), 1)
            pool.wait_ge(ev("pool_step"), 5)
            pool.sem_inc(ev("pads_zeroed"), 1)
            rows_of(dt_b, a["dt_bias"][0], "head_rows_loaded")
            rows_of(alog_b, a["a_log"][0], "head_rows_loaded")
            rows_of(dskip_b, a["d_skip"][0], "head_rows_loaded")
            for g in range(4):
                lo = 64 * (g % 2)
                pool.dma_start(wpool[lo:lo + 64, g // 2, lo:lo + 64], a["w_pool"][0][g]).then_inc(ev("pool_weights_loaded"), 16)
            for n, (nm, w) in enumerate((("g_q_nope_2", 128), ("g_k_nope_2", 128), ("g_q_rope_2", 64),
                                         ("g_k_rope_2", 64), ("g_q_mem_2", 64), ("g_k_mem_2", 64))):
                lo = (0, 128, 256, 320, 384, 448)[n]
                rows_of(rows2[:, lo:lo + w], a[nm][0], "norm_rows_loaded")
            rows_of(rb[:, 0:EG], a["b_group"][0], "router_rows_loaded")
            rows_of(rb[:, EG:], a["b_router"][0], "router_rows_loaded")
            pool.dma_start(pos_i, a["positions_2"][0].rearrange("(t p) -> p t", p=P),
                           allow_slow_non_contiguous=True).then_inc(ev("positions_loaded"), 16)
            ps.wait_drained(pool, "adaT3")
            pool.dma_start(mem_x, a["mem_2"][0].rearrange("(t p) d -> p t d", p=P)).then_inc(ev("memory_loaded"), 16)
            pool.dma_start(flat(prc), a["pool_table"]).then_inc(ev("pool_table_loaded"), 16)
            rows_of(g1b[:, :], a["b_ada"][0][2 * D:3 * D], "gate_rows_loaded")
            rows_of(g2b[:, :], a["b_ada"][0][5 * D:6 * D], "gate_rows_loaded")
            rows_of(fnw[:, :], a["final_norm_w"], "final_rows_loaded")
            pool.wait_ge(ev("ssd_normed"), 1)
            pool.dma_start(wr[:, :, 0:EG], a["w_group"][0].rearrange("(k p) n -> p k n", p=P)).then_inc(ev("router_loaded"), 16)
            pool.dma_start(wr[:, :, EG:], a["w_router"][0].rearrange("(k p) n -> p k n", p=P)).then_inc(ev("router_loaded"), 16)
            pool.wait_ge(ev("x_updated"), 2)
            rows_of(g1b[:, :], a["b_gate_2"][0][2 * D:3 * D], "gate_bias_loaded_2")
            pool.wait_ge(ev("x_updated"), 4)
            rows_of(g2b[:, :], a["b_gate_2"][0][D:2 * D], "gate_bias_loaded_1")
            pool.wait_ge(ev("x_updated"), 6)
            rows_of(fnw[:, :], a["b_gate_2"][0][0:D], "gate_bias_loaded_0")
            pool.dma_start(wgate[0:GRANK, :], a["w_gla_gate_2"][0]).then_inc(ev("gla_rows_loaded"), 16)
            rows_of(bgla, a["b_gla_gate_2"][0], "gla_rows_loaded")
            rows_of(ggla, a["g_gla_out_2"][0], "gla_rows_loaded")
        @block.sync
        def _(sp):
            sp.dma_start(cst[:, :], a["const"]).then_inc(ev("constants_loaded"), 16)

            def load_rows(name, src, rows):
                sp.dma_start(prm_rows[ROWS[name]:ROWS[name] + rows, 0:P], src).then_inc(ev("param_rows_loaded"), 16)
            load_rows("c", a["c"][0].rearrange("(k p) -> k p", p=P), 8)
            load_rows("conv_w", a["conv_w"][0].rearrange("t (k p) -> (t k) p", p=P), CONV * NXB)
            load_rows("conv_b", a["conv_b"][0].rearrange("(k p) -> k p", p=P), NXB)
            load_rows("ssd_norm_w", a["ssd_norm_w"][0].rearrange("(k p) -> k p", p=P), 6)
            load_rows("pool_scale", a["pool_scale"][0].rearrange("(k p) -> k p", p=P), 2)
            load_rows("g_mix", a["g_mix_2"][0].rearrange("(k p) -> k p", p=P), 8)
            load_rows("g_mem", a["g_mem_2"][0].rearrange("(k p) -> k p", p=P), 8)
            load_rows("g_ffn", a["g_ffn_2"][0].rearrange("(k p) -> k p", p=P), 8)
            load_rows("g_ckv", a["g_ckv_2"][0].rearrange("(k p) -> k p", p=P), 2)
            load_rows("g_q_nope", a["g_q_nope_2"], 1)
            load_rows("g_k_nope", a["g_k_nope_2"], 1)
            sp.dma_start(prm_rows[0:48, P:2 * P],
                         a["b_ada"][0].rearrange("(k p) -> k p", p=P)).then_inc(ev("param_rows_loaded"), 16)
            sp.dma_start(x, a["x"][0].rearrange("(t p) d -> p t d", p=P)).then_inc(ev("x_loaded"), 16)
            for n in ADA1:
                ring.load(sp, cols_of(512), k_rows(w_ada, slice(n * 512, n * 512 + 512)))
            for n in IN_ORDER:
                c0, w = IN_SLOTS[n]
                ring.load(sp, cols_of(w), k_rows(w_in, slice(c0, c0 + w)))
            for step in BESIDE:
                for what, n, *t in step:
                    if what == "ada":
                        ring.load(sp, cols_of(512), k_rows(w_ada, slice(n * 512, n * 512 + 512)))
                    elif (what, n) == ("mk", 0) or (what == "mv" and n and t == [0]):
                        c0, w = MEM_SLOTS[n]
                        ring.load(sp, cols_of(w), k_rows(w_mkv, slice(c0, c0 + w)))
            for n in range(2):
                ring.load(sp, cols_of(512), k_rows(w_out, slice(n * 512, n * 512 + 512)))
            def load_w13(part, es, wait=None):
                for b, e in es:
                    if wait:
                        wait(3 * b + part)
                    src = w13[bass.ds(e, 1), part * 512:part * 512 + 512, :]
                    sp.dma_start(slots[3 * b + part].rearrange("p (k n) -> p k n", k=4),
                                 src.rearrange("e (k p) n -> (e p) k n", p=P)).then_inc(xw_landed[3 * b + part], 16)

            def load_w2(es, wait=None, slot=2):
                for b, e in es:
                    at = 3 * b + slot
                    if wait:
                        wait(at)
                    src = w2[bass.ds(e, 1), :, :]
                    sp.dma_start(slots[at].rearrange("p (k n) -> p k n", k=4),
                                 src.rearrange("e (k p) n -> (e p) k n", p=P)).then_inc(xw_landed[at], 16)

            last_of = {n % 4: name for n, name in sorted(ring.free_at.items())}

            def ring_free(slot):
                if slot in last_of:
                    ps.wait_filled(sp, last_of[slot])
            ps.wait_drained(sp, "yd7")
            ps.wait_filled(sp, "adaT11")
            ps.wait_filled(sp, "mv21")
            for b_e in ((1, 0), (0, NE - 1)):
                load_w13(0, [b_e], ring_free)
                load_w13(1, [b_e], ring_free)
                load_w2([b_e], ring_free)
            sp.wait_ge(ev("routed"), 1)
            pairs = sp.value_load(meta[0:1, P:P + 1], min_val=4, max_val=MAXB // 2)
            last = sp.value_load(meta[0:1, P + 1:P + 2], min_val=3, max_val=MAXB // 2 - 1)

            def expert_of(block):
                return sp.value_load(meta[0:1, block:block + 1] if isinstance(block, int)
                                     else meta[0:1, bass.ds(block, 1)], min_val=0, max_val=NE - 1)
            es = [(b, expert_of(2 + b)) for b in range(2)]
            sp.wait_ge(ev("first_halves_used"), 1)
            load_w13(0, es)
            sp.wait_ge(ev("hidden_filled"), 2)
            load_w13(1, es)
            with sp.Fori(2, last) as i:
                old, es = ([(b, expert_of(i * 2 + (n + b))) for b in range(2)] for n in (-2, 0))
                sp.wait_ge(ev("first_halves_used"), i)
                load_w13(0, es)
                sp.wait_ge(ev("hidden_filled"), i * 2)
                load_w13(1, es)
                sp.wait_ge(ev("rows_filled_for_dve"), i - 1)
                load_w2(old)
            blocks = sp.value_load(meta[0:1, P + 2:P + 3], min_val=1, max_val=2)
            old, es = ([(b, expert_of(last * 2 + (n + b))) for b in range(2)] for n in (-2, 0))

            blocks_reg = sp.to_reg(blocks)

            def second_block(load, slot):
                with sp.If_eq(blocks_reg, 2):
                    load()
                with sp.Else():
                    sp.sem_inc(xw_landed[slot], 16)
            sp.wait_ge(ev("first_halves_used"), last)
            load_w13(0, es[:1])
            second_block(lambda: load_w13(0, es[1:]), 3)
            sp.wait_ge(ev("hidden_filled"), last * 2)
            load_w13(1, es[:1])
            second_block(lambda: load_w13(1, es[1:]), 4)
            sp.wait_ge(ev("hidden_transposed"), last * 2)
            load_w2(old)
            sp.wait_ge(ev("first_halves_used"), pairs)
            load_w2(es[:1], slot=0)
            second_block(lambda: load_w2(es[1:], slot=0), 3)
            for n, (c0, w) in enumerate(LATE_A):
                need = None
                if n < 4:
                    need = [(ev("rows_filled_for_dve"), pairs), (ev("hidden_filled"), pairs * 2),
                            (ev("rows_filled_for_dve"), last), (ev("rows_filled_for_dve"), pairs)][n]
                ring2.load(sp, cols_of(w), k_rows(w_in2, slice(c0, c0 + w)), need)
            ring2.load(sp, cols_of(2048, 2), w_ukv.rearrange("(k p) n -> p k n", p=P))
            for c0, w in LATE_B:
                ring2.load(sp, cols_of(w), k_rows(w_in2, slice(c0, c0 + w)))
            for n in range(2):
                ring2.load(sp, cols_of(512), k_rows(w_o2, slice(n * 512, n * 512 + 512)))
            for n in range(8):
                ring2.load(sp, cols_of(512), k_rows(w_up, slice(n * 512, n * 512 + 512)))
            for n in range(8):
                ring2.load(sp, cols_of(D, 4), w_down[n * 512:n * 512 + 512, :].rearrange("(k p) n -> p k n", p=P))
            sp.wait_ge(ev("output_ready"), 4)
            sp.dma_start(out[0].rearrange("(t p) d -> p t d", p=P), x).then_inc(ev("output_written"), 16)
            sp.wait_ge(ev("output_written"), 16)


_INS = ["x", "c", "w_ada", "b_ada", "w_in", "w_pool", "pool_scale", "conv_w", "conv_b", "dt_bias", "a_log",
        "d_skip", "ssd_norm_w", "w_out", "w_group", "b_group", "w_router", "b_router", "w13", "w2",
        "final_norm_w", "mem_2", "positions_2", "g_mix_2", "w_in_2", "b_gate_2", "g_ckv_2", "w_ukv_2",
        "g_q_nope_2", "g_k_nope_2", "g_q_rope_2", "g_k_rope_2", "w_gla_gate_2", "b_gla_gate_2", "g_gla_out_2",
        "g_mem_2", "w_mem_kv_2", "g_q_mem_2", "g_k_mem_2", "w_o_2", "g_ffn_2", "w_up_2", "w_down_2"]


def program(nc, arrays):
    args = {}
    for name, v in arrays.items():
        args[name] = nc.dram_tensor(f"in_{name}_dram", v.shape, mybir.dt.from_np(v.dtype), kind="ExternalInput").ap()
    out = nc.dram_tensor("out_0_dram", (1, T, D), F32, kind="ExternalOutput").ap()
    build(nc, args, out)


def kernel(**inputs):
    import concourse.bacc as _bacc
    from concourse.bass_utils import run_bass_kernel_spmd as _run

    nc = _bacc.Bacc("TRN2", target_bir_lowering=False, num_devices=1)
    arrays = {name: np.ascontiguousarray(inputs[name]) for name in _INS}
    arrays["const"], arrays["pool_table"] = constants()
    program(nc, arrays)
    r = _run(nc, [{f"in_{k}_dram": v for k, v in arrays.items()}], core_ids=[0])
    return r.results[0]["out_0_dram"]
```
